# Optimizing a Trainium2 kernel written in Bass

```python
import math
import jax
import jax.numpy as jnp
from jax import lax
import numpy as np

D_MODEL = 1024
BATCH = 1
SEQ = 1024
DEPTH = 1
DEC_BATCH = 8
DEC_SEQ = 8
PAST_LEN = 1024
PAGE_SIZE = 128

SB_HEADS = 8
SB_HEAD_DIM = 64
SB_WIDTH = SB_HEADS * SB_HEAD_DIM
Q_BLOCK = 128
SB_BIAS_INIT = -6.0
SSM_INNER = D_MODEL
SSM_HEAD_DIM = 64
SSM_HEADS = SSM_INNER // SSM_HEAD_DIM
SSM_GROUPS = 2
SSM_STATE = 128
CONV_WIDTH = 4
SSM_CHUNK = 128
CONV_DIM = SSM_INNER + 2 * SSM_GROUPS * SSM_STATE
PEER_HEADS = 8
PEER_KEYS = 128
PEER_EXPERTS = PEER_KEYS * PEER_KEYS
PEER_KEY_DIM = 256
PEER_TOPK = 16
PEER_TOKEN_BLOCK = 128
EPS = 1e-6
IN_SPLIT_SIZES = (SB_WIDTH, SB_WIDTH, SB_WIDTH, SSM_INNER, CONV_DIM, SSM_HEADS, D_MODEL, D_MODEL)
IN_PROJ_COLS = 3 * SB_WIDTH + SSM_INNER + CONV_DIM + SSM_HEADS + 2 * D_MODEL

kernel_name = 'hybrid_stickbreak_ssd_peer_decode_step'

def _split_points(sizes):
    pts, acc = [], 0
    for s in sizes[:-1]:
        acc += s
        pts.append(acc)
    return pts

def rms_norm(x, w):
    xf = x.astype(jnp.float32)
    y = xf * lax.rsqrt(jnp.mean(xf * xf, axis=-1, keepdims=True) + EPS)
    return (y * w.astype(jnp.float32)).astype(x.dtype)

def stick_breaking_block(q, k, v, q_pos, k_pos, sb_bias):
    z = jnp.einsum('bqhd,bkhd->bhqk', q.astype(jnp.float32), k.astype(jnp.float32)) * (SB_HEAD_DIM ** -0.5)
    z = z + sb_bias.astype(jnp.float32)[None, :, None, None]
    mask = k_pos[None, :] < q_pos[:, None]
    log_keep = jnp.where(mask, jax.nn.log_sigmoid(-z), 0.0)
    after = lax.cumsum(log_keep, axis=3, reverse=True) - log_keep
    w = jnp.where(mask, jnp.exp(jax.nn.log_sigmoid(z) + after), 0.0)
    return jnp.einsum('bhqk,bkhd->bqhd', w, v.astype(jnp.float32)).astype(q.dtype)

def stick_breaking(q, k, v, q_offset, k_pos, sb_bias):
    b, tq, h, d = q.shape
    q_pos = q_offset + jnp.arange(tq)
    if tq > Q_BLOCK and tq % Q_BLOCK == 0:
        nb = tq // Q_BLOCK
        qb = q.reshape(b, nb, Q_BLOCK, h, d).transpose(1, 0, 2, 3, 4)
        pb = q_pos.reshape(nb, Q_BLOCK)
        ob = lax.map(lambda a: stick_breaking_block(a[0], k, v, a[1], k_pos, sb_bias), (qb, pb))
        return ob.transpose(1, 0, 2, 3, 4).reshape(b, tq, h, d)
    return stick_breaking_block(q, k, v, q_pos, k_pos, sb_bias)

def causal_conv(xbc, buf, conv_w, conv_b):
    L = xbc.shape[1]
    xp = jnp.concatenate([buf.astype(xbc.dtype), xbc], axis=1)
    y = sum(xp[:, i:i + L] * conv_w[i] for i in range(CONV_WIDTH)) + conv_b
    return jax.nn.silu(y), xp[:, -(CONV_WIDTH - 1):]

def ssd(x, dt, A, Bm, Cm, h0):
    b, L = x.shape[:2]
    G, R, P, N = SSM_GROUPS, SSM_HEADS // SSM_GROUPS, SSM_HEAD_DIM, SSM_STATE
    Q = min(SSM_CHUNK, L)
    pad = (-L) % Q
    if pad:
        pz = lambda a: jnp.pad(a, [(0, 0), (0, pad)] + [(0, 0)] * (a.ndim - 2))
        x, dt, Bm, Cm = pz(x), pz(dt), pz(Bm), pz(Cm)
    nc = (L + pad) // Q
    xs = x.reshape(b, nc, Q, G, R, P).astype(jnp.float32)
    dts = dt.reshape(b, nc, Q, G, R)
    Bs = Bm.reshape(b, nc, Q, G, N).astype(jnp.float32)
    Cs = Cm.reshape(b, nc, Q, G, N).astype(jnp.float32)
    Acs = jnp.cumsum(dts * A.reshape(G, R), axis=2)
    xdt = xs * dts[..., None]
    causal = jnp.tril(jnp.ones((Q, Q), bool))[:, :, None, None]
    seg = Acs[:, :, :, None] - Acs[:, :, None, :]
    decay = jnp.exp(jnp.where(causal, seg, -jnp.inf))
    cb = jnp.einsum('bcign,bcjgn->bcijg', Cs, Bs)
    y_diag = jnp.einsum('bcijg,bcijgr,bcjgrp->bcigrp', cb, decay, xdt)
    decay_end = jnp.exp(Acs[:, :, -1:] - Acs)
    chunk_states = jnp.einsum('bcjgn,bcjgr,bcjgrp->bcgrpn', Bs, decay_end, xdt)
    chunk_decay = jnp.exp(Acs[:, :, -1])

    def step(hc, inp):
        s, dcy = inp
        return hc * dcy[..., None, None] + s, hc

    h_final, h_starts = lax.scan(step, h0.astype(jnp.float32).reshape(b, G, R, P, N),
                                 (chunk_states.transpose(1, 0, 2, 3, 4, 5), chunk_decay.transpose(1, 0, 2, 3)))
    h_starts = h_starts.transpose(1, 0, 2, 3, 4, 5)
    y_off = jnp.einsum('bcign,bcigr,bcgrpn->bcigrp', Cs, jnp.exp(Acs), h_starts)
    y = (y_diag + y_off).reshape(b, nc * Q, SSM_HEADS, P)[:, :L]
    return y, h_final.reshape(b, SSM_HEADS, P, N)

def token_mixer(h, past_k, past_v, conv_buf, ssm_h0, pos_offset, w_in, sb_bias, conv_w, conv_b, dt_bias, a_log,
                d_skip, ssm_norm_w, w_br_attn, w_br_ssm, w_out):
    b, L, _ = h.shape
    proj = h @ w_in
    q, k, v, z, xbc, dt, ga, gs = jnp.split(proj, _split_points(IN_SPLIT_SIZES), axis=-1)
    q = q.reshape(b, L, SB_HEADS, SB_HEAD_DIM)
    k = k.reshape(b, L, SB_HEADS, SB_HEAD_DIM)
    v = v.reshape(b, L, SB_HEADS, SB_HEAD_DIM)
    if past_k is None:
        k_all, v_all = k, v
    else:
        k_all = jnp.concatenate([past_k.astype(k.dtype), k], axis=1)
        v_all = jnp.concatenate([past_v.astype(v.dtype), v], axis=1)
    k_pos = jnp.arange(k_all.shape[1])
    o_attn = stick_breaking(q, k_all, v_all, pos_offset, k_pos, sb_bias).reshape(b, L, SB_WIDTH)
    xbc_act, new_buf = causal_conv(xbc, conv_buf, conv_w, conv_b)
    xs, Bm, Cm = jnp.split(xbc_act, [SSM_INNER, SSM_INNER + SSM_GROUPS * SSM_STATE], axis=-1)
    dtp = jax.nn.softplus(dt.astype(jnp.float32) + dt_bias.astype(jnp.float32))
    A = -jnp.exp(a_log.astype(jnp.float32))
    xh = xs.reshape(b, L, SSM_HEADS, SSM_HEAD_DIM)
    y, h_new = ssd(xh, dtp, A, Bm.reshape(b, L, SSM_GROUPS, SSM_STATE),
                   Cm.reshape(b, L, SSM_GROUPS, SSM_STATE), ssm_h0)
    y = y + d_skip.astype(jnp.float32)[:, None] * xh.astype(jnp.float32)
    y = y.reshape(b, L, SSM_INNER) * jax.nn.silu(z.astype(jnp.float32))
    gsz = SSM_INNER // SSM_GROUPS
    y = rms_norm(y.reshape(b, L, SSM_GROUPS, gsz), ssm_norm_w.reshape(SSM_GROUPS, gsz))
    y = y.reshape(b, L, SSM_INNER).astype(h.dtype)
    merged = jax.nn.sigmoid(ga) * (o_attn @ w_br_attn) + jax.nn.sigmoid(gs) * (y @ w_br_ssm)
    return merged @ w_out, k, v, new_buf, h_new

def peer(h, peer_w_query, peer_keys1, peer_keys2, peer_u, peer_v):
    b, L, D = h.shape
    T = b * L
    nblk = -(-T // PEER_TOKEN_BLOCK)
    xt = jnp.pad(h.reshape(T, D), ((0, nblk * PEER_TOKEN_BLOCK - T), (0, 0)))

    def block(xb):
        qh = (xb @ peer_w_query).reshape(-1, PEER_HEADS, 2, PEER_KEY_DIM // 2).astype(jnp.float32)
        s1 = jnp.einsum('thd,kd->thk', qh[:, :, 0], peer_keys1.astype(jnp.float32))
        s2 = jnp.einsum('thd,kd->thk', qh[:, :, 1], peer_keys2.astype(jnp.float32))
        v1, i1 = lax.top_k(s1, PEER_TOPK)
        v2, i2 = lax.top_k(s2, PEER_TOPK)
        cand = (v1[..., :, None] + v2[..., None, :]).reshape(-1, PEER_HEADS, PEER_TOPK * PEER_TOPK)
        vals, flat = lax.top_k(cand, PEER_TOPK)
        e = (jnp.take_along_axis(i1, flat // PEER_TOPK, axis=-1) * PEER_KEYS
             + jnp.take_along_axis(i2, flat % PEER_TOPK, axis=-1))
        g = jax.nn.softmax(vals, axis=-1)
        act = jax.nn.gelu(jnp.einsum('thkd,td->thk', peer_u[e], xb).astype(jnp.float32))
        return jnp.einsum('thk,thkd->td', (g * act).astype(xb.dtype), peer_v[e])

    out = lax.map(block, xt.reshape(nblk, PEER_TOKEN_BLOCK, D))
    return out.reshape(-1, D)[:T].reshape(b, L, D)

def layer(x, c, past_k, past_v, conv_buf, ssm_h0, pos_offset, norm1_w, norm2_w, w_ada, b_ada, w_in, sb_bias,
          conv_w, conv_b, dt_bias, a_log, d_skip, ssm_norm_w, w_br_attn, w_br_ssm, w_out,
          peer_w_query, peer_keys1, peer_keys2, peer_u, peer_v):
    mod = (jax.nn.silu(c) @ w_ada + b_ada)[:, None, :]
    sh1, sc1, g1, sh2, sc2, g2 = jnp.split(mod, 6, axis=-1)
    h = rms_norm(x, norm1_w) * (1 + sc1) + sh1
    mix, k_new, v_new, buf_new, h_new = token_mixer(h, past_k, past_v, conv_buf, ssm_h0, pos_offset, w_in, sb_bias,
                                                    conv_w, conv_b, dt_bias, a_log, d_skip, ssm_norm_w,
                                                    w_br_attn, w_br_ssm, w_out)
    x = x + g1 * mix
    h = rms_norm(x, norm2_w) * (1 + sc2) + sh2
    x = x + g2 * peer(h, peer_w_query, peer_keys1, peer_keys2, peer_u, peer_v)
    return x, k_new, v_new, buf_new, h_new

def setup_inputs(seed: int = 0) -> dict:
    key = jax.random.key(seed)
    ks = jax.random.split(key, 32)
    f32 = jnp.float32

    def nrm(k, shape, scale):
        return jax.random.normal(k, shape, f32) * scale

    n_pages = PAST_LEN // PAGE_SIZE
    n_used = DEC_BATCH * n_pages
    n_pool = (5 * n_used + 3) // 4
    page_table = jax.random.permutation(ks[0], n_pool)[:n_used].reshape(DEC_BATCH, n_pages).astype(jnp.int32)
    dt0 = jnp.exp(jax.random.uniform(ks[1], (DEPTH, SSM_HEADS), f32, math.log(1e-3), math.log(1e-1)))
    dt_bias = dt0 + jnp.log(-jnp.expm1(-dt0))
    a_log = jnp.log(jax.random.uniform(ks[2], (DEPTH, SSM_HEADS), f32, 1.0, 16.0))
    return {
        'x_prompt': nrm(ks[3], (BATCH, SEQ, D_MODEL), 1.0),
        'x_sample': nrm(ks[4], (DEC_BATCH, DEC_SEQ, D_MODEL), 1.0),
        'cache_k': nrm(ks[5], (DEPTH, n_pool, PAGE_SIZE, SB_HEADS, SB_HEAD_DIM), 1.0),
        'cache_v': nrm(ks[6], (DEPTH, n_pool, PAGE_SIZE, SB_HEADS, SB_HEAD_DIM), 1.0),
        'state_conv': nrm(ks[7], (DEPTH, DEC_BATCH, CONV_WIDTH - 1, CONV_DIM), 1.0),
        'state_ssm': nrm(ks[8], (DEPTH, DEC_BATCH, SSM_HEADS, SSM_HEAD_DIM, SSM_STATE), 0.5),
        'page_table': page_table,
        'c_prompt': nrm(ks[9], (BATCH, D_MODEL), 1.0),
        'c_sample': nrm(ks[10], (DEC_BATCH, D_MODEL), 1.0),
        'norm1_w': 1.0 + nrm(ks[11], (DEPTH, D_MODEL), 0.02),
        'norm2_w': 1.0 + nrm(ks[12], (DEPTH, D_MODEL), 0.02),
        'w_ada': nrm(ks[13], (DEPTH, D_MODEL, 6 * D_MODEL), 0.5 * D_MODEL ** -0.5),
        'b_ada': nrm(ks[14], (DEPTH, 6 * D_MODEL), 0.02),
        'w_in': nrm(ks[15], (DEPTH, D_MODEL, IN_PROJ_COLS), D_MODEL ** -0.5),
        'sb_bias': SB_BIAS_INIT + nrm(ks[29], (DEPTH, SB_HEADS), 0.1),
        'conv_w': nrm(ks[16], (DEPTH, CONV_WIDTH, CONV_DIM), CONV_WIDTH ** -0.5),
        'conv_b': nrm(ks[17], (DEPTH, CONV_DIM), 0.02),
        'dt_bias': dt_bias,
        'a_log': a_log,
        'd_skip': 1.0 + nrm(ks[18], (DEPTH, SSM_HEADS), 0.02),
        'ssm_norm_w': 1.0 + nrm(ks[19], (DEPTH, SSM_INNER), 0.02),
        'w_br_attn': nrm(ks[20], (DEPTH, SB_WIDTH, D_MODEL), SB_WIDTH ** -0.5),
        'w_br_ssm': nrm(ks[21], (DEPTH, SSM_INNER, D_MODEL), SSM_INNER ** -0.5),
        'w_out': nrm(ks[22], (DEPTH, D_MODEL, D_MODEL), D_MODEL ** -0.5),
        'peer_w_query': nrm(ks[23], (DEPTH, D_MODEL, PEER_HEADS * PEER_KEY_DIM), D_MODEL ** -0.5),
        'peer_keys1': nrm(ks[24], (DEPTH, PEER_KEYS, PEER_KEY_DIM // 2), (PEER_KEY_DIM // 2) ** -0.5),
        'peer_keys2': nrm(ks[25], (DEPTH, PEER_KEYS, PEER_KEY_DIM // 2), (PEER_KEY_DIM // 2) ** -0.5),
        'peer_u': nrm(ks[26], (DEPTH, PEER_EXPERTS, D_MODEL), D_MODEL ** -0.5),
        'peer_v': nrm(ks[27], (DEPTH, PEER_EXPERTS, D_MODEL), 0.5),
        'norm_f_w': 1.0 + nrm(ks[28], (D_MODEL,), 0.02),
    }

def reference(x_prompt, x_sample, cache_k, cache_v, state_conv, state_ssm, page_table, c_prompt, c_sample,
              norm1_w, norm2_w, w_ada, b_ada, w_in, sb_bias, conv_w, conv_b, dt_bias, a_log, d_skip, ssm_norm_w,
              w_br_attn, w_br_ssm, w_out, peer_w_query, peer_keys1, peer_keys2, peer_u, peer_v, norm_f_w):
    n_seq, n_pages = page_table.shape
    past_len = n_pages * PAGE_SIZE
    xp, xs = x_prompt, x_sample
    kp_l, vp_l, bp_l, hp_l, ks_l, vs_l, bs_l, hs_l = [], [], [], [], [], [], [], []
    for d in range(DEPTH):
        lw = (norm1_w[d], norm2_w[d], w_ada[d], b_ada[d], w_in[d], sb_bias[d], conv_w[d], conv_b[d], dt_bias[d],
              a_log[d], d_skip[d], ssm_norm_w[d], w_br_attn[d], w_br_ssm[d], w_out[d], peer_w_query[d],
              peer_keys1[d], peer_keys2[d], peer_u[d], peer_v[d])
        buf0 = jnp.zeros((xp.shape[0], CONV_WIDTH - 1, CONV_DIM), xp.dtype)
        h00 = jnp.zeros((xp.shape[0], SSM_HEADS, SSM_HEAD_DIM, SSM_STATE), jnp.float32)
        xp, kp, vp, bp, hp = layer(xp, c_prompt, None, None, buf0, h00, 0, *lw)
        past_k = cache_k[d][page_table].reshape(n_seq, past_len, SB_HEADS, SB_HEAD_DIM)
        past_v = cache_v[d][page_table].reshape(n_seq, past_len, SB_HEADS, SB_HEAD_DIM)
        xs, ksn, vsn, bsn, hsn = layer(xs, c_sample, past_k, past_v, state_conv[d], state_ssm[d], past_len, *lw)
        kp_l.append(kp); vp_l.append(vp); bp_l.append(bp); hp_l.append(hp)
        ks_l.append(ksn); vs_l.append(vsn); bs_l.append(bsn); hs_l.append(hsn)
    y_prompt = rms_norm(xp, norm_f_w)
    y_sample = rms_norm(xs, norm_f_w)
    return (y_prompt, y_sample, jnp.stack(kp_l), jnp.stack(vp_l), jnp.stack(bp_l), jnp.stack(hp_l),
            jnp.stack(ks_l), jnp.stack(vs_l), jnp.stack(bs_l), jnp.stack(hs_l))


_drawn_inputs = setup_inputs


def setup_inputs(seed=0):
    import zlib

    import numpy as np

    out = dict(_drawn_inputs(seed))
    spreads = {}
    factors = {'cache_k': 3.865,
     'cache_v': 3.474,
     'norm2_w': 4.865,
     'sb_bias': 8.0,
     'd_skip': 8.0,
     'ssm_norm_w': 8.0,
     'norm_f_w': 2.744}
    for name, (base, spread) in spreads.items():
        noise = np.random.default_rng([zlib.crc32(name.encode()), seed]).standard_normal(out[name].shape)
        drawn = base * np.exp(spread * noise) if base else spread * noise
        out[name] = jnp.asarray(drawn.astype(out[name].dtype))
    for name, factor in factors.items():
        out[name] = (out[name] * factor).astype(out[name].dtype)
    return out
```

```python
from contextlib import ExitStack, contextmanager

import numpy as np

import concourse.bass as bass
from concourse import mybir

ALU = mybir.AluOpType
ACT = mybir.ActivationFunctionType
AX = mybir.AxisListType
F32 = mybir.dt.float32
I32 = mybir.dt.int32
U32 = mybir.dt.uint32

P = 128
D = 1024
KC = D // P
SEQ = 1024
NSEQ = 8
LS = 8
TS = NSEQ * LS
T = SEQ + TS
SPLITS = ((0, 384), (384, 384), (768, 320))
NS = len(SPLITS)
HEADS, HD = 8, 64
AW = HEADS * HD
SH, SP_ = 16, 64
NG, NST = 2, 128
CW = 4
CONV = D + 2 * NG * NST
PAGE = 128
NPAGE = 8
POOL = 80
EPS = 1e-6
CLAMP = 30.0
TILES = SEQ // P
TP = (TILES + 1) * P
EH, TOPK, NK = 8, 16, 128
GRP = 4
NGRP = NK // GRP
TB = 32
NTB = T // TB

CH_Q, CH_K, CH_Z, CH_X, CH_G = 0, 4, 8, 16, 28
NCH = 44
RING = 4

C_ONE, C_NEG, C_NTRI, C_TRI, C_STRICT, C_ID, C_IOTA, C_BTRI, C_BSTRICT, C_SEQ = (
    0, 128, 256, 384, 512, 640, 768, 896, 960, 1024)
NCONST = 1032

W_N1, W_N2, W_NF, W_SSM, W_DSKIP, W_BADA, W_SB, W_CB, W_CW, W_DTB, W_AL = (
    0, 8, 16, 24, 32, 40, 88, 96, 108, 156, 172)
NPAR = 188


class Chain:

    def __init__(self, eng, sem, passed=None):
        self.eng, self.sem, self.passed, self.base, self.n = eng, sem, passed, 0, 0

    def mark(self, ins):
        self.n += 1
        ins.then_inc(self.sem, 1)
        return self.base + self.n

    def wait(self, count):
        self.eng.wait_ge(self.sem, count)

    def link(self, ins):
        self.wait(self.mark(ins))

    def link_apart(self, ins):
        self.link(ins)
        self.eng.sem_inc(self.passed, 1)

    @contextmanager
    def turns(self, i, count, per):
        start = self.base + self.n
        self.base, self.n = i * per + start, 0
        yield
        assert self.n == per, (self.n, per)
        self.base, self.n = start + count * per, 0


def constants():
    c = np.zeros((P, NCONST), np.float32)
    r, q = np.arange(P)[:, None], np.arange(P)[None, :]
    c[:, C_ONE:C_ONE + P] = 1
    c[:, C_NEG:C_NEG + P] = -1
    c[:, C_NTRI:C_NTRI + P] = np.where(r >= q, -1, 0)
    c[:, C_TRI:C_TRI + P] = r <= q
    c[:, C_STRICT:C_STRICT + P] = r < q
    c[:, C_ID:C_ID + P] = r == q
    c[:, C_IOTA:C_IOTA + P] = q
    r, q = np.arange(TS)[:, None], np.arange(TS)[None, :]
    same = r // LS == q // LS
    c[:TS, C_BTRI:C_BTRI + TS] = same & (r <= q)
    c[:TS, C_BSTRICT:C_BSTRICT + TS] = same & (r < q)
    c[:TS, C_SEQ:C_SEQ + NSEQ] = r // LS == np.arange(NSEQ)[None, :]
    return c


def build(nc, a):
    with ExitStack() as top:
        taken = []

        def sem(name):
            taken.append(nc.alloc_semaphore(name=name))
            return taken[-1]

        def keep(name, shape, dt=F32):
            return top.enter_context(nc.sbuf_tensor(name, shape, dt))

        s = dict(
            const=keep("const", [P, NCONST]),
            par=keep("par", [P, NPAR]),
            mod=keep("mod", [P, 48, 1 + NSEQ]),
            h=keep("h", [P, KC, T]),
            rstd=keep("rstd", [P, T]),
            gain=keep("gain", [P, KC, 1 + NSEQ]),
        )
        with nc.sbuf_tensor("x", [P, KC, T], F32) as s["x"], \
                nc.sbuf_tensor("dt_tok", [P, TILES + 1, SH], F32) as s["dt_tok"]:
            with nc.sbuf_tensor("squares", [P, KC, T], F32) as s["y"]:
                ada_phase(nc, a, s, sem)
            with nc.sbuf_tensor("v_tok", [P, TILES + 1, AW], F32) as s["v_tok"]:
                project_phase(nc, a, s, sem)
                attend_phase(nc, a, s, sem)
                attend_sample_phase(nc, a, s, sem)
            with nc.sbuf_tensor("y", [P, KC, T], F32) as s["y"]:
                ssd_phase(nc, a, s, sem)
                merge_phase(nc, a, s, sem)
        nc.clear_and_free_semaphores(taken)
        nc.all_engine_barrier()
        with nc.sbuf_tensor("choice", [P, 3, TP], F32) as s["choice"]:
            route_phase(nc, a, s, sem)
            weights_phase(nc, a, s, sem)
        s["acc"] = s["h"]
        experts_phase(nc, a, s, sem)
        final_phase(nc, a, s, sem)


class Norm:

    def __init__(self, nc, sem, name, src, squares, s, psum, chunks=KC):
        self.nc, self.src, self.sq, self.s, self.psum, self.chunks = nc, src, squares, s, psum, chunks
        self.squared = sem(name + "_squared")
        self.summed = sem(name + "_summed")
        self.meaned = sem(name + "_meaned")
        self.rooted = sem(name + "_rooted")
        self.scaled = sem(name + "_scaled")

    def scalar(self, act):
        for k in range(self.chunks):
            act.activation(self.sq[:, k, :], self.src[:, k, :], ACT.Square).then_inc(self.squared, 1)
        for i, (t0, n) in enumerate(SPLITS):
            act.wait_ge(self.meaned, i + 1)
            r = self.s["rstd"][:, t0:t0 + n]
            act.activation(r, r, ACT.Sqrt).then_inc(self.rooted, 1)

    def tensor(self, pe):
        ones = self.s["const"][:, C_ONE:C_ONE + P]
        for k in range(self.chunks):
            pe.wait_ge(self.squared, k + 1)
            for i, (t0, n) in enumerate(SPLITS):
                mm = pe.matmul(self.psum[:, i, 0:n], ones, self.sq[:, k, t0:t0 + n],
                               start=(k == 0), stop=(k == self.chunks - 1))
                if k == self.chunks - 1:
                    mm.then_inc(self.summed, 1)

    def vector(self, dve):
        for i, (t0, n) in enumerate(SPLITS):
            dve.wait_ge(self.summed, i + 1)
            dve.tensor_scalar(self.s["rstd"][:, t0:t0 + n], self.psum[:, i, 0:n], 1.0 / (self.chunks * P), EPS,
                              ALU.mult, ALU.add).then_inc(self.meaned, 1)
        for i, (t0, n) in enumerate(SPLITS):
            dve.wait_ge(self.rooted, i + 1)
            r = self.s["rstd"][:, t0:t0 + n]
            dve.reciprocal(r, r).then_inc(self.scaled, 1)
        dve.wait_ge(self.scaled, NS)


def modulated(dve, link, s, src, dst, norm_w, shift, scale, done):
    gain = s["gain"]
    link(dve.tensor_scalar(gain[:, :, :], s["mod"][:, scale:scale + KC, :], 1.0, None, ALU.add))
    w = s["par"][:, norm_w:norm_w + KC].unsqueeze(2).to_broadcast([P, KC, 1 + NSEQ])
    link(dve.tensor_tensor(gain[:, :, :], gain[:, :, :], w, ALU.mult))
    sh = s["mod"][:, shift:shift + KC, :]

    def per_seq(t, k):
        return t[:, k, 1:].unsqueeze(2).to_broadcast([P, NSEQ, LS])

    for k in range(KC):
        link(dve.tensor_tensor(dst[:, k, :], src[:, k, :], s["rstd"][:, :], ALU.mult))
        own = dst[:, k, SEQ:T].rearrange("p (s l) -> p s l", l=LS)
        dve.tensor_scalar(dst[:, k, 0:SEQ], dst[:, k, 0:SEQ], gain[:, k, 0:1], sh[:, k, 0:1],
                          ALU.mult, ALU.add).then_inc(done, 1)
        link(dve.tensor_tensor(own, own, per_seq(gain, k), ALU.mult))
        dve.tensor_tensor(own, own, per_seq(sh, k), ALU.add).then_inc(done, 1)


def ada_phase(nc, a, s, sem):
    n_loads = 48
    with ExitStack() as ctx:
        ring = ctx.enter_context(nc.sbuf_tensor("ada_ring", [P, RING, KC, P], F32))
        cond = ctx.enter_context(nc.sbuf_tensor("cond", [P, KC, 1 + NSEQ], F32))
        cond_act = ctx.enter_context(nc.sbuf_tensor("cond_act", [P, KC, 1 + NSEQ], F32))
        mod_ps = ctx.enter_context(nc.psum_tensor("mod_ps", [P, RING, 512], F32))
        sum_ps = ctx.enter_context(nc.psum_tensor("sum_ps", [P, NS, 512], F32))
        small_in = sem("small_in")
        x_in = sem("x_in")
        ada_in = [sem(f"ada_in{u}") for u in range(RING)]
        cond_ready = sem("cond_ready")
        mod_summed = sem("mod_summed")
        mod_ready = sem("mod_ready")
        h_ready = sem("h_ready")
        chain = sem("ada_chain")
        norm = Norm(nc, sem, "norm1", s["x"], s["y"], s, sum_ps)

        with nc.Block() as block:
            @block.sync
            def _(sp):
                sp.dma_start(s["const"][:, :], a["const"]).then_inc(small_in, 16)
                sp.dma_start(s["par"][:, :], a["par"]).then_inc(small_in, 16)
                sp.dma_start(cond[:, :, :], a["cond"]).then_inc(small_in, 16)
                sp.dma_start(s["x"][:, :, :], a["x"]).then_inc(x_in, 16)
                for u in range(RING):
                    sp.dma_start(ring[:, u, :, :], a["w_ada"][u]).then_inc(ada_in[u], 16)
                with sp.Fori(1, n_loads // RING) as i:
                    for u in range(RING):
                        sp.wait_ge(mod_summed, (i - 1) * RING + u + 1)
                        sp.dma_start(ring[:, u, :, :], a["w_ada"][i * RING + u]).then_inc(ada_in[u], 16)

            @block.scalar
            def _(act):
                act.wait_ge(small_in, 48)
                act.activation(cond_act[:, :, :], cond[:, :, :], ACT.Silu).then_inc(cond_ready, 1)
                act.wait_ge(x_in, 16)
                norm.scalar(act)
                act.sem_inc(mod_ready, RING)
                with act.Fori(0, n_loads // RING) as i:
                    for u in range(RING):
                        c = i * RING + u
                        act.wait_ge(mod_summed, c + 1)
                        act.activation(s["mod"][:, bass.ds(c, 1), :].rearrange("p o n -> p (o n)"),
                                       mod_ps[:, u, 0:1 + NSEQ], ACT.Identity,
                                       bias=s["par"][:, bass.ds(c + W_BADA, 1)]).then_inc(mod_ready, 1)

            @block.tensor
            def _(pe):
                pe.wait_ge(small_in, 48)
                norm.tensor(pe)
                pe.wait_ge(cond_ready, 1)
                with pe.Fori(0, n_loads // RING) as i:
                    for u in range(RING):
                        pe.wait_ge(ada_in[u], (i + 1) * 16)
                        pe.wait_ge(mod_ready, i * RING + u + 1)
                        for k in range(KC):
                            mm = pe.matmul(mod_ps[:, u, 0:1 + NSEQ], ring[:, u, k, :], cond_act[:, k, :],
                                           start=(k == 0), stop=(k == KC - 1))
                        mm.then_inc(mod_summed, 1)

            @block.vector
            def _(dve):
                norm.vector(dve)
                dve.wait_ge(mod_ready, RING + 2 * KC)
                modulated(dve, Chain(dve, chain).link, s, s["x"], s["h"], W_N1, 0, KC, h_ready)


def project_phase(nc, a, s, sem):
    with ExitStack() as ctx:
        def sb(name, shape):
            return ctx.enter_context(nc.sbuf_tensor(name, shape, F32))

        ring = sb("in_ring", [P, RING, KC, P])
        wv = sb("wv", [P, KC, AW])
        wdt = sb("wdt", [P, KC, SH])
        stage = sb("stage", [P, 2, T])
        raw_p = sb("raw_p", [P, CW - 1 + SEQ])
        raw_s = sb("raw_s", [P, NSEQ, CW - 1 + LS])
        conv = sb("conv", [P, T])
        state = sb("state", [P, 12, NSEQ, CW - 1])
        tail = sb("tail", [P, 12, 1 + NSEQ, CW - 1])
        ps = ctx.enter_context(nc.psum_tensor("in_ps", [P, 2 * NS, 512], F32))
        ps_v = ctx.enter_context(nc.psum_tensor("v_ps", [P, 512], F32))
        ps_dt = ctx.enter_context(nc.psum_tensor("dt_ps", [P, 512], F32))
        w_in = [sem(f"w_in{u}") for u in range(RING)]
        wide_in = sem("wide_in")
        summed = sem("proj_summed")
        banks_free = sem("proj_banks_free")
        staged = sem("proj_staged")
        stored = [sem(f"proj_stored{u}") for u in range(2)]
        raw_ready = sem("raw_ready")
        zeroed = sem("raw_zeroed")
        convolved = sem("convolved")
        chain = sem("conv_chain")
        v_summed, v_taken = sem("v_summed"), sem("v_taken")
        dt_summed, dt_taken = sem("dt_summed"), sem("dt_taken")
        rows_out = sem("rows_out")
        h = s["h"]

        with nc.Block() as block:
            @block.sync
            def _(sp):
                for u in range(RING):
                    sp.dma_start(ring[:, u, :, :], a["w_in"][u]).then_inc(w_in[u], 16)
                sp.dma_start(state[:, :, :, :], a["state_conv"]).then_inc(wide_in, 16)
                sp.dma_start(wv[:, :, :], a["w_v"]).then_inc(wide_in, 16)
                sp.dma_start(wdt[:, :, :], a["w_dt"]).then_inc(wide_in, 16)
                with sp.Fori(1, NCH // RING) as i:
                    for u in range(RING):
                        sp.wait_ge(summed, (i - 1) * (RING * NS) + (u + 1) * NS)
                        sp.dma_start(ring[:, u, :, :], a["w_in"][i * RING + u]).then_inc(w_in[u], 16)
                sp.wait_ge(v_taken, 1 + TILES + 1)
                vp = a["v_out"][0:SEQ, :].rearrange("(n p) c -> p n c", p=P)
                sp.dma_start(vp, s["v_tok"][:, 0:TILES, :]).then_inc(rows_out, 16)
                sp.dma_start(a["v_out"][SEQ:T, :], s["v_tok"][0:TS, TILES, :]).then_inc(rows_out, 16)
                sp.wait_ge(convolved, 12)
                sp.dma_start(a["conv_out"], tail[:, :, :, :]).then_inc(rows_out, 16)
                sp.wait_ge(rows_out, 48)
                for u in range(2):
                    sp.wait_ge(stored[u], 16 * (NCH // 2 + 1))

            @block.tensor
            def _(pe):
                with pe.Fori(0, NCH // RING) as i:
                    for u in range(RING):
                        pe.wait_ge(w_in[u], (i + 1) * 16)
                        for j, (t0, n) in enumerate(SPLITS):
                            b = (u % 2) * NS + j
                            pe.wait_ge(banks_free, i * (RING * NS) + u * NS + j + 1)
                            for k in range(KC):
                                mm = pe.matmul(ps[:, b, 0:n], ring[:, u, k, :], h[:, k, t0:t0 + n],
                                               start=(k == 0), stop=(k == KC - 1))
                            mm.then_inc(summed, 1)
                pe.wait_ge(wide_in, 48)
                for t in range(TILES + 1):
                    n = min(P, T - t * P)
                    pe.wait_ge(v_taken, t + 1)
                    for k in range(KC):
                        mm = pe.matmul(ps_v[0:n, :], h[:, k, t * P:t * P + n], wv[:, k, :],
                                       start=(k == 0), stop=(k == KC - 1))
                    mm.then_inc(v_summed, 1)
                    pe.wait_ge(dt_taken, t + 1)
                    for k in range(KC):
                        mm = pe.matmul(ps_dt[0:n, 0:SH], h[:, k, t * P:t * P + n], wdt[:, k, :],
                                       start=(k == 0), stop=(k == KC - 1))
                    mm.then_inc(dt_summed, 1)

            @block.scalar
            def _(act):
                act.sem_inc(banks_free, 2 * NS)
                act.sem_inc(v_taken, 1)
                for u in range(2):
                    act.sem_inc(stored[u], 16)

                def take(first, count, func, scale, row0, dest):
                    with act.Fori(first // RING, (first + count) // RING) as i:
                        for u in range(RING):
                            b = u % 2
                            act.wait_ge(stored[b], i * (16 * RING // 2) + 16 * (u // 2 + 1))
                            for j, (t0, n) in enumerate(SPLITS):
                                act.wait_ge(summed, i * (RING * NS) + u * NS + j + 1)
                                act.activation(stage[:, b, t0:t0 + n], ps[:, b * NS + j, 0:n], func,
                                               scale=scale).then_inc(banks_free, 1)
                            act.wait_ge(banks_free, i * (RING * NS) + (u + 1) * NS + 2 * NS)
                            act.dma_start(dest[i * RING + (u - row0)], stage[:, b, :]).then_inc(stored[b], 16)

                take(CH_Q, 4, ACT.Copy, HD ** -0.5, 0, a["proj"])
                take(CH_K, 4, ACT.Copy, 1.0, CH_K, a["k_out"])
                take(CH_Z, 8, ACT.Silu, 1.0, 0, a["proj"])
                act.wait_ge(zeroed, 1)
                act.wait_ge(wide_in, 48)
                with act.Fori(CH_X // RING, CH_G // RING) as i:
                    for u in range(RING):
                        b = u % 2
                        for j, (t0, n) in enumerate(SPLITS):
                            act.wait_ge(summed, i * (RING * NS) + u * NS + j + 1)
                            own = min(n, SEQ - t0)
                            ins = act.copy(raw_p[:, CW - 1 + t0:CW - 1 + t0 + own], ps[:, b * NS + j, 0:own])
                            if own < n:
                                ins = act.copy(raw_s[:, :, CW - 1:],
                                               ps[:, b * NS + j, own:n].rearrange("p (s l) -> p s l", l=LS))
                            ins.then_inc(banks_free, 1)
                        act.copy(raw_s[:, :, 0:CW - 1],
                                 state[:, bass.ds(i * RING + (u - CH_X), 1), :, :].rearrange(
                                     "p o s l -> p (o s) l")).then_inc(raw_ready, 1)
                        act.wait_ge(stored[b], i * (16 * RING // 2) + 16 * (u // 2 + 1))
                        act.wait_ge(convolved, i * RING + (u + 1 - CH_X))
                        act.activation(stage[:, b, :], conv[:, :], ACT.Silu).then_inc(staged, 1)
                        act.wait_ge(staged, i * RING + (u + 1 - CH_X))
                        act.dma_start(a["proj"][i * RING + u], stage[:, b, :]).then_inc(stored[b], 16)
                take(CH_G, 16, ACT.Sigmoid, 1.0, 0, a["proj"])
                for t in range(TILES + 1):
                    n = min(P, T - t * P)
                    act.wait_ge(v_summed, t + 1)
                    act.copy(s["v_tok"][0:n, t, :], ps_v[0:n, :]).then_inc(v_taken, 1)

            @block.vector
            def _(dve):
                link = Chain(dve, chain)
                dve.sem_inc(dt_taken, 1)
                dve.memset(raw_p[:, 0:CW - 1], 0.0).then_inc(zeroed, 1)
                dve.memset(s["v_tok"][TS:P, TILES, :], 0.0)
                with dve.Fori(0, 12 // RING) as i, link.turns(i, 12 // RING, RING * 6):
                    for u in range(RING):
                        c = i * RING + u
                        dve.wait_ge(raw_ready, c + 1)

                        def tap(j):
                            return s["par"][:, bass.ds(c * CW + (W_CW + j), 1)]

                        cs = conv[:, SEQ:T].rearrange("p (s l) -> p s l", l=LS)
                        bias = s["par"][:, bass.ds(c + W_CB, 1)]
                        at_p = link.mark(dve.tensor_scalar(conv[:, 0:SEQ], raw_p[:, 0:SEQ], tap(0), bias,
                                                           ALU.mult, ALU.add))
                        at_s = link.mark(dve.tensor_scalar(cs, raw_s[:, :, 0:LS], tap(0), bias,
                                                           ALU.mult, ALU.add))
                        for j in range(1, CW):
                            link.wait(at_p)
                            ins = dve.scalar_tensor_tensor(conv[:, 0:SEQ], raw_p[:, j:j + SEQ], tap(j),
                                                           conv[:, 0:SEQ], ALU.mult, ALU.add)
                            at_p = link.mark(ins) if j < CW - 1 else None
                            link.wait(at_s)
                            ins = dve.scalar_tensor_tensor(cs, raw_s[:, :, j:j + LS], tap(j), cs,
                                                           ALU.mult, ALU.add)
                            at_s = link.mark(ins) if j < CW - 1 else None
                        out = tail[:, bass.ds(c, 1), :, :].rearrange("p o s l -> p (o s) l")
                        dve.tensor_copy(out[:, 0, :], raw_p[:, SEQ:SEQ + CW - 1])
                        dve.tensor_copy(out[:, 1:, :], raw_s[:, :, LS:LS + CW - 1]).then_inc(convolved, 1)
                for t in range(TILES + 1):
                    n = min(P, T - t * P)
                    dve.wait_ge(dt_summed, t + 1)
                    dve.tensor_tensor(s["dt_tok"][0:n, t, :], ps_dt[0:n, 0:SH],
                                      s["par"][0:n, W_DTB:W_DTB + SH], ALU.add).then_inc(dt_taken, 1)


STEPS = [(sp, kb, max(0, kb - 4 * sp) * P) for sp in range(2) for kb in range(4 * sp + 3, -1, -1)]
NSTEP = len(STEPS)
HALF = SEQ // 2


def attend_phase(nc, a, s, sem):
    with ExitStack() as ctx:
        def sb(name, shape):
            return ctx.enter_context(nc.sbuf_tensor(name, shape, F32))

        q = sb("q", [HD, 2, SEQ])
        k = sb("k", [HD, 2, SEQ])
        v = sb("v", [P, 2, TILES, HD])
        soft = sb("soft", [P, 3, HALF])
        later = sb("later", [P, 2, HALF])
        wgt = sb("wgt", [P, 2, HALF])
        out = sb("o_stage", [HD, 2, SEQ])
        bias_v = sb("bias_v", [P, 2])
        bias_a = sb("bias_a", [P, 2])
        zs = ctx.enter_context(nc.psum_tensor("z_ps", [P, 4, 512], F32))
        os_ = ctx.enter_context(nc.psum_tensor("o_ps", [P, 2, 512], F32))
        qk_in = [sem(f"qk_in{u}") for u in range(2)]
        v_ready = sem("v_ready")
        z_ready, clamped, logged, soft_ready, later_ready = (
            sem("z_ready"), sem("clamped"), sem("logged"), sem("soft_ready"), sem("later_ready"))
        exped, masked, weighted, w_ready, w_masked, pv_done, o_taken = (
            sem("exped"), sem("masked"), sem("weighted"), sem("w_ready"), sem("w_masked"), sem("pv_done"),
            sem("o_taken"))
        o_out = [sem(f"o_out{u}") for u in range(2)]
        bias_in_v, bias_in_a = sem("bias_in_v"), sem("bias_in_a")
        const = s["const"]
        ntri, neg = const[:, C_NTRI:C_NTRI + P], const[:, C_NEG:C_NEG + P]
        strict = const[:, C_STRICT:C_STRICT + P]
        q_rows = a["proj"].rearrange("c p t -> (c p) t")
        k_rows = a["k_out"].rearrange("c p t -> (c p) t")
        NDIAG = sum(kb >= 4 * sp for sp, kb, _ in STEPS)
        diag_no = {n: sum(kb >= 4 * sp for sp, kb, _ in STEPS[:n]) for n in range(NSTEP)}
        NLATER = sum(kb > 0 for _, kb, _ in STEPS)
        later_no = {n: sum(kb > 0 for _, kb, _ in STEPS[:n]) for n in range(NSTEP)}

        with nc.Block() as block:
            @block.sync
            def _(sp):
                def load(h, u):
                    row = h * HD if isinstance(h, int) else bass.ds(h * HD, HD)
                    rows = slice(row, row + HD) if isinstance(h, int) else row
                    sp.dma_start(q[:, u, :], q_rows[rows, 0:SEQ]).then_inc(qk_in[u], 16)
                    sp.dma_start(k[:, u, :], k_rows[rows, 0:SEQ]).then_inc(qk_in[u], 16)

                load(0, 0)
                load(1, 1)
                with sp.Fori(1, HEADS // 2) as i:
                    for u in range(2):
                        sp.wait_ge(pv_done, (i - 1) * (2 * NSTEP) + (u + 1) * NSTEP)
                        load(i * 2 + u, u)
                for u in range(2):
                    sp.wait_ge(o_out[u], 16 * (HEADS // 2 + 1))

            @block.gpsimd
            def _(pool):
                def fetch(h, u):
                    cols = bass.ds(h * HD, HD) if not isinstance(h, int) else slice(h * HD, h * HD + HD)
                    pool.tensor_copy(v[:, u, :, :], s["v_tok"][:, 0:TILES, cols]).then_inc(v_ready, 1)

                fetch(0, 0)
                fetch(1, 1)
                with pool.Fori(1, HEADS // 2) as i:
                    for u in range(2):
                        pool.wait_ge(pv_done, (i - 1) * (2 * NSTEP) + (u + 1) * NSTEP)
                        fetch(i * 2 + u, u)

            @block.tensor
            def _(pe):
                with pe.Fori(0, HEADS // 2) as i:
                    for u in range(2):
                        base = i * (2 * NSTEP) + u * NSTEP

                        def scores(n):
                            half, kb, off = STEPS[n]
                            pe.matmul(zs[:, n % 4, off:HALF], k[:, u, kb * P:(kb + 1) * P],
                                      q[:, u, half * HALF + off:(half + 1) * HALF],
                                      start=True, stop=True).then_inc(z_ready, 1)

                        def sums(n):
                            half, kb, off = STEPS[n]
                            diag = kb >= 4 * half
                            off2 = off + P if diag else 0
                            pe.wait_ge(soft_ready, base + n + 1)
                            mm = pe.matmul(zs[:, n % 4, off:HALF], ntri, soft[:, n % 3, off:HALF],
                                           start=False, stop=True, skip_group_check=True)
                            if off2 < HALF:
                                pe.wait_ge(later_ready, i * (2 * NLATER) + u * NLATER + later_no[n])
                                mm = pe.matmul(zs[:, n % 4, off2:HALF], neg, later[:, n % 2, off2:HALF],
                                               start=False, stop=True, skip_group_check=True)
                            mm.then_inc(weighted, 1)

                        def values(n):
                            half, kb, off = STEPS[n]
                            pe.wait_ge(w_ready, base + n + 1)
                            if kb >= 4 * half:
                                pe.wait_ge(w_masked, i * (2 * NDIAG) + u * NDIAG + diag_no[n] + 1)
                            if kb == 4 * half + 3:
                                pe.wait_ge(o_taken, i * 4 + u * 2 + half + 1)
                            pe.matmul(os_[0:HD, half, off:HALF], v[:, u, kb, :], wgt[:, n % 2, off:HALF],
                                      start=(kb == 4 * half + 3), stop=(kb == 0),
                                      skip_group_check=True).then_inc(pv_done, 1)

                        pe.wait_ge(qk_in[u], (i + 1) * 32)
                        scores(0)
                        scores(1)
                        pe.wait_ge(v_ready, i * 2 + u + 1)
                        for n in range(NSTEP):
                            if n + 2 < NSTEP:
                                scores(n + 2)
                            sums(n)
                            if n >= 1:
                                values(n - 1)
                        values(NSTEP - 1)

            @block.vector
            def _(dve):
                with dve.Fori(0, HEADS // 2) as i:
                    for u in range(2):
                        base = i * (2 * NSTEP) + u * NSTEP
                        bias = bias_v[:, u:u + 1]
                        dve.tensor_copy(bias, s["par"][:, bass.ds(i * 2 + (u + W_SB), 1)]).then_inc(bias_in_v, 1)
                        dve.wait_ge(bias_in_v, i * 2 + u + 1)

                        def clamp(n):
                            _, _, off = STEPS[n]
                            dve.wait_ge(z_ready, base + n + 1)
                            if n >= 3:
                                dve.wait_ge(weighted, base + n - 2)
                            dve.tensor_scalar(soft[:, n % 3, off:HALF], zs[:, n % 4, off:HALF], bias, CLAMP,
                                              ALU.add, ALU.min).then_inc(clamped, 1)

                        def soften(n):
                            half, kb, off = STEPS[n]
                            dve.wait_ge(logged, base + n + 1)
                            x = soft[:, n % 3, :]
                            ins = dve.scalar_tensor_tensor(x[:, off:HALF], zs[:, n % 4, off:HALF], bias,
                                                           x[:, off:HALF], ALU.add, ALU.max)
                            if kb >= 4 * half:
                                ins.then_inc(masked, 1)
                                dve.wait_ge(masked, i * (2 * NDIAG) + u * NDIAG + diag_no[n] + 1)
                                ins = dve.tensor_tensor(x[:, off:off + P], x[:, off:off + P], strict, ALU.mult)
                            ins.then_inc(soft_ready, 1)
                            if kb == 0:
                                return
                            dve.wait_ge(soft_ready, base + n + 1)
                            if n >= 1:
                                dve.wait_ge(weighted, base + n)
                            now, then = later[:, n % 2, :], later[:, (n + 1) % 2, :]
                            if kb >= 4 * half:
                                ins = dve.tensor_copy(then[:, off:off + P], x[:, off:off + P])
                                off += P
                            if off < HALF:
                                if n >= 1:
                                    dve.wait_ge(later_ready, i * (2 * NLATER) + u * NLATER + later_no[n])
                                ins = dve.tensor_tensor(then[:, off:HALF], now[:, off:HALF], x[:, off:HALF],
                                                        ALU.add)
                            ins.then_inc(later_ready, 1)

                        def mask(n):
                            half, kb, off = STEPS[n]
                            if kb >= 4 * half:
                                dve.wait_ge(w_ready, base + n + 1)
                                x = wgt[:, n % 2, off:off + P]
                                dve.tensor_tensor(x, x, strict, ALU.mult).then_inc(w_masked, 1)

                        clamp(0)
                        for n in range(NSTEP):
                            if n + 1 < NSTEP:
                                clamp(n + 1)
                            soften(n)
                            if n >= 1:
                                mask(n - 1)

            @block.scalar
            def _(act):
                act.preload_act_table_set("natural_log_exp_and_others")
                act.sem_inc(o_taken, 2)
                for u in range(2):
                    act.sem_inc(o_out[u], 16)
                with act.Fori(0, HEADS // 2) as i:
                    for u in range(2):
                        base = i * (2 * NSTEP) + u * NSTEP
                        bias = bias_a[:, u:u + 1]
                        act.copy(bias, s["par"][:, bass.ds(i * 2 + (u + W_SB), 1)]).then_inc(bias_in_a, 1)
                        act.wait_ge(bias_in_a, i * 2 + u + 1)

                        def log(n):
                            _, _, off = STEPS[n]
                            x = soft[:, n % 3, off:HALF]
                            act.wait_ge(clamped, base + n + 1)
                            act.activation(x, x, ACT.Exp).then_inc(exped, 1)
                            act.wait_ge(exped, base + n + 1)
                            act.activation(x, x, ACT.Ln, bias=1.0).then_inc(logged, 1)

                        def weigh(n):
                            _, _, off = STEPS[n]
                            act.wait_ge(weighted, base + n + 1)
                            if n >= 2:
                                act.wait_ge(pv_done, base + n - 1)
                            act.activation(wgt[:, n % 2, off:HALF], zs[:, n % 4, off:HALF], ACT.Exp,
                                           bias=bias).then_inc(w_ready, 1)

                        def take(half, after):
                            act.wait_ge(pv_done, base + after)
                            act.copy(out[:, u, half * HALF:(half + 1) * HALF],
                                     os_[0:HD, half, :]).then_inc(o_taken, 1)

                        log(0)
                        act.wait_ge(o_out[u], (i + 1) * 16)
                        for n in range(1, NSTEP):
                            log(n)
                            weigh(n - 1)
                            if n == 7:
                                take(0, 4)
                        weigh(NSTEP - 1)
                        take(1, NSTEP)
                        act.wait_ge(o_taken, i * 4 + u * 2 + 4)
                        act.dma_start(a["o"][bass.ds((i * 2 + u) * HD, HD), 0:SEQ],
                                      out[:, u, :]).then_inc(o_out[u], 16)


def attend_sample_phase(nc, a, s, sem):
    with ExitStack() as ctx:
        def sb(name, shape, dt=F32):
            return ctx.enter_context(nc.sbuf_tensor(name, shape, dt))

        NC_ = AW // P
        pages = sb("pages", [1, NSEQ * NPAGE], I32)
        kp = sb("kp", [P, 2, NPAGE, AW])
        vp = sb("vp", [P, 2, NPAGE, AW])
        qd = sb("qd", [P, NC_, TS])
        qz = sb("qz", [P, NSEQ, NC_, 2, LS])
        qn = sb("qn", [HD, HEADS, TS])
        kn = sb("kn", [HD, HEADS, TS])
        bias = sb("bias_cols", [P, HEADS, LS])
        z_new = sb("z_new", [TS, HEADS, TS])
        soft_new = sb("soft_new", [P, HEADS, TS])
        w_new = sb("w_new", [P, HEADS, TS])
        z = sb("z_past", [P, 2, NPAGE, TS])
        soft = sb("soft_past", [P, 2, NPAGE, TS])
        later = sb("later_past", [P, 2, NPAGE, TS])
        o = sb("o_sample", [P, NC_, TS])
        zs = ctx.enter_context(nc.psum_tensor("zp_ps", [P, 2, 512], F32))
        os_ = ctx.enter_context(nc.psum_tensor("op_ps", [P, 2, 512], F32))
        zn = ctx.enter_context(nc.psum_tensor("zn_ps", [P, 512], F32))
        pages_in, q_in = sem("pages_in"), sem("q_in")
        k_in = [sem(f"k_page_in{u}") for u in range(2)]
        v_in = [sem(f"v_page_in{u}") for u in range(2)]
        ready, zn_done, sn_done, new_act, new_ready = (
            sem("q_blocks_ready"), sem("zn_done"), sem("sn_done"), sem("new_act"), sem("new_ready"))
        chain = sem("sample_chain")
        zp_done, sp_done, op_done = sem("zp_done"), sem("sp_done"), sem("op_done")
        clamped, exped, logged, softened, arg_ready, w_ready, o_taken, o_out = (
            sem("s_clamped"), sem("s_exped"), sem("s_logged"), sem("s_softened"), sem("s_arg"), sem("s_w"),
            sem("s_o_taken"), sem("s_o_out"))
        const = s["const"]
        ntri, neg = const[:, C_NTRI:C_NTRI + P], const[:, C_NEG:C_NEG + P]

        with nc.Block() as block:
            @block.sync
            def _(sp):
                sp.dma_start(pages[:, :], a["pages"]).then_inc(pages_in, 16)
                sp.dma_start(qd[:, :, :], a["proj"][0:NC_, :, SEQ:T].rearrange("c p t -> p c t")).then_inc(q_in, 16)
                by_head = a["proj"][0:NC_].rearrange("c (g d) t -> d (c g) t", g=2)
                sp.dma_start(qn[:, :, :], by_head[:, :, SEQ:T]).then_inc(q_in, 16)
                by_head = a["k_out"].rearrange("c (g d) t -> d (c g) t", g=2)
                sp.dma_start(kn[:, :, :], by_head[:, :, SEQ:T]).then_inc(q_in, 16)
                sp.wait_ge(pages_in, 16)

                with sp.Fori(0, NSEQ // 2) as i:
                    for u in range(2):
                        sp.wait_ge(zp_done, i * 2 + u + 1)
                        for j in range(NPAGE):
                            at = bass.ds((i * 2 + u) * NPAGE + j, 1)
                            page = sp.value_load(pages[0:1, at], min_val=0, max_val=POOL - 1)
                            sp.dma_start(kp[:, u, j, :], a["cache_k"][bass.ds(page, 1)].rearrange(
                                "o p c k -> (o p) (c k)")).then_inc(k_in[u], 16)
                sp.wait_ge(o_taken, NSEQ + 2)
                for c in range(NC_):
                    sp.dma_start(a["o"][c * P:(c + 1) * P, SEQ:T], o[:, c, :]).then_inc(o_out, 16)
                sp.wait_ge(o_out, 16 * NC_)

            @block.gpsimd
            def _(pool):
                pool.wait_ge(pages_in, 16)
                with pool.Fori(0, NSEQ // 2) as i:
                    for u in range(2):
                        pool.wait_ge(op_done, i * 2 + u + 1)
                        for j in range(NPAGE):
                            at = bass.ds((i * 2 + u) * NPAGE + j, 1)
                            page = pool.value_load(pages[0:1, at], min_val=0, max_val=POOL - 1)
                            pool.dma_start(vp[:, u, j, :], a["cache_v"][bass.ds(page, 1)].rearrange(
                                "o k c -> (o k) c")).then_inc(v_in[u], 16)

            @block.tensor
            def _(pe):
                pe.sem_inc(op_done, 2)
                pe.sem_inc(zp_done, 2)
                pe.wait_ge(q_in, 48)
                for h in range(HEADS):
                    mm = pe.matmul(zn[0:TS, h * TS:(h + 1) * TS], kn[:, h, :], qn[:, h, :],
                                   start=(h == 0), stop=True, skip_group_check=True)
                mm.then_inc(zn_done, 1)
                pe.wait_ge(new_ready, 1)
                pe.matmul(zn[0:TS, :], ntri[0:TS, 0:TS], soft_new[0:TS, :, :], start=False, stop=True,
                          skip_group_check=True).then_inc(sn_done, 1)
                pe.wait_ge(ready, 1)

                def scores(seq, i, u):
                    pe.wait_ge(k_in[u], (i + 1) * (16 * NPAGE))
                    for j in range(NPAGE):
                        for c in range(NC_):
                            col = (j * NC_ + c) * 2 * LS
                            rhs = qz[:, bass.ds(seq, 1), c, :, :].rearrange("p o g l -> p (o g l)")
                            mm = pe.matmul(zs[:, u, col:col + 2 * LS], kp[:, u, j, c * P:(c + 1) * P], rhs,
                                           start=(j == 0 and c == 0), stop=True, skip_group_check=True)
                    mm.then_inc(zp_done, 1)

                def rest(seq, i, u):
                    pe.wait_ge(softened, seq + 1)
                    pe.matmul(zs[:, u, :], ntri, soft[:, u, :, :], start=False, stop=True,
                              skip_group_check=True)
                    pe.matmul(zs[:, u, :], neg, later[:, u, :, :], start=False, stop=True,
                              skip_group_check=True).then_inc(sp_done, 1)
                    pe.wait_ge(w_ready, seq + 1)
                    pe.wait_ge(v_in[u], (i + 1) * (16 * NPAGE))
                    pe.wait_ge(o_taken, seq + 1)
                    for c in range(NC_):
                        out = os_[:, u, c * 2 * LS:(c + 1) * 2 * LS]
                        for j in range(NPAGE):
                            pe.matmul(out, vp[:, u, j, c * P:(c + 1) * P], z[:, u, j, c * 2 * LS:(c + 1) * 2 * LS],
                                      start=(j == 0), stop=False)
                        mm = pe.matmul(out, s["v_tok"][:, TILES, c * P:(c + 1) * P],
                                       w_new[:, 2 * c:2 * c + 2, bass.ds(seq * LS, LS)], start=False, stop=True)
                    mm.then_inc(op_done, 1)

                pe.wait_ge(new_ready, 2)
                scores(0, 0, 0)
                with pe.Fori(0, NSEQ // 2 - 1) as i:
                    scores(i * 2 + 1, i, 1)
                    rest(i * 2, i, 0)
                    scores(i * 2 + 2, i + 1, 0)
                    rest(i * 2 + 1, i, 1)
                scores(NSEQ - 1, NSEQ // 2 - 1, 1)
                rest(NSEQ - 2, NSEQ // 2 - 1, 0)
                rest(NSEQ - 1, NSEQ // 2 - 1, 1)

            @block.vector
            def _(dve):
                link = Chain(dve, chain)
                dve.memset(qz[:, :, :, :, :], 0.0)
                dve.memset(soft_new[:, :, :], 0.0)
                link.link(dve.memset(w_new[:, :, :], 0.0))
                cols = s["par"][:, W_SB:W_SB + HEADS]
                link.mark(dve.tensor_copy(bias[:, :, :], cols.unsqueeze(2).to_broadcast([P, HEADS, LS])))
                dve.wait_ge(q_in, 48)
                for g in range(2):
                    rows = slice(g * HD, (g + 1) * HD)
                    for c in range(NC_):
                        ins = dve.tensor_copy(qz[rows, :, c, g, :],
                                              qd[rows, c, :].rearrange("p (s l) -> p s l", l=LS))
                ins.then_inc(ready, 1)
                dve.wait_ge(zn_done, 1)
                b_new = s["par"][0:TS, W_SB:W_SB + HEADS].unsqueeze(2).to_broadcast([TS, HEADS, TS])
                strict = const[0:TS, C_BSTRICT:C_BSTRICT + TS].unsqueeze(1).to_broadcast([TS, HEADS, TS])
                zn3 = zn[0:TS, :].rearrange("p (h t) -> p h t", t=TS)
                sn = soft_new[0:TS, :, :]
                wn = w_new[0:TS, :, :]
                link.link(dve.tensor_tensor(z_new[:, :, :], zn3, b_new, ALU.add))
                dve.tensor_scalar(sn, z_new[:, :, :], CLAMP, None, ALU.min).then_inc(clamped, 1)
                dve.wait_ge(new_act, 2)
                link.link(dve.tensor_tensor(sn, sn, z_new[:, :, :], ALU.max))
                dve.tensor_tensor(sn, sn, strict, ALU.mult).then_inc(new_ready, 1)
                dve.wait_ge(sn_done, 1)
                dve.tensor_tensor(wn, zn3, b_new, ALU.add).then_inc(arg_ready, 1)
                dve.wait_ge(new_act, 3)
                dve.tensor_tensor(wn, wn, strict, ALU.mult).then_inc(new_ready, 1)

                b4 = bias[:, :, :].rearrange("p h l -> p (h l)").unsqueeze(1).to_broadcast([P, NPAGE, TS])

                def first(seq, u):
                    dve.wait_ge(zp_done, seq + 3)
                    link.link(dve.tensor_tensor(z[:, u, :, :], zs[:, u, :].rearrange("p (j n) -> p j n", n=TS),
                                                b4, ALU.add))
                    dve.tensor_scalar(soft[:, u, :, :], z[:, u, :, :], CLAMP, None, ALU.min).then_inc(clamped, 1)

                def second(seq, u):
                    dve.wait_ge(logged, seq + 1)
                    new = soft_new[:, :, bass.ds(seq * LS, LS)]
                    dve.tensor_copy(later[:, u, NPAGE - 1, :].rearrange("p (h l) -> p h l", l=LS), new)
                    link.link(dve.tensor_tensor(soft[:, u, :, :], soft[:, u, :, :], z[:, u, :, :], ALU.max))
                    for j in range(NPAGE - 2, -1, -1):
                        ins = dve.tensor_tensor(later[:, u, j, :], later[:, u, j + 1, :], soft[:, u, j + 1, :],
                                                ALU.add)
                        if j:
                            link.link(ins)
                    ins.then_inc(softened, 1)
                    dve.wait_ge(sp_done, seq + 1)
                    dve.tensor_tensor(z[:, u, :, :], zs[:, u, :].rearrange("p (j n) -> p j n", n=TS),
                                      b4, ALU.add).then_inc(arg_ready, 1)

                with dve.Fori(0, NSEQ // 2) as i, link.turns(i, NSEQ // 2, 2 * NPAGE):
                    for u in range(2):
                        first(i * 2 + u, u)
                        second(i * 2 + u, u)

            @block.scalar
            def _(act):
                act.preload_act_table_set("natural_log_exp_and_others")
                act.sem_inc(o_taken, 2)
                sn, wn = soft_new[0:TS, :, :], w_new[0:TS, :, :]
                act.wait_ge(clamped, 1)
                act.activation(sn, sn, ACT.Exp).then_inc(new_act, 1)
                act.wait_ge(new_act, 1)
                act.activation(sn, sn, ACT.Ln, bias=1.0).then_inc(new_act, 1)
                act.wait_ge(arg_ready, 1)
                act.activation(wn, wn, ACT.Exp).then_inc(new_act, 1)
                with act.Fori(0, NSEQ // 2) as i:
                    for u in range(2):
                        seq = i * 2 + u
                        x = soft[:, u, :, :]
                        act.wait_ge(clamped, seq + 2)
                        act.activation(x, x, ACT.Exp).then_inc(exped, 1)
                        act.wait_ge(exped, seq + 1)
                        act.activation(x, x, ACT.Ln, bias=1.0).then_inc(logged, 1)
                        act.wait_ge(arg_ready, seq + 2)
                        act.activation(z[:, u, :, :], z[:, u, :, :], ACT.Exp).then_inc(w_ready, 1)
                        act.wait_ge(op_done, seq + 3)
                        for g in range(2):
                            rows = slice(g * HD, (g + 1) * HD)
                            src = os_[rows, u, 0:TS].rearrange("p (c g l) -> p c g l", g=2, l=LS)
                            ins = act.copy(o[rows, :, bass.ds(seq * LS, LS)], src[:, :, g, :])
                        ins.then_inc(o_taken, 1)


def ssd_phase(nc, a, s, sem):
    with ExitStack() as ctx:
        def sb(name, shape):
            return ctx.enter_context(nc.sbuf_tensor(name, shape, F32))

        def ps(name, cols):
            return ctx.enter_context(nc.psum_tensor(name, [P, cols], F32))

        NX = CONV // P
        PER_G = SH // NG
        xc = sb("xc", [P, 2, NX, P])
        zc = sb("zc", [P, 2, KC, P])
        st = sb("st", [P, D])
        dta = sb("dta", [P, TILES + 1, SH])
        neg_a = sb("neg_a", [P, SH])
        dt_c = sb("dt_c", [P, SH])
        dta_c = sb("dta_c", [P, SH])
        acs = sb("acs", [P, SH])
        xdt = sb("xdt", [P, SH, SP_])
        xend = sb("xend", [P, SH, SP_])
        btok = sb("btok", [P, NG, NST])
        cbm = sb("cbm", [P, NG, P])
        seg = sb("seg", [P, SH, P])
        grow = sb("grow", [P, SH, P])
        end = sb("end", [P, SH])
        decay = sb("decay", [P, SH])
        xt_ps = ps("xt_ps", 1024)
        bc_ps, acs_ps, ab_ps = ps("bc_ps", 512), ps("acs_ps", 512), ps("ab_ps", 2048)
        y_ps, st_ps = xt_ps, ab_ps
        in_ = [sem(f"ssd_in{u}") for u in range(2)]
        dta_done, dt_ready, head_done, spread = sem("dta_done"), sem("dt_ready"), sem("head_done"), sem("spread")
        seg_ready, grown, seg_exp, tail_in, y_done, st_done, taken = (
            sem("seg_ready"), sem("grown"), sem("seg_exp"), sem("tail_in"), sem("y_done"), sem("st_done"),
            sem("ssd_taken"))
        b_ready = sem("b_ready")
        dt_act = sem("dt_act")
        chain = sem("ssd_chain")
        h0_in, st_out = [sem(f"h0_in{u}") for u in range(2)], [sem(f"st_out{u}") for u in range(2)]
        last_out = sem("last_out")
        own_b, s_free = sem("own_b"), sem("s_free")
        const, par = s["const"], s["par"]
        ident = const[:, C_ID:C_ID + P]
        h0 = sb("h0", [P, 2, D])
        bseq = sb("bseq", [P, 2, NG, NST])
        growth = sb("growth", [P, SH, NSEQ])
        h1 = sb("h1", [P, 2, D])

        def heads(t, g):
            return t[:, g * PER_G:(g + 1) * PER_G, :]

        with nc.Block() as block:
            @block.sync
            def _(sp):
                def load(chunk, u):
                    cols = bass.ds(chunk * P, P)
                    x_rows = a["proj"][CH_X:CH_X + NX].rearrange("c p t -> p c t")
                    z_rows = a["proj"][CH_Z:CH_Z + KC].rearrange("c p t -> p c t")
                    sp.dma_start(xc[:, u, :, :], x_rows[:, :, cols]).then_inc(in_[u], 16)
                    sp.dma_start(zc[:, u, :, :], z_rows[:, :, cols]).then_inc(in_[u], 16)

                with sp.Fori(0, TILES // 2) as i:
                    for u in range(2):
                        sp.wait_ge(taken, i * 2 + u + 1)
                        load(i * 2 + u, u)
                sp.wait_ge(taken, TILES + 1)
                sp.dma_start(xc[:, 0, :, 0:TS],
                             a["proj"][CH_X:CH_X + NX].rearrange("c p t -> p c t")[:, :, SEQ:T]).then_inc(in_[0], 16)
                sp.dma_start(zc[:, 0, :, 0:TS],
                             a["proj"][CH_Z:CH_Z + KC].rearrange("c p t -> p c t")[:, :, SEQ:T]).then_inc(in_[0], 16)
                sp.wait_ge(taken, TILES + 2)
                sp.dma_start(a["ssm_out"][0], st[:, :]).then_inc(last_out, 16)
                for q in range(NSEQ):
                    if q >= 2:
                        sp.wait_ge(s_free, q - 1)
                    sp.dma_start(h0[:, q % 2, :], a["state_ssm"][q]).then_inc(h0_in[q % 2], 16)
                    if q >= 1:
                        sp.wait_ge(s_free, q)
                        sp.dma_start(a["ssm_out"][q], h1[:, (q - 1) % 2, :]).then_inc(st_out[(q - 1) % 2], 16)
                sp.wait_ge(s_free, NSEQ)
                sp.dma_start(a["ssm_out"][NSEQ], h1[:, (NSEQ - 1) % 2, :]).then_inc(st_out[(NSEQ - 1) % 2], 16)
                for u in range(2):
                    sp.wait_ge(st_out[u], 16 * (NSEQ // 2))
                sp.wait_ge(last_out, 16)

            @block.tensor
            def _(pe):
                def first(chunk, n, u, tri, loads):
                    x = xc[:, u, :, 0:n]
                    pe.wait_ge(in_[u], loads)
                    pe.wait_ge(taken, chunk + 2)
                    for c in range(KC):
                        mm = pe.transpose(xt_ps[0:n, c * P:(c + 1) * P], x[:, c, :], ident)
                    mm.then_inc(head_done, 1)
                    for g in range(NG):
                        pe.transpose(bc_ps[0:n, g * NST:(g + 1) * NST], x[:, KC + g, :], ident)
                        mm = pe.matmul(bc_ps[0:n, 256 + g * P:256 + g * P + n], x[:, KC + g, :],
                                       x[:, KC + NG + g, :], start=True, stop=True)
                    mm.then_inc(head_done, 1)
                    pe.wait_ge(dt_ready, chunk + 1)
                    pe.matmul(acs_ps[0:n, 0:SH], tri[0:n, 0:n], dta_c[0:n, :], start=True,
                              stop=True).then_inc(head_done, 1)
                    for h in range(SH):
                        mm = pe.matmul(ab_ps[:, h * P:h * P + n], dta_c[0:n, h:h + 1].to_broadcast([n, P]),
                                       tri[0:n, 0:n], start=True, stop=True)
                        if h % 4 == 3:
                            mm.then_inc(spread, 1)

                with pe.Fori(0, TILES // 2) as i:
                    for u in range(2):
                        chunk = i * 2 + u
                        first(chunk, P, u, const[:, C_TRI:C_TRI + P], (i + 1) * 32)
                        pe.wait_ge(tail_in, chunk + 1)
                        for h in range(SH):
                            rows, c = (h % 2) * SP_, h // 2
                            out = y_ps[rows:rows + SP_, c * P:(c + 1) * P]
                            pe.matmul(out, xdt[:, h, :], seg[:, h, :], start=True, stop=False)
                            mm = pe.matmul(out, st[:, h * SP_:(h + 1) * SP_], grow[:, h, :], start=False, stop=True)
                        mm.then_inc(y_done, 1)
                        for g in range(NG):
                            mm = pe.matmul(st_ps[:, g * 512:(g + 1) * 512], btok[:, g, :], heads(xend, g),
                                           start=True, stop=True)
                        mm.then_inc(st_done, 1)
                n = TS
                first(TILES, n, 0, const[:, C_BTRI:C_BTRI + TS], TILES // 2 * 32 + 32)
                pe.wait_ge(tail_in, TILES + 1)
                for h in range(SH):
                    rows, c = (h % 2) * SP_, h // 2
                    pe.matmul(y_ps[rows:rows + SP_, c * P:c * P + n], xdt[0:n, h, :], seg[0:n, h, 0:n],
                              start=(c % 4 == 0), stop=True, skip_group_check=True)
                for q in range(NSEQ):
                    pe.wait_ge(h0_in[q % 2], 16 * (q // 2 + 1))
                    for h in range(SH):
                        rows, c = (h % 2) * SP_, h // 2
                        mm = pe.matmul(y_ps[rows:rows + SP_, c * P + q * LS:c * P + (q + 1) * LS],
                                       h0[:, q % 2, h * SP_:(h + 1) * SP_], grow[:, h, q * LS:(q + 1) * LS],
                                       start=False, stop=True, skip_group_check=True)
                    if q == NSEQ - 1:
                        mm.then_inc(y_done, 1)
                    pe.wait_ge(own_b, q + 1)
                    if q:
                        pe.wait_ge(s_free, q)
                    for g in range(NG):
                        mm = pe.matmul(st_ps[:, g * 512:(g + 1) * 512], bseq[0:n, q % 2, g, :],
                                       heads(xend, g)[0:n], start=True, stop=True)
                    mm.then_inc(st_done, 1)

            @block.scalar
            def _(act):
                act.wait_ge(dta_done, 1)
                for x in (s["dt_tok"][:, 0:TILES, :], s["dt_tok"][0:TS, TILES, :]):
                    act.activation(x, x, ACT.Exp)
                act.activation(neg_a[:, :], par[:, W_AL:W_AL + SH], ACT.Exp).then_inc(dt_act, 1)
                act.wait_ge(dt_act, 1)
                act.activation(s["dt_tok"][:, 0:TILES, :], s["dt_tok"][:, 0:TILES, :], ACT.Ln, bias=1.0)
                act.activation(s["dt_tok"][0:TS, TILES, :], s["dt_tok"][0:TS, TILES, :], ACT.Ln,
                               bias=1.0).then_inc(dt_act, 1)

                def middle(chunk, n):
                    act.wait_ge(head_done, chunk * 3 + 2)
                    act.copy(btok[0:n, :, :],
                             bc_ps[0:n, 0:256].rearrange("p (g k) -> p g k", g=NG)).then_inc(b_ready, 1)
                    for b in range(4):
                        act.wait_ge(spread, chunk * 4 + b + 1)
                        src = ab_ps[:, b * 512:(b + 1) * 512].rearrange("p (h i) -> p h i", i=P)
                        act.activation(grow[:, b * 4:(b + 1) * 4, 0:n], src[:, :, 0:n], ACT.Exp).then_inc(grown, 1)
                    act.wait_ge(seg_ready, chunk + 1)
                    act.activation(seg[0:n, :, 0:n], seg[0:n, :, 0:n], ACT.Exp).then_inc(seg_exp, 1)

                with act.Fori(0, TILES // 2) as i:
                    for u in range(2):
                        middle(i * 2 + u, P)
                middle(TILES, TS)

            @block.vector
            def _(dve):
                link = Chain(dve, chain)
                dve.sem_inc(taken, 2)
                link.mark(dve.memset(st[:, :], 0.0))
                dve.tensor_copy(dta[:, 0:TILES, :], s["dt_tok"][:, 0:TILES, :])
                link.link(dve.tensor_copy(dta[0:TS, TILES, :], s["dt_tok"][0:TS, TILES, :]))
                dve.tensor_scalar(s["dt_tok"][:, 0:TILES, :], dta[:, 0:TILES, :], CLAMP, None, ALU.min)
                dve.tensor_scalar(s["dt_tok"][0:TS, TILES, :], dta[0:TS, TILES, :], CLAMP, None,
                                  ALU.min).then_inc(dta_done, 1)
                dve.wait_ge(dt_act, 2)
                for rows, t in ((P, slice(0, TILES)), (TS, slice(TILES, TILES + 1))):
                    dt = s["dt_tok"][0:rows, t, :]
                    link.link(dve.tensor_tensor(dt, dt, dta[0:rows, t, :], ALU.max))
                    w = neg_a[0:rows, :].unsqueeze(1).to_broadcast([rows, t.stop - t.start, SH])
                    link.link(dve.scalar_tensor_tensor(dta[0:rows, t, :], dt, -1.0, w, ALU.mult, ALU.mult))

                def start(chunk, n, u, tri):
                    at = bass.ds(chunk, 1) if not isinstance(chunk, int) else slice(chunk, chunk + 1)
                    dve.tensor_copy(dt_c[0:n, :], s["dt_tok"][0:n, at, :].rearrange("p o h -> p (o h)"))
                    dve.tensor_copy(dta_c[0:n, :],
                                    dta[0:n, at, :].rearrange("p o h -> p (o h)")).then_inc(dt_ready, 1)
                    dve.wait_ge(dt_ready, chunk + 1)
                    dve.wait_ge(head_done, chunk * 3 + 1)
                    for g in range(NG):
                        link.mark(dve.tensor_tensor(
                            heads(xdt, g)[0:n],
                            xt_ps[0:n, g * 512:(g + 1) * 512].rearrange("p (h k) -> p h k", k=SP_),
                            dt_c[0:n, g * PER_G:(g + 1) * PER_G].unsqueeze(2).to_broadcast([n, PER_G, SP_]),
                            ALU.mult))
                    dve.wait_ge(b_ready, chunk + 1)
                    cb = bc_ps[0:n, 256:512].rearrange("p (g i) -> p g i", g=NG)[:, :, 0:n]
                    link.mark(dve.tensor_tensor(cbm[0:n, :, 0:n], cb,
                                                tri[0:n, 0:n].unsqueeze(1).to_broadcast([n, NG, n]), ALU.mult))
                    dve.wait_ge(head_done, chunk * 3 + 3)
                    link.link(dve.tensor_copy(acs[0:n, :], acs_ps[0:n, 0:SH]))
                    for h in range(SH):
                        if h % 4 == 0:
                            dve.wait_ge(grown, chunk * 4 + h // 4 + 1)
                        ins = dve.tensor_scalar(seg[0:n, h, 0:n], ab_ps[0:n, h * P:h * P + n], acs[0:n, h:h + 1],
                                                0.0, ALU.subtract, ALU.min)
                    ins.then_inc(seg_ready, 1)

                def scale(chunk, n, u):
                    if n == P:
                        link.link(dve.tensor_copy(decay[:, :], grow[:, :, P - 1]))
                    else:
                        own = grow[:, :, 0:n].rearrange("p h (q l) -> p h q l", l=LS)[:, :, :, LS - 1]
                        link.link(dve.tensor_copy(growth[:, :, :], own))
                    for g in range(NG):
                        ct = xc[:, u, KC + NG + g, 0:n].unsqueeze(1).to_broadcast([P, PER_G, n])
                        x = heads(grow, g)[:, :, 0:n]
                        link.mark(dve.tensor_tensor(x, x, ct, ALU.mult))
                    dve.wait_ge(seg_exp, chunk + 1)

                def kernel_(n):
                    for g in range(NG):
                        x = heads(seg, g)[0:n, :, 0:n]
                        link.mark(dve.tensor_tensor(
                            x, x, cbm[0:n, g, 0:n].unsqueeze(1).to_broadcast([n, PER_G, n]), ALU.mult))

                def close(chunk, t, n, u):
                    y = s["y"][:, :, t]
                    for c in range(KC):
                        ins = dve.scalar_tensor_tensor(y[:, c, :], xc[:, u, c, 0:n],
                                                       par[:, W_DSKIP + c:W_DSKIP + c + 1],
                                                       y_ps[:, c * P:c * P + n], ALU.mult, ALU.add)
                    link.link(ins)
                    dve.tensor_tensor(y, y, zc[:, u, :, 0:n], ALU.mult).then_inc(taken, 1)

                with dve.Fori(0, TILES // 2) as i, link.turns(i, TILES // 2, 2 * 14):
                    for u in range(2):
                        chunk = i * 2 + u
                        start(chunk, P, u, const[:, C_TRI:C_TRI + P])
                        scale(chunk, P, u)
                        link.link(dve.tensor_copy(end[:, :], seg[:, :, P - 1]))
                        kernel_(P)
                        dve.tensor_tensor(xend[:, :, :], xdt[:, :, :],
                                          end[:, :].unsqueeze(2).to_broadcast([P, SH, SP_]),
                                          ALU.mult).then_inc(tail_in, 1)
                        dve.wait_ge(st_done, chunk + 1)
                        st3 = st[:, :].rearrange("p (h k) -> p h k", k=SP_)
                        link.link(dve.tensor_tensor(st3, st3,
                                                    decay[:, :].unsqueeze(2).to_broadcast([P, SH, SP_]), ALU.mult))
                        dve.wait_ge(y_done, chunk + 1)
                        ins = dve.tensor_tensor(st[:, 0:512], st[:, 0:512], st_ps[:, 0:512], ALU.add)
                        link.mark(ins)
                        link.mark(dve.tensor_tensor(st[:, 512:], st[:, 512:], st_ps[:, 512:1024], ALU.add))
                        close(chunk, bass.ds(chunk * P, P), P, u)
                n = TS
                start(TILES, n, 0, const[:, C_BTRI:C_BTRI + TS])
                scale(TILES, n, 0)
                last = seg[0:n, :, 0:n].rearrange("p h (q l) -> p h q l", l=LS)[:, :, :, LS - 1]
                pick = h1[0:n, 0, 0:SH * NSEQ].rearrange("p (h q) -> p h q", q=NSEQ)
                mask = const[0:n, C_SEQ:C_SEQ + NSEQ]
                link.link(dve.tensor_tensor(pick, last, mask.unsqueeze(1).to_broadcast([n, SH, NSEQ]), ALU.mult))
                link.link(dve.tensor_reduce(end[0:n, :], pick, AX.X, ALU.add))
                kernel_(n)
                dve.tensor_tensor(xend[0:n, :, :], xdt[0:n, :, :],
                                  end[0:n, :].unsqueeze(2).to_broadcast([n, SH, SP_]), ALU.mult).then_inc(tail_in, 1)
                for q in range(NSEQ):
                    slot = q % 2
                    if q >= 2:
                        dve.wait_ge(st_done, TILES + q - 1)
                        dve.wait_ge(st_out[slot], 16 * (q // 2))
                    dve.tensor_scalar(bseq[0:n, slot, :, :], btok[0:n, :, :], mask[:, q:q + 1], None,
                                      ALU.mult).then_inc(own_b, 1)
                    dve.wait_ge(h0_in[slot], 16 * (q // 2 + 1))
                    link.link(dve.tensor_tensor(
                        h1[:, slot, :].rearrange("p (h k) -> p h k", k=SP_),
                        h0[:, slot, :].rearrange("p (h k) -> p h k", k=SP_),
                        growth[:, :, q].unsqueeze(2).to_broadcast([P, SH, SP_]), ALU.mult))
                    dve.wait_ge(st_done, TILES + q + 1)
                    dve.tensor_tensor(h1[:, slot, :], h1[:, slot, :], st_ps[:, 0:1024], ALU.add).then_inc(s_free, 1)
                dve.wait_ge(y_done, TILES + 1)
                close(TILES, slice(SEQ, T), n, 0)
                dve.wait_ge(taken, TILES + 3)


def add_gated(dve, link, dst, gate, src, src_sample, spare):
    for t0, ap in src:
        n = ap.shape[-1]
        dve.scalar_tensor_tensor(dst[:, t0:t0 + n], ap, gate[:, 0:1], dst[:, t0:t0 + n], ALU.mult, ALU.add)
    own = dst[:, SEQ:T].rearrange("p (q l) -> p q l", l=LS)
    g = gate[:, 1:].unsqueeze(2).to_broadcast([P, NSEQ, LS])
    link.link(dve.tensor_tensor(spare, src_sample.rearrange("p (q l) -> p q l", l=LS), g, ALU.mult))
    return dve.tensor_tensor(own, own, spare, ALU.add)


def merge_phase(nc, a, s, sem):
    with ExitStack() as ctx:
        def sb(name, shape):
            return ctx.enter_context(nc.sbuf_tensor(name, shape, F32))

        NA = AW // P
        o = sb("o_all", [P, NA, T])
        wa = sb("wa", [P, 2, NA, P])
        wb = sb("wb", [P, 2, KC, P])
        gates = sb("gates", [P, 2, 2, T])
        part = sb("part", [P, NS, 384])
        spare = sb("spare", [P, 2, NSEQ, LS])
        ps = ctx.enter_context(nc.psum_tensor("merge_ps", [P, 2 * NS, 512], F32))
        o_in = sem("o_in")
        br_in = [sem(f"br_in{u}") for u in range(2)]
        out_in = [sem(f"out_in{u}") for u in range(2)]
        y_ready, br_done, br_taken, parted = sem("y_ready"), sem("br_done"), sem("br_taken"), sem("parted")
        mix_done, mix_taken, x_out, h_ready = sem("mix_done"), sem("mix_taken"), sem("x_out"), sem("h2_ready")
        banks_taken = sem("banks_taken")
        chain = sem("merge_chain")
        y, h, x = s["y"], s["h"], s["x"]
        HALF_C = KC // NG
        group = [Norm(nc, sem, f"group{g}", y[:, g * HALF_C:(g + 1) * HALF_C, :],
                      h[:, g * HALF_C:(g + 1) * HALF_C, :], s, ps, HALF_C) for g in range(NG)]
        norm = Norm(nc, sem, "norm2", x, y, s, ps)

        with nc.Block() as block:
            @block.sync
            def _(sp):
                sp.dma_start(o[:, :, :], a["o"].rearrange("(c p) t -> p c t", p=P)).then_inc(o_in, 16)

                def branch(m, u):
                    sp.dma_start(wa[:, u, :, :], a["w_attn"][m]).then_inc(br_in[u], 16)
                    sp.dma_start(wb[:, u, :, :], a["w_ssm"][m]).then_inc(br_in[u], 16)
                    sp.dma_start(gates[:, u, 0, :], a["proj"][m + CH_G]).then_inc(br_in[u], 16)
                    sp.dma_start(gates[:, u, 1, :], a["proj"][m + (CH_G + KC)]).then_inc(br_in[u], 16)

                for u in range(2):
                    branch(u, u)
                with sp.Fori(1, KC // 2) as i:
                    for u in range(2):
                        sp.wait_ge(br_taken, (i - 1) * (2 * NS) + (u + 1) * NS)
                        branch(i * 2 + u, u)
                for u in range(2):
                    sp.wait_ge(br_taken, (KC - 2 + u + 1) * NS)
                    sp.dma_start(wb[:, u, :, :], a["w_out"][u]).then_inc(out_in[u], 16)
                with sp.Fori(1, KC // 2) as i:
                    for u in range(2):
                        sp.wait_ge(mix_done, (i - 1) * (2 * NS) + (u + 1) * NS)
                        sp.dma_start(wb[:, u, :, :], a["w_out"][i * 2 + u]).then_inc(out_in[u], 16)
                sp.wait_ge(mix_taken, KC + 2)
                sp.dma_start(a["x_mid"], x[:, :, :]).then_inc(x_out, 16)
                sp.wait_ge(x_out, 16)

            @block.tensor
            def _(pe):
                group[0].tensor(pe)
                pe.wait_ge(y_ready, 1)
                group[1].tensor(pe)
                pe.wait_ge(y_ready, 2)
                pe.wait_ge(o_in, 16)
                with pe.Fori(0, KC // 2) as i:
                    for u in range(2):
                        pe.wait_ge(br_in[u], (i + 1) * 64)
                        for j, (t0, n) in enumerate(SPLITS):
                            pe.wait_ge(banks_taken, i * (2 * NS) + u * NS + j + 1)
                            for k in range(NA):
                                pe.matmul(ps[:, j, 0:n], wa[:, u, k, :], o[:, k, t0:t0 + n],
                                          start=(k == 0), stop=(k == NA - 1))
                            for k in range(KC):
                                mm = pe.matmul(ps[:, NS + j, 0:n], wb[:, u, k, :], y[:, k, t0:t0 + n],
                                               start=(k == 0), stop=(k == KC - 1))
                            mm.then_inc(br_done, 1)
                pe.wait_ge(br_taken, KC * NS)
                with pe.Fori(0, KC // 2) as i:
                    for u in range(2):
                        pe.wait_ge(out_in[u], (i + 1) * 16)
                        pe.wait_ge(mix_taken, i * 2 + u + 1)
                        for j, (t0, n) in enumerate(SPLITS):
                            for k in range(KC):
                                mm = pe.matmul(ps[:, u * NS + j, 0:n], wb[:, u, k, :], h[:, k, t0:t0 + n],
                                               start=(k == 0), stop=(k == KC - 1))
                            mm.then_inc(mix_done, 1)
                norm.tensor(pe)

            @block.scalar
            def _(act):
                group[0].scalar(act)
                act.wait_ge(y_ready, 1)
                group[1].scalar(act)
                act.wait_ge(mix_taken, KC + 2)
                norm.scalar(act)

            @block.vector
            def _(dve):
                link = Chain(dve, chain)
                dve.sem_inc(banks_taken, NS)
                dve.sem_inc(mix_taken, 2)
                for g in range(NG):
                    group[g].vector(dve)
                    for c in range(g * HALF_C, (g + 1) * HALF_C):
                        ins = dve.scalar_tensor_tensor(y[:, c, :], y[:, c, :],
                                                       s["par"][:, W_SSM + c:W_SSM + c + 1],
                                                       s["rstd"][:, :], ALU.mult, ALU.mult)
                    ins.then_inc(y_ready, 1)
                with dve.Fori(0, KC // 2) as i:
                    for u in range(2):
                        dve.wait_ge(br_in[u], (i + 1) * 64)
                        for j, (t0, n) in enumerate(SPLITS):
                            dve.wait_ge(br_done, i * (2 * NS) + u * NS + j + 1)
                            hm = h[:, bass.ds(i * 2 + u, 1), t0:t0 + n].rearrange("p o t -> p (o t)")
                            dve.tensor_tensor(part[:, j, 0:n], ps[:, j, 0:n],
                                              gates[:, u, 0, t0:t0 + n], ALU.mult)
                            ins = dve.tensor_tensor(hm, ps[:, NS + j, 0:n], gates[:, u, 1, t0:t0 + n], ALU.mult)
                            ins.then_inc(banks_taken, 1)
                            dve.wait_ge(banks_taken, i * (2 * NS) + u * NS + j + 1 + NS)
                            dve.tensor_tensor(hm, hm, part[:, j, 0:n], ALU.add).then_inc(br_taken, 1)
                with dve.Fori(0, KC // 2) as i, link.turns(i, KC // 2, 2):
                    for u in range(2):
                        m = i * 2 + u
                        dve.wait_ge(mix_done, i * (2 * NS) + (u + 1) * NS)
                        gate = s["mod"][:, bass.ds(m + 2 * KC, 1), :].rearrange("p o q -> p (o q)")
                        xm = x[:, bass.ds(m, 1), :].rearrange("p o t -> p (o t)")
                        src = [(t0, ps[:, u * NS + j, 0:min(n, SEQ - t0)]) for j, (t0, n) in enumerate(SPLITS)]
                        t0, n = SPLITS[-1]
                        add_gated(dve, link, xm, gate, src, ps[:, u * NS + NS - 1, SEQ - t0:n],
                                  spare[:, u, :, :]).then_inc(mix_taken, 1)
                norm.vector(dve)
                modulated(dve, link.link, s, x, h, W_N2, 3 * KC, 4 * KC, h_ready)


def route_phase(nc, a, s, sem):
    with ExitStack() as ctx:
        def sb(name, shape, dt=F32):
            return ctx.enter_context(nc.sbuf_tensor(name, shape, dt))

        NT = TILES + 1
        K2 = 2 * EH
        wq = sb("wq", [P, 2, KC, P])
        keys = sb("keys", [P, 2, NK])
        qh = sb("qh", [P, 2, TP])
        sc = sb("sc", [P, 2, NT, NK])
        ps = ctx.enter_context(nc.psum_tensor("query_ps", [P, 2 * NS, 512], F32))
        ps2 = ctx.enter_context(nc.psum_tensor("score_ps", [P, 2, 512], F32))
        keys_in = sem("keys_in")
        wq_in = [sem(f"wq_in{u}") for u in range(2)]
        q_done, q_taken, padded, sc_done, sc_taken = (
            sem("q_done"), sem("q_taken"), sem("padded"), sem("sc_done"), sem("sc_taken"))
        sc_out = [sem(f"sc_out{u}") for u in range(2)]
        sc_free = sem("sc_free")
        h = s["h"]
        fills = [(0, 4), (4, 4), (8, 1)]
        NF = len(fills)

        with nc.Block() as block:
            @block.sync
            def _(sp):
                sp.dma_start(keys[:, :, :], a["keys"]).then_inc(keys_in, 16)
                for u in range(2):
                    sp.dma_start(wq[:, u, :, :], a["w_query"][u]).then_inc(wq_in[u], 16)
                with sp.Fori(1, EH) as i:
                    for u in range(2):
                        sp.wait_ge(q_done, (i - 1) * (2 * NS) + (u + 1) * NS)
                        sp.dma_start(wq[:, u, :, :], a["w_query"][i * 2 + u]).then_inc(wq_in[u], 16)

            @block.tensor
            def _(pe):
                pe.wait_ge(keys_in, 16)
                with pe.Fori(0, EH) as i:
                    for u in range(2):
                        pe.wait_ge(wq_in[u], (i + 1) * 16)
                        for j, (t0, n) in enumerate(SPLITS):
                            pe.wait_ge(q_taken, i * (2 * NS) + u * NS + j + 1)
                            for k in range(KC):
                                mm = pe.matmul(ps[:, u * NS + j, 0:n], wq[:, u, k, :], h[:, k, t0:t0 + n],
                                               start=(k == 0), stop=(k == KC - 1))
                            mm.then_inc(q_done, 1)
                        pe.wait_ge(q_taken, i * (2 * NS) + (u + 1) * NS + 2 * NS)
                        pe.wait_ge(padded, 1)
                        for f, (t0, n) in enumerate(fills):
                            pe.wait_ge(sc_taken, i * (2 * NF) + u * NF + f + 1)
                            for t in range(n):
                                mm = pe.matmul(ps2[:, (u * NF + f) % 2, t * NK:(t + 1) * NK],
                                               qh[:, u, (t0 + t) * P:(t0 + t + 1) * P], keys[:, u, :],
                                               start=True, stop=True)
                            mm.then_inc(sc_done, 1)

            @block.scalar
            def _(act):
                act.sem_inc(q_taken, 2 * NS)
                with act.Fori(0, EH) as i:
                    for u in range(2):
                        for j, (t0, n) in enumerate(SPLITS):
                            act.wait_ge(q_done, i * (2 * NS) + u * NS + j + 1)
                            act.wait_ge(sc_free, i * 2 + u + 1)
                            act.copy(qh[:, u, t0:t0 + n], ps[:, u * NS + j, 0:n]).then_inc(q_taken, 1)
                        act.wait_ge(sc_taken, i * (2 * NF) + (u + 1) * NF + 2)
                        out = a["scores"][:, :, bass.ds(i * 2 + u, 1), :].rearrange("t p o k -> p t (o k)")
                        act.dma_start(out, sc[:, u, :, :]).then_inc(sc_out[u], 16)
                for u in range(2):
                    act.wait_ge(sc_out[u], 16 * (EH + 1))

            @block.vector
            def _(dve):
                dve.sem_inc(sc_taken, 2)
                dve.sem_inc(sc_free, 2)
                for u in range(2):
                    dve.sem_inc(sc_out[u], 16)
                dve.memset(qh[:, :, T:TP], 0.0).then_inc(padded, 1)
                with dve.Fori(0, EH) as i:
                    for u in range(2):
                        dve.wait_ge(sc_out[u], (i + 1) * 16)
                        for f, (t0, n) in enumerate(fills):
                            dve.wait_ge(sc_done, i * (2 * NF) + u * NF + f + 1)
                            dve.tensor_copy(sc[:, u, t0:t0 + n, :],
                                            ps2[:, (u * NF + f) % 2, 0:n * NK].rearrange(
                                                "p (t k) -> p t k", k=NK)).then_inc(sc_taken, 1)
                        dve.sem_inc(sc_free, 1)


    select_phase(nc, a, s, sem)


def select_phase(nc, a, s, sem):
    with ExitStack() as ctx:
        def sb(name, shape, dt=F32):
            return ctx.enter_context(nc.sbuf_tensor(name, shape, dt))

        NT = TILES + 1
        K2 = 2 * EH
        HK = EH * TOPK
        sc = sb("sc_tile", [P, K2, NK])
        rest = sb("sc_rest", [P, K2, NK])
        top = sb("top", [P, K2, TOPK])
        top_i = sb("top_i", [P, K2, TOPK], U32)
        top_f = sb("top_f", [P, K2, TOPK])
        cand = sb("cand", [P, EH, TOPK * TOPK])
        cand2 = sb("cand2", [P, EH, TOPK * TOPK])
        val = sb("val", [P, EH, TOPK])
        flat = sb("flat", [P, EH, TOPK], U32)
        rank = sb("rank", [P, 2, HK], U32)
        rank_f = sb("rank_f", [P, 2, HK])
        hit = sb("hit", [P, 2, HK, TOPK])
        pick = sb("pick", [P, 3, HK])
        total = sb("total", [P, EH])
        ps = ctx.enter_context(nc.psum_tensor("pick_ps", [P, 3, 512], F32))
        tile_in, tile_read, chain, val_ready, val_exp, picked, turned, kept, top_ready, hits = (
            sem("tile_in"), sem("tile_read"), sem("select_chain"), sem("val_ready"), sem("val_exp"),
            sem("picked"), sem("turned"), sem("kept"), sem("top_ready"), sem("hits"))
        passed = sem("select_passed")
        const = s["const"]
        ident = const[:, C_ID:C_ID + P]
        lane = const[:, C_IOTA:C_IOTA + TOPK].unsqueeze(1).to_broadcast([P, HK, TOPK])
        LOW = -3.0e38

        with nc.Block() as block:
            @block.sync
            def _(sp):
                with sp.Fori(0, NT) as t:
                    sp.wait_ge(tile_read, t + 1)
                    sp.dma_start(sc[:, :, :], a["scores"][t]).then_inc(tile_in, 16)

            @block.vector
            def _(dve):
                link = Chain(dve, chain, passed)
                dve.sem_inc(tile_read, 1)
                with dve.Fori(0, NT) as t, link.turns(t, NT, 15):
                    def top16(src, left, vals, idx, n, last=None):
                        for c in range(n):
                            ins = dve.max(vals[:, c, 0:8], src[:, c, :])
                        link.link_apart(ins)
                        for c in range(n):
                            dve.max_index(idx[:, c, 0:8], vals[:, c, 0:8], src[:, c, :])
                            ins = dve.match_replace(left[:, c, :], vals[:, c, 0:8], src[:, c, :], LOW)
                        link.link_apart(ins)
                        if last is not None:
                            last()
                        for c in range(n):
                            ins = dve.max(vals[:, c, 8:16], left[:, c, :])
                        link.link_apart(ins)
                        for c in range(n):
                            ins = dve.max_index(idx[:, c, 8:16], vals[:, c, 8:16], left[:, c, :])
                        link.link(ins)

                    dve.wait_ge(tile_in, (t + 1) * 16)
                    dve.sem_inc(passed, 1)
                    top16(sc, rest, top, top_i, K2, lambda: dve.sem_inc(tile_read, 1))
                    dve.tensor_copy(top_f[:, :, :], top_i[:, :, :])
                    both = top[:, :, :].rearrange("p (h e) k -> p h e k", e=2)
                    link.link_apart(dve.tensor_tensor(
                        cand[:, :, :].rearrange("p h (x y) -> p h x y", y=TOPK),
                        both[:, :, 0, :].unsqueeze(3).to_broadcast([P, EH, TOPK, TOPK]),
                        both[:, :, 1, :].unsqueeze(2).to_broadcast([P, EH, TOPK, TOPK]), ALU.add))
                    top16(cand, cand2, val, flat, EH)
                    g = pick[:, 2, :].rearrange("p (h k) -> p h k", k=TOPK)
                    dve.tensor_tensor(g, val[:, :, :], val[:, :, 0:1].to_broadcast([P, EH, TOPK]),
                                      ALU.subtract).then_inc(val_ready, 1)
                    f = flat[:, :, :].rearrange("p h k -> p (h k)")
                    dve.tensor_scalar(rank[:, 0, :], f, 4, None, ALU.logical_shift_right)
                    link.link(dve.tensor_scalar(rank[:, 1, :], f, 15, None, ALU.bitwise_and))
                    link.link(dve.tensor_copy(rank_f[:, :, :], rank[:, :, :]))
                    for e in range(2):
                        ins = dve.tensor_tensor(hit[:, e, :, :],
                                                rank_f[:, e, :].unsqueeze(2).to_broadcast([P, HK, TOPK]), lane,
                                                ALU.is_equal)
                    link.link(ins)
                    place = top_f[:, :, :].rearrange("p (h e) k -> p h e k", e=2)
                    for e in range(2):
                        x = hit[:, e, :, :].rearrange("p (h k) j -> p h k j", k=TOPK)
                        ins = dve.tensor_tensor(x, x, place[:, :, e, :].unsqueeze(2).to_broadcast(
                            [P, EH, TOPK, TOPK]), ALU.mult)
                    link.link(ins)
                    dve.tensor_reduce(pick[:, 0:2, :], hit[:, :, :, :], AX.X, ALU.add)
                    dve.wait_ge(val_exp, t + 1)
                    link.link(dve.tensor_reduce(total[:, :], g, AX.X, ALU.add))
                    link.link(dve.reciprocal(total[:, :], total[:, :]))
                    dve.tensor_tensor(g, g, total[:, :].unsqueeze(2).to_broadcast([P, EH, TOPK]),
                                      ALU.mult).then_inc(picked, 1)
                    dve.wait_ge(turned, t + 1)

            @block.scalar
            def _(act):
                g = pick[:, 2, :]
                with act.Fori(0, NT) as t:
                    act.wait_ge(val_ready, t + 1)
                    act.activation(g, g, ACT.Exp).then_inc(val_exp, 1)
                    act.wait_ge(turned, t + 1)
                    act.copy(s["choice"][:, :, bass.ds(t * P, P)], ps[:, :, 0:P]).then_inc(kept, 1)

            @block.tensor
            def _(pe):
                pe.sem_inc(kept, 1)
                with pe.Fori(0, NT) as t:
                    pe.wait_ge(picked, t + 1)
                    pe.wait_ge(kept, t + 1)
                    for e in range(3):
                        mm = pe.transpose(ps[:, e, 0:P], pick[:, e, :], ident)
                    mm.then_inc(turned, 1)


def weights_phase(nc, a, s, sem):
    NQ = 4
    PER = 2 * TB
    NG4 = PER // NQ
    with ExitStack() as ctx:
        def sb(name, shape):
            return ctx.enter_context(nc.sbuf_tensor(name, shape, F32))

        left = sb("left", [P, 4, NQ, NK])
        right = sb("right", [P, 4, NQ, NK])
        e1 = sb("e1", [P, PER])
        mine = sb("choice_v", [P, 3, PER])
        out = sb("w_stage", [P, 2, NK, TB])
        ps = ctx.enter_context(nc.psum_tensor("w_ps", [P, 8, 512], F32))
        pool_chain, dve_chain = sem("w_pool_chain"), sem("w_dve_chain")
        left_ready, right_ready, w_done, w_taken = (
            sem("left_ready"), sem("right_ready"), sem("w_done"), sem("w_taken"))
        w_out = [sem(f"w_out{u}") for u in range(2)]
        w_passed = sem("w_passed")

        def share(g):
            return 2 if g % 2 == 0 else 1

        iota = s["const"][:, C_IOTA:C_IOTA + NK]

        with nc.Block() as block:
            @block.gpsimd
            def _(pool):
                link = Chain(pool, pool_chain)
                with pool.Fori(0, T // PER) as i, link.turns(i, T // PER, 1):
                    link.link(pool.tensor_copy(e1[:, :], s["choice"][:, 0, bass.ds(i * PER, PER)]))
                    for g in range(NG4):
                        pool.wait_ge(w_done, i * NG4 + g + 1)
                        pool.sem_inc(w_passed, 1)
                        for n in range(share(g)):
                            t = g * NQ + n
                            ins = pool.tensor_scalar(left[:, g % 4, n, :], iota, e1[:, t:t + 1], None,
                                                     ALU.is_equal)
                        ins.then_inc(left_ready, 1)
                    pool.wait_ge(left_ready, (i + 1) * NG4)

            @block.vector
            def _(dve):
                link = Chain(dve, dve_chain)
                with dve.Fori(0, T // PER) as i, link.turns(i, T // PER, 1):
                    link.link(dve.tensor_copy(mine[:, :, :], s["choice"][:, :, bass.ds(i * PER, PER)]))
                    for g in range(NG4):
                        dve.wait_ge(w_done, i * NG4 + g + 1)
                        for n in range(share(g), NQ):
                            t = g * NQ + n
                            dve.tensor_scalar(left[:, g % 4, n, :], iota, mine[:, 0, t:t + 1], None,
                                              ALU.is_equal)
                        for n in range(NQ):
                            t = g * NQ + n
                            ins = dve.tensor_scalar(right[:, g % 4, n, :], iota, mine[:, 1, t:t + 1],
                                                    mine[:, 2, t:t + 1], ALU.is_equal, ALU.mult)
                        ins.then_inc(right_ready, 1)
                    dve.wait_ge(right_ready, (i + 1) * NG4)

            @block.tensor
            def _(pe):
                pe.sem_inc(w_done, 4)
                with pe.Fori(0, T // PER) as i:
                    for g in range(NG4):
                        pe.wait_ge(left_ready, i * NG4 + g + 1)
                        pe.wait_ge(right_ready, i * NG4 + g + 1)
                        pe.wait_ge(w_taken, i * NG4 + g + 1)
                        for n in range(NQ):
                            mm = pe.matmul(ps[:, g % 8, n * NK:(n + 1) * NK], left[:, g % 4, n, :],
                                           right[:, g % 4, n, :], start=True, stop=True)
                        mm.then_inc(w_done, 1)

            @block.scalar
            def _(act):
                act.sem_inc(w_taken, 8)
                for u in range(2):
                    act.sem_inc(w_out[u], 16)
                with act.Fori(0, T // PER) as i:
                    for g in range(NG4):
                        b = g * NQ // TB
                        if g * NQ % TB == 0:
                            act.wait_ge(w_out[b], (i + 1) * 16)
                        act.wait_ge(w_done, i * NG4 + g + 1 + 4)
                        t = g * NQ % TB
                        act.copy(out[:, b, :, t:t + NQ].rearrange("p e t -> p t e"),
                                 ps[:, g % 8, :].rearrange("p (t e) -> p t e", e=NK)).then_inc(w_taken, 1)

            @block.sync
            def _(sp):
                with sp.Fori(0, T // PER) as i:
                    for b in range(2):
                        sp.wait_ge(w_taken, i * NG4 + (b + 1) * (NG4 // 2) + 8)
                        sp.dma_start(a["w"][i * 2 + b], out[:, b, :, :]).then_inc(w_out[b], 16)
                for b in range(2):
                    sp.wait_ge(w_out[b], 16 * (T // PER + 1))


F16 = mybir.dt.float16


class Scales:
    ROWS, N = 32, 3

    def __init__(self, nc, sb, sem, s, psum):
        self.s, self.ps = s, psum
        self.tops = sb("tops", [P, self.ROWS])
        self.top = sb("top_all", [self.ROWS, 1])
        self.exp = sb("exponent", [self.ROWS, 1], I32)
        self.pow = sb("powers", [self.ROWS, 2, 1], I32)
        self.diag = sb("powers_diag", [self.ROWS, 2, self.N])
        self.value = sb("scales", [P, 2 * self.N])
        self.found, self.turned, self.powered, self.spread, self.ready = (
            sem("tops_found"), sem("tops_turned"), sem("powered"), sem("scales_spread"), sem("scales_ready"))

    def turn(self, pe, c):
        pe.wait_ge(self.found, c + 1)
        pe.transpose(self.ps[0:self.ROWS, 0:P], self.tops[:, :],
                     self.s["const"][:, C_ID:C_ID + P]).then_inc(self.turned, 1)

    def spread_out(self, pe, c):
        pe.wait_ge(self.powered, c + 1)
        pe.matmul(self.ps[:, P:P + 2 * self.N], self.s["const"][0:self.ROWS, C_ONE:C_ONE + P],
                  self.diag[:, :, :], start=True, stop=True).then_inc(self.spread, 1)

    def powers(self, dve, link, c):
        dve.wait_ge(self.turned, c + 1)
        link(dve.tensor_reduce(self.top[:, :], self.ps[0:self.ROWS, 0:P], AX.X, ALU.max))
        link(dve.tensor_scalar(self.exp[:, :], self.top[:, :].bitcast(I32), 23, None, ALU.logical_shift_right))
        link(dve.tensor_scalar(self.exp[:, :], self.exp[:, :], 15, 254, ALU.max, ALU.min))
        dve.tensor_scalar(self.pow[:, 0, :], self.exp[:, :], -1, 268, ALU.mult, ALU.add)
        link(dve.tensor_scalar(self.pow[:, 1, :], self.exp[:, :], -14, None, ALU.add))
        link(dve.tensor_scalar(self.pow[:, :, :], self.pow[:, :, :], 23, None, ALU.logical_shift_left))
        ident = self.s["const"][0:self.ROWS, C_ID:C_ID + self.N].unsqueeze(1)
        dve.tensor_tensor(self.diag[:, :, :], ident.to_broadcast([self.ROWS, 2, self.N]),
                          self.pow[:, :, :].bitcast(F32).to_broadcast([self.ROWS, 2, self.N]),
                          ALU.mult).then_inc(self.powered, 1)
    POWERS_LINKS = 5

    def take(self, dve, link, c):
        dve.wait_ge(self.spread, c + 1)
        link(dve.tensor_copy(self.value[:, :], self.ps[:, P:P + 2 * self.N]))


def experts_phase(nc, a, s, sem):
    NB = 3
    with ExitStack() as ctx:
        def sb(name, shape, dt=F32):
            return ctx.enter_context(nc.sbuf_tensor(name, shape, dt))

        u = sb("u_chunks", [P, GRP, KC, P])
        v = sb("v_group", [P, GRP, D])
        w = sb("w_groups", [P, 2, NTB, GRP, TB])
        h16 = sb("h_parts", [P, 2, KC, T], F16)
        u16 = sb("u_parts", [P, 2, GRP, KC, P], F16)
        v16 = sb("v_parts", [P, 2, GRP, D], F16)
        a16 = sb("act_parts", [P, 2, GRP, T], F16)
        act_sb = sb("gelu", [P, NB, 384])
        act_top = sb("act_top", [P, GRP])
        dot_unit = sb("dot_unit", [P, 2])
        h_unit = sb("h_unit", [P, 1])
        sum_unit = sb("sum_unit", [P, 1])
        ps = ctx.enter_context(nc.psum_tensor("expert_ps", [P, 2, NS, 512], F32))
        scale_ps = ctx.enter_context(nc.psum_tensor("scale_ps", [P, 512], F32))
        u_in = [sem(f"u_in{j}") for j in range(GRP)]
        v_in = sem("v_in")
        w_in = [sem(f"wt_in{p}") for p in range(2)]
        dot_done, gelu_done, act_done, sum_done, sum_taken = (
            sem("dot_done"), sem("gelu_done"), sem("act_done"), sem("sum_done"), sem("sum_taken"))
        h_hi, u_hi, v_hi, a_hi = sem("h_hi"), sem("u_hi"), sem("v_hi"), sem("a_hi")
        h_split, u_split, v_split, a_split = sem("h_split"), sem("u_split"), sem("v_split"), sem("a_split")
        chain = sem("experts_chain")
        scales = Scales(nc, sb, sem, s, scale_ps)
        S_ACT, S_V, S_U = 0, 1, 2
        h, acc = s["h"], s["acc"]
        PER_A = GRP * NS
        PER_B = KC * NS
        LAST = NGRP - 1
        LOOPS = (NGRP - 4) // 2

        def tokens(slot, j, t0, n):
            return w[:, slot, t0 // TB:(t0 + n) // TB, j, :]

        def flat(x):
            return x.rearrange("p (b t) -> p b t", t=TB)

        def rounds(eng, body):
            with eng.Fori(0, LOOPS) as i:
                for p in range(2):
                    body(i * 2 + p, i, p, 0)
            for g in range(2 * LOOPS, NGRP):
                body(g, g // 2, g % 2, g)

        with nc.Block() as block:
            @block.sync
            def _(sp):
                def load_u(g, j):
                    sp.dma_start(u[:, j, :, :], a["u"][g * GRP + j]).then_inc(u_in[j], 16)

                def load_w(g, p):
                    cols = slice(g * GRP, (g + 1) * GRP) if isinstance(g, int) else bass.ds(g * GRP, GRP)
                    sp.dma_start(w[:, p, :, :, :],
                                 a["w"][:, :, cols, :].rearrange("b p e t -> p b (e t)")).then_inc(w_in[p], 16)

                for j in range(GRP):
                    load_u(0, j)
                load_w(0, 0)
                sp.dma_start(v[:, :, :], a["v"][0]).then_inc(v_in, 16)
                load_w(1, 1)
                for g in (1, 2):
                    for j in range(GRP):
                        sp.wait_ge(u_split, (g - 1) * GRP + j + 1)
                        load_u(g, j)

                def turn(g, i, p, at):
                    if at < LAST:
                        sp.wait_ge(v_split, (g + 1) * GRP)
                        sp.dma_start(v[:, :, :], a["v"][g + 1]).then_inc(v_in, 16)
                    if at < LAST - 1:
                        sp.wait_ge(a_split, (g + 1) * GRP)
                        load_w(g + 2, p)
                    if at < LAST - 2:
                        for j in range(GRP):
                            sp.wait_ge(u_split, (g + 2) * GRP + j + 1)
                            load_u(g + 3, j)

                rounds(sp, turn)

            @block.tensor
            def _(pe):
                def product(bank, left, right, first, last):
                    for x, parts in ((0, (0, 1)), (1, (0,))):
                        for q, (t0, n) in enumerate(SPLITS):
                            if first is not None and x == 0:
                                first(q)
                            for y in parts:
                                mm = pe.matmul(bank(q), left(x), right(y, t0, n),
                                               start=first is not None and x == 0 and y == 0,
                                               stop=last is not None and x == 1)
                            if last is not None and x == 1:
                                mm.then_inc(last, 1)

                def dot(g, c=None, at=0):
                    for j in range(GRP):
                        pe.wait_ge(u_split, g * GRP + j + 1)

                        def free(q):
                            if j >= 2:
                                pe.wait_ge(gelu_done, g * PER_A + (j - 2) * NS + q + 1)
                            elif at == 1:
                                pe.wait_ge(gelu_done, (g - 1) * PER_A + (j + 2) * NS + q + 1)
                            elif at != 0:
                                pe.wait_ge(sum_taken, (g - 2) * PER_B + (KC - 2 + j) * NS + q + 1)

                        for k in range(KC):
                            product(lambda q: ps[:, j % 2, q, 0:SPLITS[q][1]],
                                    lambda x: u16[:, x, j, k, :],
                                    lambda y, t0, n: h16[:, y, k, t0:t0 + n],
                                    free if k == 0 else None, dot_done if k == KC - 1 else None)
                        if j == 0 and c is not None:
                            scales.turn(pe, c)
                        if j == 1 and c is not None:
                            scales.spread_out(pe, c)

                def total(g, at=0):
                    pe.wait_ge(v_split, (g + 1) * GRP)
                    pe.wait_ge(a_split, (g + 1) * GRP)
                    for m in range(KC):
                        def free(q):
                            if m >= 2:
                                pe.wait_ge(sum_taken, g * PER_B + (m - 2) * NS + q + 1)
                            elif at < LAST:
                                pe.wait_ge(gelu_done, (g + 1) * PER_A + (2 + m) * NS + q + 1)
                            else:
                                pe.wait_ge(sum_taken, (g - 1) * PER_B + (KC - 2 + m) * NS + q + 1)

                        for j in range(GRP):
                            product(lambda q: ps[:, m % 2, q, 0:SPLITS[q][1]],
                                    lambda x: v16[:, x, j, m * P:(m + 1) * P],
                                    lambda y, t0, n: a16[:, y, j, t0:t0 + n],
                                    free if j == 0 else None, sum_done if j == GRP - 1 else None)

                scales.turn(pe, 0)
                scales.spread_out(pe, 0)
                pe.wait_ge(h_split, KC)
                dot(0, 1)
                dot(1, 2, 1)
                total(0)
                dot(2, 3, 2)
                total(1)
                with pe.Fori(1, LOOPS + 1) as i:
                    for p in range(2):
                        dot(i * 2 + (p + 1), i * 2 + (p + 2), 2)
                        total(i * 2 + p)
                dot(LAST, LAST + 1, 2)
                total(LAST - 1)
                scales.turn(pe, LAST + 2)
                scales.spread_out(pe, LAST + 2)
                total(LAST, LAST)

            @block.scalar
            def _(act):
                def scaled(out, src, n, done):
                    act.activation(out, src, ACT.Copy, scale=scales.value[:, n:n + 1]).then_inc(done, 1)

                def gelu(g, p, chunks):
                    for j in chunks:
                        for q, (t0, n) in enumerate(SPLITS):
                            act.wait_ge(dot_done, g * PER_A + j * NS + q + 1)
                            act.wait_ge(act_done, g * PER_A + j * NS + q + 1)
                            act.activation(act_sb[:, q, 0:n], ps[:, j % 2, q, 0:n], ACT.Gelu_apprx_tanh,
                                           scale=dot_unit[:, p:p + 1]).then_inc(gelu_done, 1)

                def split_u(g):
                    act.wait_ge(dot_done, g * PER_A)
                    for j in range(GRP):
                        scaled(u16[:, 0, j, :, :], u[:, j, :, :], S_U, u_hi)

                def turn(g, i, p, at):
                    if at < LAST:
                        gelu(g + 1, 1 - p, (0, 1))
                    act.wait_ge(scales.ready, g + 3)
                    if not isinstance(g, int) or g > 0:
                        act.wait_ge(sum_done, g * PER_B)
                    for j in range(GRP):
                        scaled(flat(a16[:, 0, j, :]), w[:, p, :, j, :], S_ACT, a_hi)
                    for j in range(GRP):
                        scaled(v16[:, 0, j, :], v[:, j, :], S_V, v_hi)
                    if at < LAST:
                        gelu(g + 1, 1 - p, (2, 3))
                    if at < LAST - 1:
                        split_u(g + 2)

                act.wait_ge(scales.ready, 1)
                for k in range(KC):
                    scaled(h16[:, 0, k, :], h[:, k, :], S_ACT, h_hi)
                for j in range(GRP):
                    scaled(u16[:, 0, j, :, :], u[:, j, :, :], S_U, u_hi)
                gelu(0, 0, (0, 1, 2, 3))
                act.wait_ge(scales.ready, 2)
                split_u(1)
                turn(0, 0, 0, 0)
                turn(1, 0, 1, 0)
                with act.Fori(1, LOOPS) as i:
                    for p in range(2):
                        turn(i * 2 + p, i, p, 0)
                for g in range(2 * LOOPS, NGRP):
                    turn(g, g // 2, g % 2, g)

            @block.vector
            def _(dve):
                link = Chain(dve, chain)
                tops = scales.tops

                def largest(out, src, axis=AX.X):
                    link.mark(dve.tensor_reduce(out, src, axis, ALU.max, apply_absolute_value=True))

                def rest(out, src, n, hi, done):
                    dve.scalar_tensor_tensor(out, src, scales.value[:, n:n + 1], hi, ALU.mult,
                                             ALU.subtract).then_inc(done, 1)

                def weigh(g, i, p, j):
                    if j == 0:
                        dve.wait_ge(w_in[p], (i + 1) * 16)
                    for q, (t0, n) in enumerate(SPLITS):
                        dve.wait_ge(gelu_done, g * PER_A + j * NS + q + 1)
                        x = tokens(p, j, t0, n)
                        dve.tensor_tensor(x, x, flat(act_sb[:, q, 0:n]), ALU.mult).then_inc(act_done, 1)
                    dve.wait_ge(act_done, g * PER_A + (j + 1) * NS + NB)
                    largest(act_top[:, j:j + 1], w[:, p, :, j, :], AX.XY)

                def split_u(g):
                    for j in range(GRP):
                        dve.wait_ge(u_hi, g * GRP + j + 1)
                        rest(u16[:, 1, j, :, :], u[:, j, :, :], S_U, u16[:, 0, j, :, :], u_split)

                def top_u(g):
                    for j in range(GRP):
                        dve.wait_ge(u_in[j], (g + 1) * 16)
                    largest(tops[:, S_U:S_U + 1], u[:, :, :, :].rearrange("p j k e -> p (j k e)"))

                def top_v(g):
                    dve.wait_ge(v_in, (g + 1) * 16)
                    largest(tops[:, S_V:S_V + 1], v[:, :, :].rearrange("p j d -> p (j d)"))

                def found(g=None):
                    if g is not None:
                        link.wait(link.base + link.n)
                        link.mark(dve.tensor_reduce(tops[:, S_ACT:S_ACT + 1], act_top[:, :], AX.X, ALU.max))
                    link.wait(link.base + link.n)
                    dve.sem_inc(scales.found, 1)

                def take(c, p):
                    scales.take(dve, link.link, c)
                    v_ = scales.value
                    link.mark(dve.tensor_tensor(dot_unit[:, p:p + 1], v_[:, 3 + S_U:4 + S_U], h_unit[:, :],
                                                ALU.mult))
                    link.link(dve.tensor_tensor(sum_unit[:, :], v_[:, 3 + S_ACT:4 + S_ACT],
                                                v_[:, 3 + S_V:4 + S_V], ALU.mult))
                    dve.sem_inc(scales.ready, 1)

                def add(g, chunks):
                    for m in chunks:
                        for q, (t0, n) in enumerate(SPLITS):
                            dve.wait_ge(sum_done, g * PER_B + m * NS + q + 1)
                            x = acc[:, m, t0:t0 + n]
                            dve.scalar_tensor_tensor(x, ps[:, m % 2, q, 0:n], sum_unit[:, :], x, ALU.mult,
                                                     ALU.add).then_inc(sum_taken, 1)

                def turn(g, i, p, at):
                    found(g)
                    scales.powers(dve, link.link, g + 2)
                    if at < LAST:
                        weigh(g + 1, i + p, 1 - p, 0)
                    take(g + 2, p)
                    for j in range(GRP):
                        dve.wait_ge(a_hi, g * GRP + j + 1)
                        rest(flat(a16[:, 1, j, :]), w[:, p, :, j, :], S_ACT, flat(a16[:, 0, j, :]), a_split)
                    for j in range(GRP):
                        dve.wait_ge(v_hi, g * GRP + j + 1)
                        rest(v16[:, 1, j, :], v[:, j, :], S_V, v16[:, 0, j, :], v_split)
                    if at < LAST:
                        for j in (1, 2, 3):
                            weigh(g + 1, i + p, 1 - p, j)
                    add(g, (0,))
                    if at < LAST - 1:
                        split_u(g + 2)
                    add(g, (1, 2, 3, 4, 5, 6))
                    if at < LAST:
                        top_v(g + 1)
                    if at < LAST - 2:
                        top_u(g + 3)
                    add(g, (7,))

                dve.sem_inc(act_done, NB)
                link.link(dve.memset(tops[:, :], 1.0))
                largest(tops[:, S_ACT:S_ACT + 1], h[:, :, :].rearrange("p k t -> p (k t)"))
                top_u(0)
                found()
                scales.powers(dve, link.link, 0)
                scales.take(dve, link.link, 0)
                link.mark(dve.tensor_copy(h_unit[:, :], scales.value[:, 3 + S_ACT:4 + S_ACT]))
                link.wait(link.base + link.n)
                link.link(dve.tensor_tensor(dot_unit[:, 0:1], scales.value[:, 3 + S_U:4 + S_U], h_unit[:, :],
                                            ALU.mult))
                dve.sem_inc(scales.ready, 1)
                for k in range(KC):
                    dve.wait_ge(h_hi, k + 1)
                    rest(h16[:, 1, k, :], h[:, k, :], S_ACT, h16[:, 0, k, :], h_split)
                split_u(0)
                dve.wait_ge(h_split, KC)
                link.link(dve.memset(acc[:, :, :], 0.0))
                top_u(1)
                found()
                scales.powers(dve, link.link, 1)
                weigh(0, 0, 0, 0)
                take(1, 1)
                for j in (1, 2, 3):
                    weigh(0, 0, 0, j)
                split_u(1)
                top_v(0)
                top_u(2)
                per = 1 + Scales.POWERS_LINKS + GRP + 3 + 2
                with dve.Fori(0, LOOPS) as i, link.turns(i, LOOPS, 2 * per):
                    for p in range(2):
                        turn(i * 2 + p, i, p, 0)
                for g in range(2 * LOOPS, NGRP):
                    turn(g, g // 2, g % 2, g)


def final_phase(nc, a, s, sem):
    with ExitStack() as ctx:
        x = ctx.enter_context(nc.sbuf_tensor("x_end", [P, KC, T], F32))
        squares = ctx.enter_context(nc.sbuf_tensor("squares_end", [P, KC, T], F32))
        spare = ctx.enter_context(nc.sbuf_tensor("spare_end", [P, 2, NSEQ, LS], F32))
        ps = ctx.enter_context(nc.psum_tensor("end_ps", [P, NS, 512], F32))
        x_in, x_ready, y_ready, y_out, chain = (
            sem("x_in2"), sem("x_ready"), sem("y_final"), sem("y_out"), sem("final_chain"))
        norm = Norm(nc, sem, "norm_f", x, squares, s, ps)

        with nc.Block() as block:
            @block.sync
            def _(sp):
                for k in range(KC):
                    sp.dma_start(x[:, k, :], a["x_mid"][:, k, :]).then_inc(x_in, 16)
                for k in range(KC):
                    sp.wait_ge(y_ready, k + 1)
                    sp.dma_start(a["y_out"][:, k, :], x[:, k, :]).then_inc(y_out, 16)
                sp.wait_ge(y_out, 16 * KC)

            @block.scalar
            def _(act):
                act.wait_ge(x_ready, KC)
                norm.scalar(act)

            @block.tensor
            def _(pe):
                norm.tensor(pe)

            @block.vector
            def _(dve):
                link = Chain(dve, chain)
                dve.wait_ge(x_in, 16 * KC)
                for k in range(KC):
                    add_gated(dve, link, x[:, k, :], s["mod"][:, 5 * KC + k, :], [(0, s["acc"][:, k, 0:SEQ])],
                              s["acc"][:, k, SEQ:T], spare[:, k % 2, :, :]).then_inc(x_ready, 1)
                norm.vector(dve)
                for k in range(KC):
                    dve.scalar_tensor_tensor(x[:, k, :], x[:, k, :], s["par"][:, W_NF + k:W_NF + k + 1],
                                             s["rstd"][:, :], ALU.mult, ALU.mult).then_inc(y_ready, 1)


OUTS = {
    "y_out": (P, KC, T), "k_out": (4, P, T), "v_out": (T, AW), "conv_out": (P, 12, 1 + NSEQ, CW - 1),
    "ssm_out": (1 + NSEQ, NST, D),
}


def chunked(w):
    k, m = w.shape
    return w.reshape(k // P, P, m // P, P).transpose(2, 1, 0, 3)


def channels(v):
    return v.reshape(-1, P).T


def wide(v):
    return np.broadcast_to(v[None, :], (P, v.size))


def laid_out(i):
    x = np.concatenate([i["x_prompt"][0], i["x_sample"].reshape(TS, D)])
    c = np.concatenate([i["c_prompt"], i["c_sample"]])
    w = i["w_in"][0]
    ends = np.cumsum([0, AW, AW, AW, D, CONV, SH, D, D])
    q, k, v, z, xbc, dt, ga, gs = (w[:, ends[n]:ends[n + 1]] for n in range(8))
    par = np.concatenate([
        channels(i["norm1_w"][0]), channels(i["norm2_w"][0]), channels(i["norm_f_w"]),
        channels(i["ssm_norm_w"][0]), channels(np.repeat(i["d_skip"][0], SP_)), channels(i["b_ada"][0]),
        wide(i["sb_bias"][0]), channels(i["conv_b"][0]),
        i["conv_w"][0].reshape(CW, 12, P).transpose(2, 1, 0).reshape(P, 12 * CW),
        wide(i["dt_bias"][0]), wide(i["a_log"][0]),
    ], axis=1)
    return {
        "const": constants(),
        "par": par,
        "x": x.T.reshape(KC, P, T).transpose(1, 0, 2),
        "cond": c.T.reshape(KC, P, 1 + NSEQ).transpose(1, 0, 2),
        "w_ada": chunked(i["w_ada"][0]),
        "w_in": chunked(np.concatenate([q, k, z, xbc, ga, gs], axis=1)),
        "w_v": v.reshape(KC, P, AW).transpose(1, 0, 2),
        "w_dt": dt.reshape(KC, P, SH).transpose(1, 0, 2),
        "state_conv": i["state_conv"][0].reshape(NSEQ, CW - 1, 12, P).transpose(3, 2, 0, 1),
        "state_ssm": i["state_ssm"][0].reshape(NSEQ, D, NST).transpose(0, 2, 1),
        "pages": i["page_table"].reshape(1, NSEQ * NPAGE),
        "cache_k": i["cache_k"][0].reshape(POOL, PAGE, 4, P).transpose(0, 3, 2, 1),
        "cache_v": i["cache_v"][0].reshape(POOL, PAGE, AW),
        "w_attn": chunked(i["w_br_attn"][0]),
        "w_ssm": chunked(i["w_br_ssm"][0]),
        "w_out": chunked(i["w_out"][0]),
        "w_query": chunked(i["peer_w_query"][0]),
        "keys": np.stack([i["peer_keys1"][0].T, i["peer_keys2"][0].T], axis=1),
        "u": i["peer_u"][0].reshape(NK, NK, KC, P).transpose(1, 3, 2, 0),
        "v": i["peer_v"][0].reshape(NK, NGRP, GRP, D).transpose(1, 0, 2, 3),
    }


SCRATCH = {"proj": (NCH, P, T), "o": (AW, T), "x_mid": (P, KC, T), "w": (NTB, P, NK, TB),
           "scores": (TILES + 1, P, 2 * EH, NK)}


def kernel(**inputs):
    import concourse.bacc as bacc
    from concourse.bass_utils import run_bass_kernel_spmd

    nc = bacc.Bacc("TRN2", target_bir_lowering=False, num_devices=1)
    arrays, a = {}, {}
    for name, v in laid_out({k: np.asarray(v) for k, v in inputs.items()}).items():
        arrays[f"in_{name}"] = np.ascontiguousarray(v)
        a[name] = nc.dram_tensor(f"in_{name}", v.shape, mybir.dt.from_np(v.dtype), kind="ExternalInput").ap()
    for name, shape in OUTS.items():
        a[name] = nc.dram_tensor(name, shape, F32, kind="ExternalOutput").ap()
    for name, shape in SCRATCH.items():
        a[name] = nc.dram_tensor(f"tmp_{name}", shape, F32, kind="Internal").ap()
    build(nc, a)
    r = run_bass_kernel_spmd(nc, [arrays], core_ids=[0]).results[0]

    y = r["y_out"].transpose(2, 1, 0).reshape(T, D)
    k = r["k_out"].reshape(AW, T).T
    v = r["v_out"]
    conv = r["conv_out"].transpose(2, 3, 1, 0).reshape(1 + NSEQ, CW - 1, CONV)
    ssm = r["ssm_out"].transpose(0, 2, 1).reshape(1 + NSEQ, SH, SP_, NST)
    return (
        y[None, :SEQ], y[SEQ:].reshape(NSEQ, LS, D),
        k[:SEQ].reshape(1, 1, SEQ, HEADS, HD), v[:SEQ].reshape(1, 1, SEQ, HEADS, HD),
        conv[None, :1], ssm[None, :1],
        k[SEQ:].reshape(1, NSEQ, LS, HEADS, HD), v[SEQ:].reshape(1, NSEQ, LS, HEADS, HD),
        conv[None, 1:], ssm[None, 1:],
    )
```

```python
from contextlib import ExitStack, contextmanager

import numpy as np

import concourse.bass as bass
from concourse import mybir

ALU = mybir.AluOpType
ACT = mybir.ActivationFunctionType
AX = mybir.AxisListType
F32 = mybir.dt.float32
F16 = mybir.dt.float16
I32 = mybir.dt.int32
U32 = mybir.dt.uint32

P = 128
D = 1024
KC = D // P
SEQ = 1024
NSEQ = 8
LS = 8
TS = NSEQ * LS
T = SEQ + TS
SPLITS = ((0, 384), (384, 384), (768, 320))
NS = len(SPLITS)
HEADS, HD = 8, 64
AW = HEADS * HD
SH, SP_ = 16, 64
NG, NST = 2, 128
CW = 4
CONV = D + 2 * NG * NST
PAGE = 128
NPAGE = 8
POOL = 80
EPS = 1e-6
CLAMP = 30.0
TILES = SEQ // P
TP = (TILES + 1) * P
EH, TOPK, NK = 8, 16, 128
GRP = 4
NGRP = NK // GRP
TB = 32
NTB = T // TB

CH_Q, CH_K, CH_Z, CH_X, CH_G = 0, 4, 8, 16, 28
NCH = 44
RING = 4
MOD_FIRST = 2 * KC

C_ONE, C_NEG, C_NTRI, C_TRI, C_STRICT, C_ID, C_IOTA, C_BTRI, C_BSTRICT, C_SEQ = (
    0, 128, 256, 384, 512, 640, 768, 896, 960, 1024)
NCONST = 1032

W_N1, W_N2, W_NF, W_SSM, W_DSKIP, W_BADA, W_SB, W_CB, W_CW, W_DTB, W_AL = (
    0, 8, 16, 24, 32, 40, 88, 96, 108, 156, 172)
NPAR = 188


class Chain:

    def __init__(self, eng, sem, passed=None):
        self.eng, self.sem, self.passed, self.base, self.n = eng, sem, passed, 0, 0

    def mark(self, ins):
        self.n += 1
        ins.then_inc(self.sem, 1)
        return self.base + self.n

    def wait(self, count):
        self.eng.wait_ge(self.sem, count)

    def link(self, ins):
        self.wait(self.mark(ins))

    def link_apart(self, ins):
        self.link(ins)
        self.eng.sem_inc(self.passed, 1)

    @contextmanager
    def turns(self, i, count, per):
        start = self.base + self.n
        self.base, self.n = i * per + start, 0
        yield
        assert self.n == per, (self.n, per)
        self.base, self.n = start + count * per, 0


def constants():
    c = np.zeros((P, NCONST), np.float32)
    r, q = np.arange(P)[:, None], np.arange(P)[None, :]
    c[:, C_ONE:C_ONE + P] = 1
    c[:, C_NEG:C_NEG + P] = -1
    c[:, C_NTRI:C_NTRI + P] = np.where(r >= q, -1, 0)
    c[:, C_TRI:C_TRI + P] = r <= q
    c[:, C_STRICT:C_STRICT + P] = r < q
    c[:, C_ID:C_ID + P] = r == q
    c[:, C_IOTA:C_IOTA + P] = q
    r, q = np.arange(TS)[:, None], np.arange(TS)[None, :]
    same = r // LS == q // LS
    c[:TS, C_BTRI:C_BTRI + TS] = same & (r <= q)
    c[:TS, C_BSTRICT:C_BSTRICT + TS] = same & (r < q)
    c[:TS, C_SEQ:C_SEQ + NSEQ] = r // LS == np.arange(NSEQ)[None, :]
    return c


def build(nc, a):
    with ExitStack() as top:
        taken = []

        def sem(name):
            taken.append(nc.alloc_semaphore(name=name))
            return taken[-1]

        def keep(name, shape, dt=F32):
            return top.enter_context(nc.sbuf_tensor(name, shape, dt))

        s = dict(
            const=keep("const", [P, NCONST]),
            par=keep("par", [P, NPAR]),
            mod=keep("mod", [P, 48, 1 + NSEQ]),
            h_top=keep("h_top", [P, 1]),
            cond_act=keep("cond_act", [P, KC, 1 + NSEQ]),
            h=keep("h", [P, KC, T]),
            rstd=keep("rstd", [P, T]),
            gain=keep("gain", [P, KC, 1 + NSEQ]),
        )
        with nc.sbuf_tensor("x", [P, KC, T], F32) as s["x"], \
                nc.sbuf_tensor("dt_tok", [P, TILES + 1, SH], F32) as s["dt_tok"]:
            with nc.sbuf_tensor("squares", [P, KC, T], F32) as s["y"]:
                ada_phase(nc, a, s, sem)
            with nc.sbuf_tensor("v_tok", [P, TILES + 1, AW], F32) as s["v_tok"]:
                project_phase(nc, a, s, sem)
                attend_phase(nc, a, s, sem)
                attend_sample_phase(nc, a, s, sem)
            with nc.sbuf_tensor("y", [P, KC, T], F32) as s["y"]:
                ssd_phase(nc, a, s, sem)
                merge_phase(nc, a, s, sem)
        nc.clear_and_free_semaphores(taken)
        nc.all_engine_barrier()
        with nc.sbuf_tensor("choice", [P, 3, TP], F32) as s["choice"]:
            route_phase(nc, a, s, sem)
            weights_phase(nc, a, s, sem)
        s["acc"] = s["h"]
        experts_phase(nc, a, s, sem)
        final_phase(nc, a, s, sem)


class Norm:

    def __init__(self, nc, sem, name, src, squares, s, psum, chunks=KC):
        self.nc, self.src, self.sq, self.s, self.psum, self.chunks = nc, src, squares, s, psum, chunks
        self.squared = sem(name + "_squared")
        self.summed = sem(name + "_summed")
        self.meaned = sem(name + "_meaned")
        self.rooted = sem(name + "_rooted")
        self.scaled = sem(name + "_scaled")

    def scalar(self, act):
        for k in range(self.chunks):
            act.activation(self.sq[:, k, :], self.src[:, k, :], ACT.Square).then_inc(self.squared, 1)
        for i, (t0, n) in enumerate(SPLITS):
            act.wait_ge(self.meaned, i + 1)
            r = self.s["rstd"][:, t0:t0 + n]
            act.activation(r, r, ACT.Sqrt).then_inc(self.rooted, 1)

    def tensor(self, pe):
        ones = self.s["const"][:, C_ONE:C_ONE + P]
        for k in range(self.chunks):
            pe.wait_ge(self.squared, k + 1)
            for i, (t0, n) in enumerate(SPLITS):
                mm = pe.matmul(self.psum[:, i, 0:n], ones, self.sq[:, k, t0:t0 + n],
                               start=(k == 0), stop=(k == self.chunks - 1))
                if k == self.chunks - 1:
                    mm.then_inc(self.summed, 1)

    def vector(self, dve):
        for i, (t0, n) in enumerate(SPLITS):
            dve.wait_ge(self.summed, i + 1)
            dve.tensor_scalar(self.s["rstd"][:, t0:t0 + n], self.psum[:, i, 0:n], 1.0 / (self.chunks * P), EPS,
                              ALU.mult, ALU.add).then_inc(self.meaned, 1)
        for i, (t0, n) in enumerate(SPLITS):
            dve.wait_ge(self.rooted, i + 1)
            r = self.s["rstd"][:, t0:t0 + n]
            dve.reciprocal(r, r).then_inc(self.scaled, 1)
        dve.wait_ge(self.scaled, NS)


def modulated(dve, link, s, src, dst, norm_w, shift, scale, scaled):
    gain = s["gain"]
    link(dve.tensor_scalar(gain[:, :, :], s["mod"][:, scale:scale + KC, :], 1.0, None, ALU.add))
    w = s["par"][:, norm_w:norm_w + KC].unsqueeze(2).to_broadcast([P, KC, 1 + NSEQ])
    link(dve.tensor_tensor(gain[:, :, :], gain[:, :, :], w, ALU.mult))
    sh = s["mod"][:, shift:shift + KC, :]

    def per_seq(t, k):
        return t[:, k, 1:].unsqueeze(2).to_broadcast([P, NSEQ, LS])

    for k in range(KC):
        dve.tensor_tensor(dst[:, k, :], src[:, k, :], s["rstd"][:, :], ALU.mult).then_inc(scaled, 1)
        dve.wait_ge(scaled, k + 1)
        own = dst[:, k, SEQ:T].rearrange("p (s l) -> p s l", l=LS)
        link(dve.tensor_tensor(own, own, per_seq(gain, k), ALU.mult))
        dve.tensor_tensor(own, own, per_seq(sh, k), ALU.add)


def shifted(act, s, dst, shift, scaled):
    for k in range(KC):
        act.wait_ge(scaled, k + 1)
        act.activation(dst[:, k, 0:SEQ], dst[:, k, 0:SEQ], ACT.Identity, scale=s["gain"][:, k, 0:1],
                       bias=s["mod"][:, shift + k, 0:1])


class Scales:
    ROWS, N = 32, 3

    def __init__(self, nc, sb, sem, s, psum):
        self.s, self.ps = s, psum
        self.tops = sb("tops", [P, self.ROWS])
        self.top = sb("top_all", [self.ROWS, 1])
        self.exp = sb("exponent", [self.ROWS, 1], I32)
        self.pow = sb("powers", [self.ROWS, 2, 1], I32)
        self.diag = sb("powers_diag", [self.ROWS, 2, self.N])
        self.value = sb("scales", [P, 2 * self.N])
        self.found, self.turned, self.powered, self.spread, self.ready = (
            sem("tops_found"), sem("tops_turned"), sem("powered"), sem("scales_spread"), sem("scales_ready"))

    def turn(self, pe, c):
        pe.wait_ge(self.found, c + 1)
        pe.transpose(self.ps[0:self.ROWS, 0:P], self.tops[:, :],
                     self.s["const"][:, C_ID:C_ID + P]).then_inc(self.turned, 1)

    def spread_out(self, pe, c):
        pe.wait_ge(self.powered, c + 1)
        pe.matmul(self.ps[:, P:P + 2 * self.N], self.s["const"][0:self.ROWS, C_ONE:C_ONE + P],
                  self.diag[:, :, :], start=True, stop=True).then_inc(self.spread, 1)

    def powers(self, dve, link, c):
        dve.wait_ge(self.turned, c + 1)
        link(dve.tensor_reduce(self.top[:, :], self.ps[0:self.ROWS, 0:P], AX.X, ALU.max))
        link(dve.tensor_scalar(self.exp[:, :], self.top[:, :].bitcast(I32), 23, None, ALU.logical_shift_right))
        link(dve.tensor_scalar(self.exp[:, :], self.exp[:, :], 15, 254, ALU.max, ALU.min))
        dve.tensor_scalar(self.pow[:, 0, :], self.exp[:, :], -1, 268, ALU.mult, ALU.add)
        link(dve.tensor_scalar(self.pow[:, 1, :], self.exp[:, :], -14, None, ALU.add))
        link(dve.tensor_scalar(self.pow[:, :, :], self.pow[:, :, :], 23, None, ALU.logical_shift_left))
        ident = self.s["const"][0:self.ROWS, C_ID:C_ID + self.N].unsqueeze(1)
        dve.tensor_tensor(self.diag[:, :, :], ident.to_broadcast([self.ROWS, 2, self.N]),
                          self.pow[:, :, :].bitcast(F32).to_broadcast([self.ROWS, 2, self.N]),
                          ALU.mult).then_inc(self.powered, 1)
    POWERS_LINKS = 5

    def take(self, dve, link, c):
        dve.wait_ge(self.spread, c + 1)
        link(dve.tensor_copy(self.value[:, :], self.ps[:, P:P + 2 * self.N]))


def product(pe, bank, left, right, first, last):
    for x, parts in ((0, (0, 1)), (1, (0,))):
        for q, (t0, n) in enumerate(SPLITS):
            if first is not None and x == 0:
                first(q)
            for y in parts:
                mm = pe.matmul(bank(q), left(x), right(y, t0, n),
                               start=first is not None and x == 0 and y == 0,
                               stop=last is not None and x == 1)
            if last is not None and x == 1:
                mm.then_inc(last, 1)


def ada_phase(nc, a, s, sem):
    n_loads = MOD_FIRST
    RA, BANKS = 8, 4
    with ExitStack() as ctx:
        ring = ctx.enter_context(nc.sbuf_tensor("ada_ring", [P, RA, KC, P], F32))
        cond = ctx.enter_context(nc.sbuf_tensor("cond", [P, KC, 1 + NSEQ], F32))
        cond_act = s["cond_act"]
        mod_ps = ctx.enter_context(nc.psum_tensor("mod_ps", [P, BANKS, 512], F32))
        sum_ps = ctx.enter_context(nc.psum_tensor("sum_ps", [P, NS, 512], F32))
        small_in = sem("small_in")
        x_in = sem("x_in")
        ada_in = [sem(f"ada_in{u}") for u in range(RA)]
        cond_ready = sem("cond_ready")
        mod_summed = sem("mod_summed")
        mod_ready = sem("mod_ready")
        h_scaled = sem("h_scaled")
        chain = sem("ada_chain")
        norm = Norm(nc, sem, "norm1", s["x"], s["y"], s, sum_ps)

        with nc.Block() as block:
            @block.sync
            def _(sp):
                sp.dma_start(s["const"][:, :], a["const"]).then_inc(small_in, 16)
                sp.dma_start(s["par"][:, :], a["par"]).then_inc(small_in, 16)
                sp.dma_start(cond[:, :, :], a["cond"]).then_inc(small_in, 16)
                for k in range(KC):
                    sp.dma_start(s["x"][:, k, :], a["x"][:, k, :]).then_inc(x_in, 16)
                for u in range(RA):
                    sp.dma_start(ring[:, u, :, :], a["w_ada"][u]).then_inc(ada_in[u], 16)
                with sp.Fori(1, n_loads // RA) as i:
                    for u in range(RA):
                        sp.wait_ge(mod_summed, (i - 1) * RA + u + 1)
                        sp.dma_start(ring[:, u, :, :], a["w_ada"][i * RA + u]).then_inc(ada_in[u], 16)


            @block.scalar
            def _(act):
                act.wait_ge(small_in, 48)
                act.activation(cond_act[:, :, :], cond[:, :, :], ACT.Silu).then_inc(cond_ready, 1)
                act.wait_ge(x_in, 16 * KC)
                norm.scalar(act)
                act.sem_inc(mod_ready, BANKS)
                with act.Fori(0, n_loads // RA) as i:
                    for u in range(RA):
                        c = i * RA + u
                        act.wait_ge(mod_summed, c + 1)
                        act.activation(s["mod"][:, bass.ds(c, 1), :].rearrange("p o n -> p (o n)"),
                                       mod_ps[:, u % BANKS, 0:1 + NSEQ], ACT.Identity,
                                       bias=s["par"][:, bass.ds(c + W_BADA, 1)]).then_inc(mod_ready, 1)
                shifted(act, s, s["h"], 0, h_scaled)

            @block.tensor
            def _(pe):
                pe.wait_ge(small_in, 48)
                norm.tensor(pe)
                pe.wait_ge(cond_ready, 1)
                with pe.Fori(0, n_loads // RA) as i:
                    for u in range(RA):
                        pe.wait_ge(ada_in[u], (i + 1) * 16)
                        pe.wait_ge(mod_ready, i * RA + u + 1)
                        for k in range(KC):
                            mm = pe.matmul(mod_ps[:, u % BANKS, 0:1 + NSEQ], ring[:, u, k, :], cond_act[:, k, :],
                                           start=(k == 0), stop=(k == KC - 1))
                        mm.then_inc(mod_summed, 1)

            @block.vector
            def _(dve):
                norm.vector(dve)
                dve.wait_ge(mod_ready, BANKS + 2 * KC)
                modulated(dve, Chain(dve, chain).link, s, s["x"], s["h"], W_N1, 0, KC, h_scaled)


def project_phase(nc, a, s, sem):
    TURNS = NCH // RING
    with ExitStack() as ctx:
        def sb(name, shape):
            return ctx.enter_context(nc.sbuf_tensor(name, shape, F32))

        ring = sb("in_ring", [P, RING, KC, P])
        w16 = ctx.enter_context(nc.sbuf_tensor("in_parts", [P, 2, RING, KC, P], F16))
        h16 = ctx.enter_context(nc.sbuf_tensor("h_parts_in", [P, 2, KC, T], F16))
        h_unit = sb("h_unit_in", [P, 1])
        next_unit = sb("next_unit", [P, 1])
        unit = sb("unit_in", [P, 1])
        wv = sb("wv", [P, KC, AW])
        wdt = sb("wdt", [P, KC, SH])
        stage = sb("stage", [P, 2, T])
        raw_p = sb("raw_p", [P, CW - 1 + SEQ])
        raw_s = sb("raw_s", [P, NSEQ, CW - 1 + LS])
        conv = sb("conv", [P, T])
        state = sb("state", [P, 12, NSEQ, CW - 1])
        tail = sb("tail", [P, 12, 1 + NSEQ, CW - 1])
        ps = ctx.enter_context(nc.psum_tensor("in_ps", [P, 2 * NS, 512], F32))
        ps_v = ctx.enter_context(nc.psum_tensor("v_ps", [P, 512], F32))
        ps_dt = ctx.enter_context(nc.psum_tensor("dt_ps", [P, 512], F32))
        w_in = [sem(f"w_in{u}") for u in range(RING)]
        wide_in = sem("wide_in")
        summed = sem("proj_summed")
        banks_free = sem("proj_banks_free")
        staged = sem("proj_staged")
        stored = [sem(f"proj_stored{u}") for u in range(2)]
        raw_ready = sem("raw_ready")
        zeroed = sem("raw_zeroed")
        convolved = sem("convolved")
        chain = sem("conv_chain")
        v_summed, v_taken = sem("v_summed"), sem("v_taken")
        dt_summed, dt_taken = sem("dt_summed"), sem("dt_taken")
        rows_out = sem("rows_out")
        h = s["h"]
        scales = Scales(nc, lambda n, shape, dt=F32: ctx.enter_context(nc.sbuf_tensor(n + "_in", shape, dt)),
                        lambda n: sem(n + "_in"), s, ps_dt)
        S_H, S_W = 0, 1
        h_hi, w_hi, h_split, w_split = sem("h_hi_in"), sem("w_hi_in"), sem("h_split_in"), sem("w_split_in")
        unit_ready = sem("unit_ready")

        with nc.Block() as block:
            @block.sync
            def _(sp):
                for u in range(RING):
                    sp.dma_start(ring[:, u, :, :], a["w_in"][u]).then_inc(w_in[u], 16)
                sp.dma_start(state[:, :, :, :], a["state_conv"]).then_inc(wide_in, 16)
                sp.dma_start(wv[:, :, :], a["w_v"]).then_inc(wide_in, 16)
                sp.dma_start(wdt[:, :, :], a["w_dt"]).then_inc(wide_in, 16)
                with sp.Fori(1, TURNS) as i:
                    for u in range(RING):
                        sp.wait_ge(w_split, (i - 1) * RING + u + 1)
                        sp.dma_start(ring[:, u, :, :], a["w_in"][i * RING + u]).then_inc(w_in[u], 16)
                sp.wait_ge(v_taken, 1 + TILES + 1)
                vp = a["v_out"][0:SEQ, :].rearrange("(n p) c -> p n c", p=P)
                sp.dma_start(vp, s["v_tok"][:, 0:TILES, :]).then_inc(rows_out, 16)
                sp.dma_start(a["v_out"][SEQ:T, :], s["v_tok"][0:TS, TILES, :]).then_inc(rows_out, 16)
                sp.wait_ge(convolved, 12)
                sp.dma_start(a["conv_out"], tail[:, :, :, :]).then_inc(rows_out, 16)
                sp.wait_ge(rows_out, 48)
                for u in range(2):
                    sp.wait_ge(stored[u], 16 * (NCH // 2 + 1))

            @block.tensor
            def _(pe):
                def turn(i, last):
                    for u in range(RING):
                        pe.wait_ge(w_split, i * RING + u + 1)

                        def free(j):
                            pe.wait_ge(banks_free, i * (RING * NS) + u * NS + j + 1)

                        for k in range(KC):
                            if isinstance(i, int) and u == 0:
                                pe.wait_ge(h_split, k + 1)
                            product(pe, lambda j: ps[:, (u % 2) * NS + j, 0:SPLITS[j][1]],
                                    lambda x: w16[:, x, u, k, :], lambda y, t0, n: h16[:, y, k, t0:t0 + n],
                                    free if k == 0 else None, summed if k == KC - 1 else None)
                        if u == 1 and not last:
                            scales.turn(pe, i + 1)
                        if u == 2 and not last:
                            scales.spread_out(pe, i + 1)

                scales.turn(pe, 0)
                scales.spread_out(pe, 0)
                turn(0, False)
                with pe.Fori(1, TURNS - 1) as i:
                    turn(i, False)
                turn(TURNS - 1, True)
                pe.wait_ge(wide_in, 48)
                for t in range(TILES + 1):
                    n = min(P, T - t * P)
                    pe.wait_ge(v_taken, t + 1)
                    for k in range(KC):
                        mm = pe.matmul(ps_v[0:n, :], h[:, k, t * P:t * P + n], wv[:, k, :],
                                       start=(k == 0), stop=(k == KC - 1))
                    mm.then_inc(v_summed, 1)
                    pe.wait_ge(dt_taken, t + 1)
                    for k in range(KC):
                        mm = pe.matmul(ps_dt[0:n, 0:SH], h[:, k, t * P:t * P + n], wdt[:, k, :],
                                       start=(k == 0), stop=(k == KC - 1))
                    mm.then_inc(dt_summed, 1)

            @block.scalar
            def _(act):
                act.sem_inc(banks_free, 2 * NS)
                act.sem_inc(v_taken, 1)
                for u in range(2):
                    act.sem_inc(stored[u], 16)

                def scaled(out, src, n, done):
                    act.activation(out, src, ACT.Copy, scale=scales.value[:, n:n + 1]).then_inc(done, 1)

                def split(i, u):
                    act.wait_ge(summed, i * (RING * NS) + (u + 1) * NS)
                    scaled(w16[:, 0, u, :, :], ring[:, u, :, :], S_W, w_hi)

                def beside(i, u, last):
                    if last:
                        return
                    if u == 2:
                        act.wait_ge(scales.ready, i + 2)
                        for v in range(3):
                            split(i, v)
                    if u == 3:
                        split(i, 3)

                def take(i, func, row0, dest, last=False):
                    act.wait_ge(unit_ready, i + 1)
                    for u in range(RING):
                        b = u % 2
                        act.wait_ge(stored[b], i * (16 * RING // 2) + 16 * (u // 2 + 1))
                        for j, (t0, n) in enumerate(SPLITS):
                            act.wait_ge(summed, i * (RING * NS) + u * NS + j + 1)
                            act.activation(stage[:, b, t0:t0 + n], ps[:, b * NS + j, 0:n], func,
                                           scale=unit[:, :]).then_inc(banks_free, 1)
                        act.wait_ge(banks_free, i * (RING * NS) + (u + 1) * NS + 2 * NS)
                        act.dma_start(dest[i * RING + (u - row0)], stage[:, b, :]).then_inc(stored[b], 16)
                        beside(i, u, last)

                act.wait_ge(scales.ready, 1)
                for k in range(KC):
                    scaled(h16[:, 0, k, :], h[:, k, :], S_H, h_hi)
                    if k < RING:
                        scaled(w16[:, 0, k, :, :], ring[:, k, :, :], S_W, w_hi)
                take(CH_Q // RING, ACT.Copy, 0, a["proj"])
                take(CH_K // RING, ACT.Copy, CH_K, a["k_out"])
                with act.Fori(CH_Z // RING, CH_X // RING) as i:
                    take(i, ACT.Silu, 0, a["proj"])
                act.wait_ge(zeroed, 1)
                act.wait_ge(wide_in, 48)
                with act.Fori(CH_X // RING, CH_G // RING) as i:
                    act.wait_ge(unit_ready, i + 1)
                    for u in range(RING):
                        b = u % 2
                        for j, (t0, n) in enumerate(SPLITS):
                            act.wait_ge(summed, i * (RING * NS) + u * NS + j + 1)
                            own = min(n, SEQ - t0)
                            ins = act.activation(raw_p[:, CW - 1 + t0:CW - 1 + t0 + own], ps[:, b * NS + j, 0:own],
                                                 ACT.Copy, scale=unit[:, :])
                            if own < n:
                                ins = act.activation(raw_s[:, :, CW - 1:], ps[:, b * NS + j, own:n].rearrange(
                                    "p (s l) -> p s l", l=LS), ACT.Copy, scale=unit[:, :])
                            ins.then_inc(banks_free, 1)
                        act.copy(raw_s[:, :, 0:CW - 1],
                                 state[:, bass.ds(i * RING + (u - CH_X), 1), :, :].rearrange(
                                     "p o s l -> p (o s) l")).then_inc(raw_ready, 1)
                        beside(i, u, False)
                        act.wait_ge(stored[b], i * (16 * RING // 2) + 16 * (u // 2 + 1))
                        act.wait_ge(convolved, i * RING + (u + 1 - CH_X))
                        act.activation(stage[:, b, :], conv[:, :], ACT.Silu).then_inc(staged, 1)
                        act.wait_ge(staged, i * RING + (u + 1 - CH_X))
                        act.dma_start(a["proj"][i * RING + u], stage[:, b, :]).then_inc(stored[b], 16)
                with act.Fori(CH_G // RING, TURNS - 1) as i:
                    take(i, ACT.Sigmoid, 0, a["proj"])
                take(TURNS - 1, ACT.Sigmoid, 0, a["proj"], True)
                for t in range(TILES + 1):
                    n = min(P, T - t * P)
                    act.wait_ge(v_summed, t + 1)
                    act.copy(s["v_tok"][0:n, t, :], ps_v[0:n, :]).then_inc(v_taken, 1)

            @block.vector
            def _(dve):
                link = Chain(dve, chain)
                dve.sem_inc(dt_taken, 1)
                dve.memset(raw_p[:, 0:CW - 1], 0.0).then_inc(zeroed, 1)
                dve.memset(s["v_tok"][TS:P, TILES, :], 0.0)
                def largest(n, src):
                    link.mark(dve.tensor_reduce(scales.tops[:, n:n + 1], src, AX.X, ALU.max,
                                                apply_absolute_value=True))

                def found(i):
                    for u in range(RING):
                        dve.wait_ge(w_in[u], (i + 1) * 16)
                    largest(S_W, ring[:, :, :, :].rearrange("p u k e -> p (u k e)"))
                    link.wait(link.base + link.n)
                    dve.sem_inc(scales.found, 1)

                def take_scales(i):
                    scales.take(dve, link.link, i)
                    if isinstance(i, int) and i == 0:
                        link.link(dve.tensor_copy(h_unit[:, :], scales.value[:, 3 + S_H:4 + S_H]))
                    link.link(dve.tensor_tensor(next_unit[:, :], scales.value[:, 3 + S_W:4 + S_W], h_unit[:, :],
                                                ALU.mult))
                    dve.sem_inc(scales.ready, 1)

                def rest(out, src, n, hi, done):
                    dve.scalar_tensor_tensor(out, src, scales.value[:, n:n + 1], hi, ALU.mult,
                                             ALU.subtract).then_inc(done, 1)

                def split(i, u):
                    dve.wait_ge(w_hi, i * RING + u + 1)
                    rest(w16[:, 1, u, :, :], ring[:, u, :, :], S_W, w16[:, 0, u, :, :], w_split)

                def convolve(c):
                    dve.wait_ge(raw_ready, c + 1)

                    def tap(j):
                        return s["par"][:, bass.ds(c * CW + (W_CW + j), 1)]

                    cs = conv[:, SEQ:T].rearrange("p (s l) -> p s l", l=LS)
                    bias = s["par"][:, bass.ds(c + W_CB, 1)]
                    at_p = link.mark(dve.tensor_scalar(conv[:, 0:SEQ], raw_p[:, 0:SEQ], tap(0), bias,
                                                       ALU.mult, ALU.add))
                    at_s = link.mark(dve.tensor_scalar(cs, raw_s[:, :, 0:LS], tap(0), bias,
                                                       ALU.mult, ALU.add))
                    for j in range(1, CW):
                        link.wait(at_p)
                        ins = dve.scalar_tensor_tensor(conv[:, 0:SEQ], raw_p[:, j:j + SEQ], tap(j),
                                                       conv[:, 0:SEQ], ALU.mult, ALU.add)
                        at_p = link.mark(ins) if j < CW - 1 else None
                        link.wait(at_s)
                        ins = dve.scalar_tensor_tensor(cs, raw_s[:, :, j:j + LS], tap(j), cs,
                                                       ALU.mult, ALU.add)
                        at_s = link.mark(ins) if j < CW - 1 else None
                    out = tail[:, bass.ds(c, 1), :, :].rearrange("p o s l -> p (o s) l")
                    dve.tensor_copy(out[:, 0, :], raw_p[:, SEQ:SEQ + CW - 1])
                    dve.tensor_copy(out[:, 1:, :], raw_s[:, :, LS:LS + CW - 1]).then_inc(convolved, 1)

                def turn(i, work=None):
                    set_unit(i)
                    found(i + 1)
                    if work:
                        work(0)
                    scales.powers(dve, link.link, i + 1)
                    if work:
                        work(1)
                    take_scales(i + 1)
                    for u in range(3):
                        split(i + 1, u)
                    if work:
                        work(2)
                    split(i + 1, 3)
                    if work:
                        work(3)

                def set_unit(i):
                    dve.wait_ge(banks_free, i * (RING * NS) + 2 * NS)
                    if isinstance(i, int) and i == 0:
                        link.link(dve.tensor_scalar(unit[:, :], next_unit[:, :], HD ** -0.5, None, ALU.mult))
                    else:
                        link.link(dve.tensor_copy(unit[:, :], next_unit[:, :]))
                    dve.sem_inc(unit_ready, 1)

                link.link(dve.memset(scales.tops[:, :], 1.0))
                largest(S_H, h[:, :, :].rearrange("p k t -> p (k t)"))
                found(0)
                scales.powers(dve, link.link, 0)
                take_scales(0)
                for k in range(KC):
                    dve.wait_ge(h_hi, k + 1)
                    rest(h16[:, 1, k, :], h[:, k, :], S_H, h16[:, 0, k, :], h_split)
                    if k < RING:
                        split(0, k)
                PER = 1 + 1 + Scales.POWERS_LINKS + 2
                turn(0)
                n = CH_X // RING - 1
                with dve.Fori(0, n) as i, link.turns(i, n, PER):
                    turn(i + 1)
                n = (CH_G - CH_X) // RING
                with dve.Fori(0, n) as i, link.turns(i, n, PER + 6 * RING):
                    turn(i + CH_X // RING, lambda u: convolve(i * RING + u))
                n = TURNS - 1 - CH_G // RING
                with dve.Fori(0, n) as i, link.turns(i, n, PER):
                    turn(i + CH_G // RING)
                set_unit(TURNS - 1)
                for t in range(TILES + 1):
                    n = min(P, T - t * P)
                    dve.wait_ge(dt_summed, t + 1)
                    dve.tensor_tensor(s["dt_tok"][0:n, t, :], ps_dt[0:n, 0:SH],
                                      s["par"][0:n, W_DTB:W_DTB + SH], ALU.add).then_inc(dt_taken, 1)


STEPS = [(sp, kb, max(0, kb - 4 * sp) * P) for sp in range(2) for kb in range(4 * sp + 3, -1, -1)]
NSTEP = len(STEPS)
HALF = SEQ // 2


def attend_phase(nc, a, s, sem):
    with ExitStack() as ctx:
        def sb(name, shape):
            return ctx.enter_context(nc.sbuf_tensor(name, shape, F32))

        q = sb("q", [HD, 2, SEQ])
        k = sb("k", [HD, 2, SEQ])
        v = sb("v", [P, 2, TILES, HD])
        soft = sb("soft", [P, 3, HALF])
        later = sb("later", [P, 2, HALF])
        wgt = sb("wgt", [P, 2, HALF])
        out = sb("o_stage", [HD, 2, SEQ])
        bias_v = sb("bias_v", [P, 2])
        bias_a = sb("bias_a", [P, 2])
        zs = ctx.enter_context(nc.psum_tensor("z_ps", [P, 4, 512], F32))
        os_ = ctx.enter_context(nc.psum_tensor("o_ps", [P, 2, 512], F32))
        qk_in = [sem(f"qk_in{u}") for u in range(2)]
        v_ready = sem("v_ready")
        z_ready, clamped, logged, soft_ready, later_ready = (
            sem("z_ready"), sem("clamped"), sem("logged"), sem("soft_ready"), sem("later_ready"))
        exped, masked, weighted, w_ready, w_masked, pv_done, o_taken = (
            sem("exped"), sem("masked"), sem("weighted"), sem("w_ready"), sem("w_masked"), sem("pv_done"),
            sem("o_taken"))
        o_out = [sem(f"o_out{u}") for u in range(2)]
        bias_in_v, bias_in_a = sem("bias_in_v"), sem("bias_in_a")
        const = s["const"]
        ntri, neg = const[:, C_NTRI:C_NTRI + P], const[:, C_NEG:C_NEG + P]
        strict = const[:, C_STRICT:C_STRICT + P]
        q_rows = a["proj"].rearrange("c p t -> (c p) t")
        k_rows = a["k_out"].rearrange("c p t -> (c p) t")
        NDIAG = sum(kb >= 4 * sp for sp, kb, _ in STEPS)
        diag_no = {n: sum(kb >= 4 * sp for sp, kb, _ in STEPS[:n]) for n in range(NSTEP)}
        NLATER = sum(kb > 0 for _, kb, _ in STEPS)
        later_no = {n: sum(kb > 0 for _, kb, _ in STEPS[:n]) for n in range(NSTEP)}

        with nc.Block() as block:
            @block.sync
            def _(sp):
                def load(h, u):
                    row = h * HD if isinstance(h, int) else bass.ds(h * HD, HD)
                    rows = slice(row, row + HD) if isinstance(h, int) else row
                    sp.dma_start(q[:, u, :], q_rows[rows, 0:SEQ]).then_inc(qk_in[u], 16)
                    sp.dma_start(k[:, u, :], k_rows[rows, 0:SEQ]).then_inc(qk_in[u], 16)

                load(0, 0)
                load(1, 1)
                with sp.Fori(1, HEADS // 2) as i:
                    for u in range(2):
                        sp.wait_ge(pv_done, (i - 1) * (2 * NSTEP) + (u + 1) * NSTEP)
                        load(i * 2 + u, u)
                for u in range(2):
                    sp.wait_ge(o_out[u], 16 * (HEADS // 2 + 1))

            @block.gpsimd
            def _(pool):
                def fetch(h, u):
                    cols = bass.ds(h * HD, HD) if not isinstance(h, int) else slice(h * HD, h * HD + HD)
                    pool.tensor_copy(v[:, u, :, :], s["v_tok"][:, 0:TILES, cols]).then_inc(v_ready, 1)

                fetch(0, 0)
                fetch(1, 1)
                with pool.Fori(1, HEADS // 2) as i:
                    for u in range(2):
                        pool.wait_ge(pv_done, (i - 1) * (2 * NSTEP) + (u + 1) * NSTEP)
                        fetch(i * 2 + u, u)

            @block.tensor
            def _(pe):
                with pe.Fori(0, HEADS // 2) as i:
                    for u in range(2):
                        base = i * (2 * NSTEP) + u * NSTEP

                        def scores(n):
                            half, kb, off = STEPS[n]
                            pe.matmul(zs[:, n % 4, off:HALF], k[:, u, kb * P:(kb + 1) * P],
                                      q[:, u, half * HALF + off:(half + 1) * HALF],
                                      start=True, stop=True).then_inc(z_ready, 1)

                        def sums(n):
                            half, kb, off = STEPS[n]
                            diag = kb >= 4 * half
                            off2 = off + P if diag else 0
                            pe.wait_ge(soft_ready, base + n + 1)
                            mm = pe.matmul(zs[:, n % 4, off:HALF], ntri, soft[:, n % 3, off:HALF],
                                           start=False, stop=True, skip_group_check=True)
                            if off2 < HALF:
                                pe.wait_ge(later_ready, i * (2 * NLATER) + u * NLATER + later_no[n])
                                mm = pe.matmul(zs[:, n % 4, off2:HALF], neg, later[:, n % 2, off2:HALF],
                                               start=False, stop=True, skip_group_check=True)
                            mm.then_inc(weighted, 1)

                        def values(n):
                            half, kb, off = STEPS[n]
                            pe.wait_ge(w_ready, base + n + 1)
                            if kb >= 4 * half:
                                pe.wait_ge(w_masked, i * (2 * NDIAG) + u * NDIAG + diag_no[n] + 1)
                            if kb == 4 * half + 3:
                                pe.wait_ge(o_taken, i * 4 + u * 2 + half + 1)
                            pe.matmul(os_[0:HD, half, off:HALF], v[:, u, kb, :], wgt[:, n % 2, off:HALF],
                                      start=(kb == 4 * half + 3), stop=(kb == 0),
                                      skip_group_check=True).then_inc(pv_done, 1)

                        pe.wait_ge(qk_in[u], (i + 1) * 32)
                        scores(0)
                        scores(1)
                        pe.wait_ge(v_ready, i * 2 + u + 1)
                        for n in range(NSTEP):
                            if n + 2 < NSTEP:
                                scores(n + 2)
                            sums(n)
                            if n >= 1:
                                values(n - 1)
                        values(NSTEP - 1)

            @block.vector
            def _(dve):
                with dve.Fori(0, HEADS // 2) as i:
                    for u in range(2):
                        base = i * (2 * NSTEP) + u * NSTEP
                        bias = bias_v[:, u:u + 1]
                        dve.tensor_copy(bias, s["par"][:, bass.ds(i * 2 + (u + W_SB), 1)]).then_inc(bias_in_v, 1)
                        dve.wait_ge(bias_in_v, i * 2 + u + 1)

                        def clamp(n):
                            _, _, off = STEPS[n]
                            dve.wait_ge(z_ready, base + n + 1)
                            if n >= 3:
                                dve.wait_ge(weighted, base + n - 2)
                            dve.tensor_scalar(soft[:, n % 3, off:HALF], zs[:, n % 4, off:HALF], bias, CLAMP,
                                              ALU.add, ALU.min).then_inc(clamped, 1)

                        def soften(n):
                            half, kb, off = STEPS[n]
                            dve.wait_ge(logged, base + n + 1)
                            x = soft[:, n % 3, :]
                            ins = dve.scalar_tensor_tensor(x[:, off:HALF], zs[:, n % 4, off:HALF], bias,
                                                           x[:, off:HALF], ALU.add, ALU.max)
                            if kb >= 4 * half:
                                ins.then_inc(masked, 1)
                                dve.wait_ge(masked, i * (2 * NDIAG) + u * NDIAG + diag_no[n] + 1)
                                ins = dve.tensor_tensor(x[:, off:off + P], x[:, off:off + P], strict, ALU.mult)
                            ins.then_inc(soft_ready, 1)
                            if kb == 0:
                                return
                            dve.wait_ge(soft_ready, base + n + 1)
                            if n >= 1:
                                dve.wait_ge(weighted, base + n)
                            now, then = later[:, n % 2, :], later[:, (n + 1) % 2, :]
                            if kb >= 4 * half:
                                ins = dve.tensor_copy(then[:, off:off + P], x[:, off:off + P])
                                off += P
                            if off < HALF:
                                if n >= 1:
                                    dve.wait_ge(later_ready, i * (2 * NLATER) + u * NLATER + later_no[n])
                                ins = dve.tensor_tensor(then[:, off:HALF], now[:, off:HALF], x[:, off:HALF],
                                                        ALU.add)
                            ins.then_inc(later_ready, 1)

                        def mask(n):
                            half, kb, off = STEPS[n]
                            if kb >= 4 * half:
                                dve.wait_ge(w_ready, base + n + 1)
                                x = wgt[:, n % 2, off:off + P]
                                dve.tensor_tensor(x, x, strict, ALU.mult).then_inc(w_masked, 1)

                        clamp(0)
                        for n in range(NSTEP):
                            if n + 1 < NSTEP:
                                clamp(n + 1)
                            soften(n)
                            if n >= 1:
                                mask(n - 1)

            @block.scalar
            def _(act):
                act.preload_act_table_set("natural_log_exp_and_others")
                act.sem_inc(o_taken, 2)
                for u in range(2):
                    act.sem_inc(o_out[u], 16)
                with act.Fori(0, HEADS // 2) as i:
                    for u in range(2):
                        base = i * (2 * NSTEP) + u * NSTEP
                        bias = bias_a[:, u:u + 1]
                        act.copy(bias, s["par"][:, bass.ds(i * 2 + (u + W_SB), 1)]).then_inc(bias_in_a, 1)
                        act.wait_ge(bias_in_a, i * 2 + u + 1)

                        def log(n):
                            _, _, off = STEPS[n]
                            x = soft[:, n % 3, off:HALF]
                            act.wait_ge(clamped, base + n + 1)
                            act.activation(x, x, ACT.Exp).then_inc(exped, 1)
                            act.wait_ge(exped, base + n + 1)
                            act.activation(x, x, ACT.Ln, bias=1.0).then_inc(logged, 1)

                        def weigh(n):
                            _, _, off = STEPS[n]
                            act.wait_ge(weighted, base + n + 1)
                            if n >= 2:
                                act.wait_ge(pv_done, base + n - 1)
                            act.activation(wgt[:, n % 2, off:HALF], zs[:, n % 4, off:HALF], ACT.Exp,
                                           bias=bias).then_inc(w_ready, 1)

                        def take(half, after):
                            act.wait_ge(pv_done, base + after)
                            act.copy(out[:, u, half * HALF:(half + 1) * HALF],
                                     os_[0:HD, half, :]).then_inc(o_taken, 1)

                        log(0)
                        act.wait_ge(o_out[u], (i + 1) * 16)
                        for n in range(1, NSTEP):
                            log(n)
                            weigh(n - 1)
                            if n == 7:
                                take(0, 4)
                        weigh(NSTEP - 1)
                        take(1, NSTEP)
                        act.wait_ge(o_taken, i * 4 + u * 2 + 4)
                        act.dma_start(a["o"][bass.ds((i * 2 + u) * HD, HD), 0:SEQ],
                                      out[:, u, :]).then_inc(o_out[u], 16)


def attend_sample_phase(nc, a, s, sem):
    with ExitStack() as ctx:
        def sb(name, shape, dt=F32):
            return ctx.enter_context(nc.sbuf_tensor(name, shape, dt))

        NC_ = AW // P
        pages = sb("pages", [1, NSEQ * NPAGE], I32)
        kp = sb("kp", [P, 2, NPAGE, AW])
        vp = sb("vp", [P, 2, NPAGE, AW])
        qd = sb("qd", [P, NC_, TS])
        qz = sb("qz", [P, NSEQ, NC_, 2, LS])
        qn = sb("qn", [HD, HEADS, TS])
        kn = sb("kn", [HD, HEADS, TS])
        bias = sb("bias_cols", [P, HEADS, LS])
        z_new = sb("z_new", [TS, HEADS, TS])
        soft_new = sb("soft_new", [P, HEADS, TS])
        w_new = sb("w_new", [P, HEADS, TS])
        z = sb("z_past", [P, 2, NPAGE, TS])
        soft = sb("soft_past", [P, 2, NPAGE, TS])
        later = sb("later_past", [P, 2, NPAGE, TS])
        o = sb("o_sample", [P, NC_, TS])
        zs = ctx.enter_context(nc.psum_tensor("zp_ps", [P, 2, 512], F32))
        os_ = ctx.enter_context(nc.psum_tensor("op_ps", [P, 2, 512], F32))
        zn = ctx.enter_context(nc.psum_tensor("zn_ps", [P, 512], F32))
        pages_in, q_in = sem("pages_in"), sem("q_in")
        k_in = [sem(f"k_page_in{u}") for u in range(2)]
        v_in = [sem(f"v_page_in{u}") for u in range(2)]
        ready, zn_done, sn_done, new_act, new_ready = (
            sem("q_blocks_ready"), sem("zn_done"), sem("sn_done"), sem("new_act"), sem("new_ready"))
        chain = sem("sample_chain")
        zp_done, sp_done, op_done = sem("zp_done"), sem("sp_done"), sem("op_done")
        clamped, exped, logged, softened, arg_ready, w_ready, o_taken, o_out = (
            sem("s_clamped"), sem("s_exped"), sem("s_logged"), sem("s_softened"), sem("s_arg"), sem("s_w"),
            sem("s_o_taken"), sem("s_o_out"))
        const = s["const"]
        ntri, neg = const[:, C_NTRI:C_NTRI + P], const[:, C_NEG:C_NEG + P]

        with nc.Block() as block:
            @block.sync
            def _(sp):
                sp.dma_start(pages[:, :], a["pages"]).then_inc(pages_in, 16)
                sp.dma_start(qd[:, :, :], a["proj"][0:NC_, :, SEQ:T].rearrange("c p t -> p c t")).then_inc(q_in, 16)
                by_head = a["proj"][0:NC_].rearrange("c (g d) t -> d (c g) t", g=2)
                sp.dma_start(qn[:, :, :], by_head[:, :, SEQ:T]).then_inc(q_in, 16)
                by_head = a["k_out"].rearrange("c (g d) t -> d (c g) t", g=2)
                sp.dma_start(kn[:, :, :], by_head[:, :, SEQ:T]).then_inc(q_in, 16)
                sp.wait_ge(pages_in, 16)

                with sp.Fori(0, NSEQ // 2) as i:
                    for u in range(2):
                        sp.wait_ge(zp_done, i * 2 + u + 1)
                        for j in range(NPAGE):
                            at = bass.ds((i * 2 + u) * NPAGE + j, 1)
                            page = sp.value_load(pages[0:1, at], min_val=0, max_val=POOL - 1)
                            sp.dma_start(kp[:, u, j, :], a["cache_k"][bass.ds(page, 1)].rearrange(
                                "o p c k -> (o p) (c k)")).then_inc(k_in[u], 16)
                sp.wait_ge(o_taken, NSEQ + 2)
                for c in range(NC_):
                    sp.dma_start(a["o"][c * P:(c + 1) * P, SEQ:T], o[:, c, :]).then_inc(o_out, 16)
                sp.wait_ge(o_out, 16 * NC_)

            @block.gpsimd
            def _(pool):
                pool.wait_ge(pages_in, 16)
                with pool.Fori(0, NSEQ // 2) as i:
                    for u in range(2):
                        pool.wait_ge(op_done, i * 2 + u + 1)
                        for j in range(NPAGE):
                            at = bass.ds((i * 2 + u) * NPAGE + j, 1)
                            page = pool.value_load(pages[0:1, at], min_val=0, max_val=POOL - 1)
                            pool.dma_start(vp[:, u, j, :], a["cache_v"][bass.ds(page, 1)].rearrange(
                                "o k c -> (o k) c")).then_inc(v_in[u], 16)

            @block.tensor
            def _(pe):
                pe.sem_inc(op_done, 2)
                pe.sem_inc(zp_done, 2)
                pe.wait_ge(q_in, 48)
                for h in range(HEADS):
                    mm = pe.matmul(zn[0:TS, h * TS:(h + 1) * TS], kn[:, h, :], qn[:, h, :],
                                   start=(h == 0), stop=True, skip_group_check=True)
                mm.then_inc(zn_done, 1)
                pe.wait_ge(new_ready, 1)
                pe.matmul(zn[0:TS, :], ntri[0:TS, 0:TS], soft_new[0:TS, :, :], start=False, stop=True,
                          skip_group_check=True).then_inc(sn_done, 1)
                pe.wait_ge(ready, 1)

                def scores(seq, i, u):
                    pe.wait_ge(k_in[u], (i + 1) * (16 * NPAGE))
                    for j in range(NPAGE):
                        for c in range(NC_):
                            col = (j * NC_ + c) * 2 * LS
                            rhs = qz[:, bass.ds(seq, 1), c, :, :].rearrange("p o g l -> p (o g l)")
                            mm = pe.matmul(zs[:, u, col:col + 2 * LS], kp[:, u, j, c * P:(c + 1) * P], rhs,
                                           start=(j == 0 and c == 0), stop=True, skip_group_check=True)
                    mm.then_inc(zp_done, 1)

                def rest(seq, i, u):
                    pe.wait_ge(softened, seq + 1)
                    pe.matmul(zs[:, u, :], ntri, soft[:, u, :, :], start=False, stop=True,
                              skip_group_check=True)
                    pe.matmul(zs[:, u, :], neg, later[:, u, :, :], start=False, stop=True,
                              skip_group_check=True).then_inc(sp_done, 1)
                    pe.wait_ge(w_ready, seq + 1)
                    pe.wait_ge(v_in[u], (i + 1) * (16 * NPAGE))
                    pe.wait_ge(o_taken, seq + 1)
                    for c in range(NC_):
                        out = os_[:, u, c * 2 * LS:(c + 1) * 2 * LS]
                        for j in range(NPAGE):
                            pe.matmul(out, vp[:, u, j, c * P:(c + 1) * P], z[:, u, j, c * 2 * LS:(c + 1) * 2 * LS],
                                      start=(j == 0), stop=False)
                        mm = pe.matmul(out, s["v_tok"][:, TILES, c * P:(c + 1) * P],
                                       w_new[:, 2 * c:2 * c + 2, bass.ds(seq * LS, LS)], start=False, stop=True)
                    mm.then_inc(op_done, 1)

                pe.wait_ge(new_ready, 2)
                scores(0, 0, 0)
                with pe.Fori(0, NSEQ // 2 - 1) as i:
                    scores(i * 2 + 1, i, 1)
                    rest(i * 2, i, 0)
                    scores(i * 2 + 2, i + 1, 0)
                    rest(i * 2 + 1, i, 1)
                scores(NSEQ - 1, NSEQ // 2 - 1, 1)
                rest(NSEQ - 2, NSEQ // 2 - 1, 0)
                rest(NSEQ - 1, NSEQ // 2 - 1, 1)

            @block.vector
            def _(dve):
                link = Chain(dve, chain)
                dve.memset(qz[:, :, :, :, :], 0.0)
                dve.memset(soft_new[:, :, :], 0.0)
                link.link(dve.memset(w_new[:, :, :], 0.0))
                cols = s["par"][:, W_SB:W_SB + HEADS]
                link.mark(dve.tensor_copy(bias[:, :, :], cols.unsqueeze(2).to_broadcast([P, HEADS, LS])))
                dve.wait_ge(q_in, 48)
                for g in range(2):
                    rows = slice(g * HD, (g + 1) * HD)
                    for c in range(NC_):
                        ins = dve.tensor_copy(qz[rows, :, c, g, :],
                                              qd[rows, c, :].rearrange("p (s l) -> p s l", l=LS))
                ins.then_inc(ready, 1)
                dve.wait_ge(zn_done, 1)
                b_new = s["par"][0:TS, W_SB:W_SB + HEADS].unsqueeze(2).to_broadcast([TS, HEADS, TS])
                strict = const[0:TS, C_BSTRICT:C_BSTRICT + TS].unsqueeze(1).to_broadcast([TS, HEADS, TS])
                zn3 = zn[0:TS, :].rearrange("p (h t) -> p h t", t=TS)
                sn = soft_new[0:TS, :, :]
                wn = w_new[0:TS, :, :]
                link.link(dve.tensor_tensor(z_new[:, :, :], zn3, b_new, ALU.add))
                dve.tensor_scalar(sn, z_new[:, :, :], CLAMP, None, ALU.min).then_inc(clamped, 1)
                dve.wait_ge(new_act, 2)
                link.link(dve.tensor_tensor(sn, sn, z_new[:, :, :], ALU.max))
                dve.tensor_tensor(sn, sn, strict, ALU.mult).then_inc(new_ready, 1)
                dve.wait_ge(sn_done, 1)
                dve.tensor_tensor(wn, zn3, b_new, ALU.add).then_inc(arg_ready, 1)
                dve.wait_ge(new_act, 3)
                dve.tensor_tensor(wn, wn, strict, ALU.mult).then_inc(new_ready, 1)

                b4 = bias[:, :, :].rearrange("p h l -> p (h l)").unsqueeze(1).to_broadcast([P, NPAGE, TS])

                def first(seq, u):
                    dve.wait_ge(zp_done, seq + 3)
                    link.link(dve.tensor_tensor(z[:, u, :, :], zs[:, u, :].rearrange("p (j n) -> p j n", n=TS),
                                                b4, ALU.add))
                    dve.tensor_scalar(soft[:, u, :, :], z[:, u, :, :], CLAMP, None, ALU.min).then_inc(clamped, 1)

                def second(seq, u):
                    dve.wait_ge(logged, seq + 1)
                    new = soft_new[:, :, bass.ds(seq * LS, LS)]
                    dve.tensor_copy(later[:, u, NPAGE - 1, :].rearrange("p (h l) -> p h l", l=LS), new)
                    link.link(dve.tensor_tensor(soft[:, u, :, :], soft[:, u, :, :], z[:, u, :, :], ALU.max))
                    for j in range(NPAGE - 2, -1, -1):
                        ins = dve.tensor_tensor(later[:, u, j, :], later[:, u, j + 1, :], soft[:, u, j + 1, :],
                                                ALU.add)
                        if j:
                            link.link(ins)
                    ins.then_inc(softened, 1)
                    dve.wait_ge(sp_done, seq + 1)
                    dve.tensor_tensor(z[:, u, :, :], zs[:, u, :].rearrange("p (j n) -> p j n", n=TS),
                                      b4, ALU.add).then_inc(arg_ready, 1)

                with dve.Fori(0, NSEQ // 2) as i, link.turns(i, NSEQ // 2, 2 * NPAGE):
                    for u in range(2):
                        first(i * 2 + u, u)
                        second(i * 2 + u, u)

            @block.scalar
            def _(act):
                act.preload_act_table_set("natural_log_exp_and_others")
                act.sem_inc(o_taken, 2)
                sn, wn = soft_new[0:TS, :, :], w_new[0:TS, :, :]
                act.wait_ge(clamped, 1)
                act.activation(sn, sn, ACT.Exp).then_inc(new_act, 1)
                act.wait_ge(new_act, 1)
                act.activation(sn, sn, ACT.Ln, bias=1.0).then_inc(new_act, 1)
                act.wait_ge(arg_ready, 1)
                act.activation(wn, wn, ACT.Exp).then_inc(new_act, 1)
                with act.Fori(0, NSEQ // 2) as i:
                    for u in range(2):
                        seq = i * 2 + u
                        x = soft[:, u, :, :]
                        act.wait_ge(clamped, seq + 2)
                        act.activation(x, x, ACT.Exp).then_inc(exped, 1)
                        act.wait_ge(exped, seq + 1)
                        act.activation(x, x, ACT.Ln, bias=1.0).then_inc(logged, 1)
                        act.wait_ge(arg_ready, seq + 2)
                        act.activation(z[:, u, :, :], z[:, u, :, :], ACT.Exp).then_inc(w_ready, 1)
                        act.wait_ge(op_done, seq + 3)
                        for g in range(2):
                            rows = slice(g * HD, (g + 1) * HD)
                            src = os_[rows, u, 0:TS].rearrange("p (c g l) -> p c g l", g=2, l=LS)
                            ins = act.copy(o[rows, :, bass.ds(seq * LS, LS)], src[:, :, g, :])
                        ins.then_inc(o_taken, 1)


def ssd_phase(nc, a, s, sem):
    with ExitStack() as ctx:
        def sb(name, shape):
            return ctx.enter_context(nc.sbuf_tensor(name, shape, F32))

        def ps(name, cols):
            return ctx.enter_context(nc.psum_tensor(name, [P, cols], F32))

        NX = CONV // P
        PER_G = SH // NG
        xc = sb("xc", [P, 2, NX, P])
        zc = sb("zc", [P, 2, KC, P])
        st = sb("st", [P, D])
        dta = sb("dta", [P, TILES + 1, SH])
        neg_a = sb("neg_a", [P, SH])
        dt_c = sb("dt_c", [P, SH])
        dta_c = sb("dta_c", [P, SH])
        acs = sb("acs", [P, SH])
        xdt = sb("xdt", [P, SH, SP_])
        xend = sb("xend", [P, SH, SP_])
        btok = sb("btok", [P, NG, NST])
        cbm = sb("cbm", [P, NG, P])
        seg = sb("seg", [P, SH, P])
        grow = sb("grow", [P, SH, P])
        end = sb("end", [P, SH])
        decay = sb("decay", [P, SH])
        xt_ps = ps("xt_ps", 1024)
        bc_ps, acs_ps, ab_ps = ps("bc_ps", 512), ps("acs_ps", 512), ps("ab_ps", 2048)
        y_ps, st_ps = xt_ps, ab_ps
        in_ = [sem(f"ssd_in{u}") for u in range(2)]
        dta_done, dt_ready, head_done, spread = sem("dta_done"), sem("dt_ready"), sem("head_done"), sem("spread")
        seg_ready, grown, seg_exp, tail_in, y_done, st_done, taken = (
            sem("seg_ready"), sem("grown"), sem("seg_exp"), sem("tail_in"), sem("y_done"), sem("st_done"),
            sem("ssd_taken"))
        b_ready = sem("b_ready")
        dt_act = sem("dt_act")
        chain = sem("ssd_chain")
        h0_in, st_out = [sem(f"h0_in{u}") for u in range(2)], [sem(f"st_out{u}") for u in range(2)]
        last_out = sem("last_out")
        own_b, s_free = sem("own_b"), sem("s_free")
        const, par = s["const"], s["par"]
        ident = const[:, C_ID:C_ID + P]
        h0 = sb("h0", [P, 2, D])
        bseq = sb("bseq", [P, 2, NG, NST])
        growth = sb("growth", [P, SH, NSEQ])
        ring = sb("ada_rest", [P, RING, KC, P])
        mod_ps = acs_ps[:, P:P + RING * (1 + NSEQ)].rearrange("p (c q) -> p c q", c=RING)
        ada_in, mod_summed = sem("ada_rest_in"), sem("mod_rest_summed")
        h1 = sb("h1", [P, 2, D])

        def heads(t, g):
            return t[:, g * PER_G:(g + 1) * PER_G, :]

        with nc.Block() as block:
            @block.sync
            def _(sp):
                def load(chunk, u):
                    cols = bass.ds(chunk * P, P)
                    x_rows = a["proj"][CH_X:CH_X + NX].rearrange("c p t -> p c t")
                    z_rows = a["proj"][CH_Z:CH_Z + KC].rearrange("c p t -> p c t")
                    sp.dma_start(xc[:, u, :, :], x_rows[:, :, cols]).then_inc(in_[u], 16)
                    sp.dma_start(zc[:, u, :, :], z_rows[:, :, cols]).then_inc(in_[u], 16)

                with sp.Fori(0, TILES // 2) as i:
                    for u in range(2):
                        sp.wait_ge(taken, i * 2 + u + 1)
                        load(i * 2 + u, u)
                        sp.wait_ge(mod_summed, i * 2 + u + 1)
                        src = a["w_ada"][bass.ds(i * (2 * RING) + (u * RING + MOD_FIRST), RING)]
                        sp.dma_start(ring[:, :, :, :], src.rearrange("c p k m -> p c k m")).then_inc(ada_in, 16)
                sp.wait_ge(taken, TILES + 1)
                sp.dma_start(xc[:, 0, :, 0:TS],
                             a["proj"][CH_X:CH_X + NX].rearrange("c p t -> p c t")[:, :, SEQ:T]).then_inc(in_[0], 16)
                sp.dma_start(zc[:, 0, :, 0:TS],
                             a["proj"][CH_Z:CH_Z + KC].rearrange("c p t -> p c t")[:, :, SEQ:T]).then_inc(in_[0], 16)
                sp.wait_ge(taken, TILES + 2)
                sp.dma_start(a["ssm_out"][0], st[:, :]).then_inc(last_out, 16)
                for q in range(NSEQ):
                    if q >= 2:
                        sp.wait_ge(s_free, q - 1)
                    sp.dma_start(h0[:, q % 2, :], a["state_ssm"][q]).then_inc(h0_in[q % 2], 16)
                    if q >= 1:
                        sp.wait_ge(s_free, q)
                        sp.dma_start(a["ssm_out"][q], h1[:, (q - 1) % 2, :]).then_inc(st_out[(q - 1) % 2], 16)
                sp.wait_ge(s_free, NSEQ)
                sp.dma_start(a["ssm_out"][NSEQ], h1[:, (NSEQ - 1) % 2, :]).then_inc(st_out[(NSEQ - 1) % 2], 16)
                for u in range(2):
                    sp.wait_ge(st_out[u], 16 * (NSEQ // 2))
                sp.wait_ge(last_out, 16)

            @block.tensor
            def _(pe):
                def first(chunk, n, u, tri, loads):
                    x = xc[:, u, :, 0:n]
                    pe.wait_ge(in_[u], loads)
                    pe.wait_ge(taken, chunk + 2)
                    for c in range(KC):
                        mm = pe.transpose(xt_ps[0:n, c * P:(c + 1) * P], x[:, c, :], ident)
                    mm.then_inc(head_done, 1)
                    for g in range(NG):
                        pe.transpose(bc_ps[0:n, g * NST:(g + 1) * NST], x[:, KC + g, :], ident)
                        mm = pe.matmul(bc_ps[0:n, 256 + g * P:256 + g * P + n], x[:, KC + g, :],
                                       x[:, KC + NG + g, :], start=True, stop=True)
                    mm.then_inc(head_done, 1)
                    pe.wait_ge(dt_ready, chunk + 1)
                    pe.matmul(acs_ps[0:n, 0:SH], tri[0:n, 0:n], dta_c[0:n, :], start=True,
                              stop=True).then_inc(head_done, 1)
                    for h in range(SH):
                        mm = pe.matmul(ab_ps[:, h * P:h * P + n], dta_c[0:n, h:h + 1].to_broadcast([n, P]),
                                       tri[0:n, 0:n], start=True, stop=True)
                        if h % 4 == 3:
                            mm.then_inc(spread, 1)

                def part_of_mod(chunks):
                    for c in chunks:
                        for k in range(KC):
                            mm = pe.matmul(mod_ps[:, c, :], ring[:, c, k, :], s["cond_act"][:, k, :],
                                           start=(k == 0), stop=(k == KC - 1))
                    return mm

                pe.sem_inc(mod_summed, 1)
                with pe.Fori(0, TILES // 2) as i:
                    for u in range(2):
                        chunk = i * 2 + u
                        first(chunk, P, u, const[:, C_TRI:C_TRI + P], (i + 1) * 32)
                        pe.wait_ge(ada_in, chunk * 16 + 16)
                        pe.wait_ge(seg_ready, chunk + 1)
                        part_of_mod(range(RING // 2))
                        pe.wait_ge(tail_in, chunk + 1)
                        for h in range(SH):
                            rows, c = (h % 2) * SP_, h // 2
                            out = y_ps[rows:rows + SP_, c * P:(c + 1) * P]
                            pe.matmul(out, xdt[:, h, :], seg[:, h, :], start=True, stop=False)
                            mm = pe.matmul(out, st[:, h * SP_:(h + 1) * SP_], grow[:, h, :], start=False, stop=True)
                        mm.then_inc(y_done, 1)
                        for g in range(NG):
                            mm = pe.matmul(st_ps[:, g * 512:(g + 1) * 512], btok[:, g, :], heads(xend, g),
                                           start=True, stop=True)
                        mm.then_inc(st_done, 1)
                        part_of_mod(range(RING // 2, RING)).then_inc(mod_summed, 1)
                n = TS
                first(TILES, n, 0, const[:, C_BTRI:C_BTRI + TS], TILES // 2 * 32 + 32)
                pe.wait_ge(tail_in, TILES + 1)
                for h in range(SH):
                    rows, c = (h % 2) * SP_, h // 2
                    pe.matmul(y_ps[rows:rows + SP_, c * P:c * P + n], xdt[0:n, h, :], seg[0:n, h, 0:n],
                              start=(c % 4 == 0), stop=True, skip_group_check=True)
                for q in range(NSEQ):
                    pe.wait_ge(h0_in[q % 2], 16 * (q // 2 + 1))
                    for h in range(SH):
                        rows, c = (h % 2) * SP_, h // 2
                        mm = pe.matmul(y_ps[rows:rows + SP_, c * P + q * LS:c * P + (q + 1) * LS],
                                       h0[:, q % 2, h * SP_:(h + 1) * SP_], grow[:, h, q * LS:(q + 1) * LS],
                                       start=False, stop=True, skip_group_check=True)
                    if q == NSEQ - 1:
                        mm.then_inc(y_done, 1)
                    pe.wait_ge(own_b, q + 1)
                    if q:
                        pe.wait_ge(s_free, q)
                    for g in range(NG):
                        mm = pe.matmul(st_ps[:, g * 512:(g + 1) * 512], bseq[0:n, q % 2, g, :],
                                       heads(xend, g)[0:n], start=True, stop=True)
                    mm.then_inc(st_done, 1)

            @block.scalar
            def _(act):
                act.wait_ge(dta_done, 1)
                for x in (s["dt_tok"][:, 0:TILES, :], s["dt_tok"][0:TS, TILES, :]):
                    act.activation(x, x, ACT.Exp)
                act.activation(neg_a[:, :], par[:, W_AL:W_AL + SH], ACT.Exp).then_inc(dt_act, 1)
                act.wait_ge(dt_act, 1)
                act.activation(s["dt_tok"][:, 0:TILES, :], s["dt_tok"][:, 0:TILES, :], ACT.Ln, bias=1.0)
                act.activation(s["dt_tok"][0:TS, TILES, :], s["dt_tok"][0:TS, TILES, :], ACT.Ln,
                               bias=1.0).then_inc(dt_act, 1)

                def middle(chunk, n):
                    act.wait_ge(head_done, chunk * 3 + 2)
                    act.copy(btok[0:n, :, :],
                             bc_ps[0:n, 0:256].rearrange("p (g k) -> p g k", g=NG)).then_inc(b_ready, 1)
                    for b in range(4):
                        act.wait_ge(spread, chunk * 4 + b + 1)
                        src = ab_ps[:, b * 512:(b + 1) * 512].rearrange("p (h i) -> p h i", i=P)
                        act.activation(grow[:, b * 4:(b + 1) * 4, 0:n], src[:, :, 0:n], ACT.Exp).then_inc(grown, 1)
                    act.wait_ge(seg_ready, chunk + 1)
                    act.activation(seg[0:n, :, 0:n], seg[0:n, :, 0:n], ACT.Exp).then_inc(seg_exp, 1)

                with act.Fori(0, TILES // 2) as i:
                    for u in range(2):
                        middle(i * 2 + u, P)
                middle(TILES, TS)

            @block.vector
            def _(dve):
                link = Chain(dve, chain)
                dve.sem_inc(taken, 2)
                link.mark(dve.memset(st[:, :], 0.0))
                dve.tensor_copy(dta[:, 0:TILES, :], s["dt_tok"][:, 0:TILES, :])
                link.link(dve.tensor_copy(dta[0:TS, TILES, :], s["dt_tok"][0:TS, TILES, :]))
                dve.tensor_scalar(s["dt_tok"][:, 0:TILES, :], dta[:, 0:TILES, :], CLAMP, None, ALU.min)
                dve.tensor_scalar(s["dt_tok"][0:TS, TILES, :], dta[0:TS, TILES, :], CLAMP, None,
                                  ALU.min).then_inc(dta_done, 1)
                dve.wait_ge(dt_act, 2)
                for rows, t in ((P, slice(0, TILES)), (TS, slice(TILES, TILES + 1))):
                    dt = s["dt_tok"][0:rows, t, :]
                    link.link(dve.tensor_tensor(dt, dt, dta[0:rows, t, :], ALU.max))
                    w = neg_a[0:rows, :].unsqueeze(1).to_broadcast([rows, t.stop - t.start, SH])
                    link.link(dve.scalar_tensor_tensor(dta[0:rows, t, :], dt, -1.0, w, ALU.mult, ALU.mult))

                def start(chunk, n, u, tri):
                    at = bass.ds(chunk, 1) if not isinstance(chunk, int) else slice(chunk, chunk + 1)
                    dve.tensor_copy(dt_c[0:n, :], s["dt_tok"][0:n, at, :].rearrange("p o h -> p (o h)"))
                    dve.tensor_copy(dta_c[0:n, :],
                                    dta[0:n, at, :].rearrange("p o h -> p (o h)")).then_inc(dt_ready, 1)
                    dve.wait_ge(dt_ready, chunk + 1)
                    dve.wait_ge(head_done, chunk * 3 + 1)
                    for g in range(NG):
                        link.mark(dve.tensor_tensor(
                            heads(xdt, g)[0:n],
                            xt_ps[0:n, g * 512:(g + 1) * 512].rearrange("p (h k) -> p h k", k=SP_),
                            dt_c[0:n, g * PER_G:(g + 1) * PER_G].unsqueeze(2).to_broadcast([n, PER_G, SP_]),
                            ALU.mult))
                    dve.wait_ge(b_ready, chunk + 1)
                    cb = bc_ps[0:n, 256:512].rearrange("p (g i) -> p g i", g=NG)[:, :, 0:n]
                    link.mark(dve.tensor_tensor(cbm[0:n, :, 0:n], cb,
                                                tri[0:n, 0:n].unsqueeze(1).to_broadcast([n, NG, n]), ALU.mult))
                    dve.wait_ge(head_done, chunk * 3 + 3)
                    link.link(dve.tensor_copy(acs[0:n, :], acs_ps[0:n, 0:SH]))
                    for h in range(SH):
                        if h % 4 == 0:
                            dve.wait_ge(grown, chunk * 4 + h // 4 + 1)
                        ins = dve.tensor_scalar(seg[0:n, h, 0:n], ab_ps[0:n, h * P:h * P + n], acs[0:n, h:h + 1],
                                                0.0, ALU.subtract, ALU.min)
                    ins.then_inc(seg_ready, 1)

                def scale(chunk, n, u):
                    if n == P:
                        link.link(dve.tensor_copy(decay[:, :], grow[:, :, P - 1]))
                    else:
                        own = grow[:, :, 0:n].rearrange("p h (q l) -> p h q l", l=LS)[:, :, :, LS - 1]
                        link.link(dve.tensor_copy(growth[:, :, :], own))
                    for g in range(NG):
                        ct = xc[:, u, KC + NG + g, 0:n].unsqueeze(1).to_broadcast([P, PER_G, n])
                        x = heads(grow, g)[:, :, 0:n]
                        link.mark(dve.tensor_tensor(x, x, ct, ALU.mult))
                    dve.wait_ge(seg_exp, chunk + 1)

                def kernel_(n):
                    for g in range(NG):
                        x = heads(seg, g)[0:n, :, 0:n]
                        link.mark(dve.tensor_tensor(
                            x, x, cbm[0:n, g, 0:n].unsqueeze(1).to_broadcast([n, PER_G, n]), ALU.mult))

                def close(chunk, t, n, u):
                    y = s["y"][:, :, t]
                    for c in range(KC):
                        ins = dve.scalar_tensor_tensor(y[:, c, :], xc[:, u, c, 0:n],
                                                       par[:, W_DSKIP + c:W_DSKIP + c + 1],
                                                       y_ps[:, c * P:c * P + n], ALU.mult, ALU.add)
                    link.link(ins)
                    dve.tensor_tensor(y, y, zc[:, u, :, 0:n], ALU.mult).then_inc(taken, 1)

                with dve.Fori(0, TILES // 2) as i, link.turns(i, TILES // 2, 2 * 14):
                    for u in range(2):
                        chunk = i * 2 + u
                        start(chunk, P, u, const[:, C_TRI:C_TRI + P])
                        scale(chunk, P, u)
                        link.link(dve.tensor_copy(end[:, :], seg[:, :, P - 1]))
                        kernel_(P)
                        dve.tensor_tensor(xend[:, :, :], xdt[:, :, :],
                                          end[:, :].unsqueeze(2).to_broadcast([P, SH, SP_]),
                                          ALU.mult).then_inc(tail_in, 1)
                        dve.wait_ge(st_done, chunk + 1)
                        st3 = st[:, :].rearrange("p (h k) -> p h k", k=SP_)
                        link.link(dve.tensor_tensor(st3, st3,
                                                    decay[:, :].unsqueeze(2).to_broadcast([P, SH, SP_]), ALU.mult))
                        dve.wait_ge(y_done, chunk + 1)
                        ins = dve.tensor_tensor(st[:, 0:512], st[:, 0:512], st_ps[:, 0:512], ALU.add)
                        link.mark(ins)
                        link.mark(dve.tensor_tensor(st[:, 512:], st[:, 512:], st_ps[:, 512:1024], ALU.add))
                        dve.wait_ge(mod_summed, chunk + 2)
                        at = i * (2 * RING) + (u * RING + MOD_FIRST)
                        offset = s["par"][:, bass.ds(at + W_BADA, RING)].unsqueeze(2)
                        dve.tensor_tensor(s["mod"][:, bass.ds(at, RING), :], mod_ps,
                                          offset.to_broadcast([P, RING, 1 + NSEQ]), ALU.add)
                        close(chunk, bass.ds(chunk * P, P), P, u)
                n = TS
                start(TILES, n, 0, const[:, C_BTRI:C_BTRI + TS])
                scale(TILES, n, 0)
                last = seg[0:n, :, 0:n].rearrange("p h (q l) -> p h q l", l=LS)[:, :, :, LS - 1]
                pick = h1[0:n, 0, 0:SH * NSEQ].rearrange("p (h q) -> p h q", q=NSEQ)
                mask = const[0:n, C_SEQ:C_SEQ + NSEQ]
                link.link(dve.tensor_tensor(pick, last, mask.unsqueeze(1).to_broadcast([n, SH, NSEQ]), ALU.mult))
                link.link(dve.tensor_reduce(end[0:n, :], pick, AX.X, ALU.add))
                kernel_(n)
                dve.tensor_tensor(xend[0:n, :, :], xdt[0:n, :, :],
                                  end[0:n, :].unsqueeze(2).to_broadcast([n, SH, SP_]), ALU.mult).then_inc(tail_in, 1)
                for q in range(NSEQ):
                    slot = q % 2
                    if q >= 2:
                        dve.wait_ge(st_done, TILES + q - 1)
                        dve.wait_ge(st_out[slot], 16 * (q // 2))
                    dve.tensor_scalar(bseq[0:n, slot, :, :], btok[0:n, :, :], mask[:, q:q + 1], None,
                                      ALU.mult).then_inc(own_b, 1)
                    dve.wait_ge(h0_in[slot], 16 * (q // 2 + 1))
                    link.link(dve.tensor_tensor(
                        h1[:, slot, :].rearrange("p (h k) -> p h k", k=SP_),
                        h0[:, slot, :].rearrange("p (h k) -> p h k", k=SP_),
                        growth[:, :, q].unsqueeze(2).to_broadcast([P, SH, SP_]), ALU.mult))
                    dve.wait_ge(st_done, TILES + q + 1)
                    dve.tensor_tensor(h1[:, slot, :], h1[:, slot, :], st_ps[:, 0:1024], ALU.add).then_inc(s_free, 1)
                dve.wait_ge(y_done, TILES + 1)
                close(TILES, slice(SEQ, T), n, 0)
                dve.wait_ge(taken, TILES + 3)


def add_gated(dve, link, dst, gate, src, src_sample, spare):
    for t0, ap in src:
        n = ap.shape[-1]
        dve.scalar_tensor_tensor(dst[:, t0:t0 + n], ap, gate[:, 0:1], dst[:, t0:t0 + n], ALU.mult, ALU.add)
    own = dst[:, SEQ:T].rearrange("p (q l) -> p q l", l=LS)
    g = gate[:, 1:].unsqueeze(2).to_broadcast([P, NSEQ, LS])
    link.link(dve.tensor_tensor(spare, src_sample.rearrange("p (q l) -> p q l", l=LS), g, ALU.mult))
    return dve.tensor_tensor(own, own, spare, ALU.add)


def merge_phase(nc, a, s, sem):
    with ExitStack() as ctx:
        def sb(name, shape):
            return ctx.enter_context(nc.sbuf_tensor(name, shape, F32))

        NA = AW // P
        o = sb("o_all", [P, NA, T])
        wa = sb("wa", [P, 2, NA, P])
        wb = sb("wb", [P, 2, KC, P])
        gates = sb("gates", [P, 2, 2, T])
        part = sb("part", [P, NS, 384])
        spare = sb("spare", [P, 2, NSEQ, LS])
        ps = ctx.enter_context(nc.psum_tensor("merge_ps", [P, 2 * NS, 512], F32))
        o_in = sem("o_in")
        br_in = [sem(f"br_in{u}") for u in range(2)]
        out_in = [sem(f"out_in{u}") for u in range(2)]
        y_ready, br_done, br_taken, parted = sem("y_ready"), sem("br_done"), sem("br_taken"), sem("parted")
        mix_done, mix_taken, x_out, h_scaled = sem("mix_done"), sem("mix_taken"), sem("x_out"), sem("h2_scaled")
        banks_taken = sem("banks_taken")
        chain = sem("merge_chain")
        y, h, x = s["y"], s["h"], s["x"]
        HALF_C = KC // NG
        group = [Norm(nc, sem, f"group{g}", y[:, g * HALF_C:(g + 1) * HALF_C, :],
                      h[:, g * HALF_C:(g + 1) * HALF_C, :], s, ps, HALF_C) for g in range(NG)]
        norm = Norm(nc, sem, "norm2", x, y, s, ps)

        with nc.Block() as block:
            @block.sync
            def _(sp):
                sp.dma_start(o[:, :, :], a["o"].rearrange("(c p) t -> p c t", p=P)).then_inc(o_in, 16)

                def branch(m, u):
                    sp.dma_start(wa[:, u, :, :], a["w_attn"][m]).then_inc(br_in[u], 16)
                    sp.dma_start(wb[:, u, :, :], a["w_ssm"][m]).then_inc(br_in[u], 16)
                    sp.dma_start(gates[:, u, 0, :], a["proj"][m + CH_G]).then_inc(br_in[u], 16)
                    sp.dma_start(gates[:, u, 1, :], a["proj"][m + (CH_G + KC)]).then_inc(br_in[u], 16)

                for u in range(2):
                    branch(u, u)
                with sp.Fori(1, KC // 2) as i:
                    for u in range(2):
                        sp.wait_ge(br_taken, (i - 1) * (2 * NS) + (u + 1) * NS)
                        branch(i * 2 + u, u)
                for u in range(2):
                    sp.wait_ge(br_taken, (KC - 2 + u + 1) * NS)
                    sp.dma_start(wb[:, u, :, :], a["w_out"][u]).then_inc(out_in[u], 16)
                with sp.Fori(1, KC // 2) as i:
                    for u in range(2):
                        sp.wait_ge(mix_done, (i - 1) * (2 * NS) + (u + 1) * NS)
                        sp.dma_start(wb[:, u, :, :], a["w_out"][i * 2 + u]).then_inc(out_in[u], 16)
                sp.wait_ge(mix_taken, KC + 2)
                sp.dma_start(a["x_mid"], x[:, :, :]).then_inc(x_out, 16)
                sp.wait_ge(x_out, 16)

            @block.tensor
            def _(pe):
                group[0].tensor(pe)
                pe.wait_ge(y_ready, 1)
                group[1].tensor(pe)
                pe.wait_ge(y_ready, 2)
                pe.wait_ge(o_in, 16)
                with pe.Fori(0, KC // 2) as i:
                    for u in range(2):
                        pe.wait_ge(br_in[u], (i + 1) * 64)
                        for j, (t0, n) in enumerate(SPLITS):
                            pe.wait_ge(banks_taken, i * (2 * NS) + u * NS + j + 1)
                            for k in range(NA):
                                pe.matmul(ps[:, j, 0:n], wa[:, u, k, :], o[:, k, t0:t0 + n],
                                          start=(k == 0), stop=(k == NA - 1))
                            for k in range(KC):
                                mm = pe.matmul(ps[:, NS + j, 0:n], wb[:, u, k, :], y[:, k, t0:t0 + n],
                                               start=(k == 0), stop=(k == KC - 1))
                            mm.then_inc(br_done, 1)
                pe.wait_ge(br_taken, KC * NS)
                with pe.Fori(0, KC // 2) as i:
                    for u in range(2):
                        pe.wait_ge(out_in[u], (i + 1) * 16)
                        pe.wait_ge(mix_taken, i * 2 + u + 1)
                        for j, (t0, n) in enumerate(SPLITS):
                            for k in range(KC):
                                mm = pe.matmul(ps[:, u * NS + j, 0:n], wb[:, u, k, :], h[:, k, t0:t0 + n],
                                               start=(k == 0), stop=(k == KC - 1))
                            mm.then_inc(mix_done, 1)
                norm.tensor(pe)

            @block.scalar
            def _(act):
                group[0].scalar(act)
                act.wait_ge(y_ready, 1)
                group[1].scalar(act)
                act.wait_ge(mix_taken, KC + 2)
                norm.scalar(act)
                shifted(act, s, h, 3 * KC, h_scaled)

            @block.vector
            def _(dve):
                link = Chain(dve, chain)
                dve.sem_inc(banks_taken, NS)
                dve.sem_inc(mix_taken, 2)
                for g in range(NG):
                    group[g].vector(dve)
                    for c in range(g * HALF_C, (g + 1) * HALF_C):
                        ins = dve.scalar_tensor_tensor(y[:, c, :], y[:, c, :],
                                                       s["par"][:, W_SSM + c:W_SSM + c + 1],
                                                       s["rstd"][:, :], ALU.mult, ALU.mult)
                    ins.then_inc(y_ready, 1)
                with dve.Fori(0, KC // 2) as i:
                    for u in range(2):
                        dve.wait_ge(br_in[u], (i + 1) * 64)
                        for j, (t0, n) in enumerate(SPLITS):
                            dve.wait_ge(br_done, i * (2 * NS) + u * NS + j + 1)
                            hm = h[:, bass.ds(i * 2 + u, 1), t0:t0 + n].rearrange("p o t -> p (o t)")
                            dve.tensor_tensor(part[:, j, 0:n], ps[:, j, 0:n],
                                              gates[:, u, 0, t0:t0 + n], ALU.mult)
                            ins = dve.tensor_tensor(hm, ps[:, NS + j, 0:n], gates[:, u, 1, t0:t0 + n], ALU.mult)
                            ins.then_inc(banks_taken, 1)
                            dve.wait_ge(banks_taken, i * (2 * NS) + u * NS + j + 1 + NS)
                            dve.tensor_tensor(hm, hm, part[:, j, 0:n], ALU.add).then_inc(br_taken, 1)
                with dve.Fori(0, KC // 2) as i, link.turns(i, KC // 2, 2):
                    for u in range(2):
                        m = i * 2 + u
                        dve.wait_ge(mix_done, i * (2 * NS) + (u + 1) * NS)
                        gate = s["mod"][:, bass.ds(m + 2 * KC, 1), :].rearrange("p o q -> p (o q)")
                        xm = x[:, bass.ds(m, 1), :].rearrange("p o t -> p (o t)")
                        src = [(t0, ps[:, u * NS + j, 0:min(n, SEQ - t0)]) for j, (t0, n) in enumerate(SPLITS)]
                        t0, n = SPLITS[-1]
                        add_gated(dve, link, xm, gate, src, ps[:, u * NS + NS - 1, SEQ - t0:n],
                                  spare[:, u, :, :]).then_inc(mix_taken, 1)
                norm.vector(dve)
                modulated(dve, link.link, s, x, h, W_N2, 3 * KC, 4 * KC, h_scaled)


def route_phase(nc, a, s, sem):
    with ExitStack() as ctx:
        def sb(name, shape, dt=F32):
            return ctx.enter_context(nc.sbuf_tensor(name, shape, dt))

        NT = TILES + 1
        K2 = 2 * EH
        HK = EH * TOPK
        sc = sb("sc_tile", [P, K2, NK])
        rest = sb("sc_rest", [P, K2, NK])
        top = sb("top", [P, K2, TOPK])
        top_i = sb("top_i", [P, K2, TOPK], U32)
        top_f = sb("top_f", [P, K2, TOPK], F16)
        FEW = 4
        NFIRST = FEW * TOPK
        NCAND = NFIRST + (TOPK - FEW) * FEW
        cand = sb("cand", [P, EH, NCAND])
        cand2 = sb("cand2", [P, EH, NCAND])
        val = sb("val", [P, EH, TOPK])
        flat = sb("flat", [P, EH, TOPK], U32)
        rank = sb("rank", [P, 5, HK], U32)
        rank_f = sb("rank_f", [P, 5, HK])
        hit = sb("hit", [P, 2, HK, TOPK], F16)
        pick = sb("pick", [P, 3, HK])
        total = sb("total", [P, EH])
        wq = sb("wq", [P, K2, KC, P])
        keys = sb("keys", [P, 2, NK])
        qh = sb("qh", [P, 4, P])
        pick_ps = ctx.enter_context(nc.psum_tensor("pick_ps", [P, 512], F32))
        q_ps = ctx.enter_context(nc.psum_tensor("query_ps", [P, 2, 512], F32))
        sc_ps = ctx.enter_context(nc.psum_tensor("score_ps", [P, 4, 512], F32))
        keys_in = sem("keys_in")
        wq_in = [sem(f"wq_in{b}") for b in range(4)]
        q_done, q_taken, sc_done, sc_taken = sem("q_done"), sem("q_taken"), sem("sc_done"), sem("sc_taken")
        tile_read, chain, val_ready, val_exp, picked, turned, kept, top_ready, hits = (
            sem("tile_read"), sem("select_chain"), sem("val_ready"), sem("val_exp"),
            sem("picked"), sem("turned"), sem("kept"), sem("top_ready"), sem("hits"))
        passed = sem("select_passed")
        cleared = sem("scores_cleared")
        h = s["h"]
        const = s["const"]
        ident = const[:, C_ID:C_ID + P]
        lane = const[:, C_IOTA:C_IOTA + TOPK].unsqueeze(1).to_broadcast([P, HK, TOPK])
        LOW = -3.0e38

        with nc.Block() as block:
            @block.sync
            def _(sp):
                sp.dma_start(keys[:, :, :], a["keys"]).then_inc(keys_in, 16)
                for b in range(4):
                    src = a["w_query"][b * 4:(b + 1) * 4].rearrange("c p k m -> p c k m")
                    sp.dma_start(wq[:, b * 4:(b + 1) * 4, :, :], src).then_inc(wq_in[b], 16)

            @block.vector
            def _(dve):
                link = Chain(dve, chain, passed)
                dve.sem_inc(tile_read, 1)
                link.link(dve.memset(sc[:, :, :], 0.0))
                dve.sem_inc(cleared, 1)
                link.link(dve.tensor_reduce(s["h_top"][:, :], h[:, :, :].rearrange("p k t -> p (k t)"), AX.X,
                                            ALU.max, apply_absolute_value=True))
                with dve.Fori(0, NT) as t, link.turns(t, NT, 18):
                    def top16(src, left, vals, idx, n, last=None, before=None):
                        for c in range(n):
                            if before:
                                before(c)
                            ins = dve.max(vals[:, c, 0:8], src[:, c, :])
                        link.link_apart(ins)
                        for c in range(n):
                            dve.max_index(idx[:, c, 0:8], vals[:, c, 0:8], src[:, c, :])
                            ins = dve.match_replace(left[:, c, :], vals[:, c, 0:8], src[:, c, :], LOW)
                        link.link_apart(ins)
                        if last is not None:
                            last()
                        for c in range(n):
                            ins = dve.max(vals[:, c, 8:16], left[:, c, :])
                        link.link_apart(ins)
                        for c in range(n):
                            ins = dve.max_index(idx[:, c, 8:16], vals[:, c, 8:16], left[:, c, :])
                        link.link(ins)

                    def bank(c):
                        if c % 4 == 0:
                            dve.wait_ge(sc_taken, t * 4 + c // 4 + 1 + 4)
                            dve.sem_inc(passed, 1)

                    top16(sc, rest, top, top_i, K2, lambda: dve.sem_inc(tile_read, 1), bank)
                    dve.tensor_copy(top_f[:, :, :], top_i[:, :, :])
                    both = top[:, :, :].rearrange("p (h e) k -> p h e k", e=2)
                    def sums(out, a0, a1, b1):
                        n = a1 - a0
                        return dve.tensor_tensor(
                            out.rearrange("p h (x y) -> p h x y", y=b1),
                            both[:, :, 0, a0:a1].unsqueeze(3).to_broadcast([P, EH, n, b1]),
                            both[:, :, 1, 0:b1].unsqueeze(2).to_broadcast([P, EH, n, b1]), ALU.add)

                    sums(cand[:, :, 0:NFIRST], 0, FEW, TOPK)
                    link.link_apart(sums(cand[:, :, NFIRST:], FEW, TOPK, FEW))
                    top16(cand, cand2, val, flat, EH)
                    g = pick[:, 2, :].rearrange("p (h k) -> p h k", k=TOPK)
                    dve.tensor_tensor(g, val[:, :, :], val[:, :, 0:1].to_broadcast([P, EH, TOPK]),
                                      ALU.subtract).then_inc(val_ready, 1)
                    f = flat[:, :, :].rearrange("p h k -> p (h k)")
                    for n, (by, op) in enumerate(((4, ALU.logical_shift_right), (15, ALU.bitwise_and),
                                                  (2, ALU.logical_shift_right), (3, ALU.bitwise_and),
                                                  (6, ALU.logical_shift_right))):
                        ins = dve.tensor_scalar(rank[:, n, :], f, by, None, op)
                    link.link(ins)
                    link.link(dve.tensor_copy(rank_f[:, :, :], rank[:, :, :]))
                    second = rank_f[:, 2:4, :]
                    dve.scalar_tensor_tensor(rank_f[:, 2, :], rank_f[:, 2, :], FEW - NFIRST / FEW, rank_f[:, 0, :],
                                             ALU.add, ALU.subtract)
                    link.link(dve.tensor_tensor(rank_f[:, 3, :], rank_f[:, 3, :], rank_f[:, 1, :], ALU.subtract))
                    link.link(dve.tensor_tensor(second, second,
                                                rank_f[:, 4:5, :].to_broadcast([P, 2, HK]), ALU.mult))
                    link.link(dve.tensor_tensor(rank_f[:, 0:2, :], rank_f[:, 0:2, :], second, ALU.add))
                    for e in range(2):
                        ins = dve.tensor_tensor(hit[:, e, :, :],
                                                rank_f[:, e, :].unsqueeze(2).to_broadcast([P, HK, TOPK]), lane,
                                                ALU.is_equal)
                    link.link(ins)
                    place = top_f[:, :, :].rearrange("p (h e) k -> p h e k", e=2)
                    for e in range(2):
                        x = hit[:, e, :, :].rearrange("p (h k) j -> p h k j", k=TOPK)
                        ins = dve.tensor_tensor(x, x, place[:, :, e, :].unsqueeze(2).to_broadcast(
                            [P, EH, TOPK, TOPK]), ALU.mult)
                    link.link(ins)
                    dve.tensor_reduce(pick[:, 0:2, :], hit[:, :, :, :], AX.X, ALU.add)
                    dve.wait_ge(val_exp, t + 1)
                    link.link(dve.tensor_reduce(total[:, :], g, AX.X, ALU.add))
                    link.link(dve.reciprocal(total[:, :], total[:, :]))
                    dve.tensor_tensor(g, g, total[:, :].unsqueeze(2).to_broadcast([P, EH, TOPK]),
                                      ALU.mult).then_inc(picked, 1)
                    dve.wait_ge(turned, t + 1)

            @block.scalar
            def _(act):
                g = pick[:, 2, :]

                def scores(t, n):
                    for c in range(K2):
                        act.wait_ge(q_done, t * K2 + c + 1)
                        act.wait_ge(sc_done, t * K2 + c + 1)
                        act.copy(qh[:, c % 4, 0:n], q_ps[:, c % 2, 0:n]).then_inc(q_taken, 1)
                    act.wait_ge(tile_read, t + 1)
                    for b in range(4):
                        act.wait_ge(sc_done, t * K2 + 4 * (b + 1) + 4)
                        act.copy(sc[0:n, 4 * b:4 * (b + 1), :], sc_ps[0:n, b, :]).then_inc(sc_taken, 1)

                def gates(t):
                    act.wait_ge(val_ready, t + 1)
                    act.activation(g, g, ACT.Exp).then_inc(val_exp, 1)
                    act.wait_ge(turned, t + 1)
                    act.copy(s["choice"][:, :, bass.ds(t * P, P)] if not isinstance(t, int) else
                             s["choice"][:, :, t * P:(t + 1) * P],
                             pick_ps[:, 0:3 * P].rearrange("p (e c) -> p e c", c=P)).then_inc(kept, 1)

                act.sem_inc(q_taken, 2)
                act.sem_inc(sc_taken, 4)
                act.wait_ge(cleared, 1)
                scores(0, P)
                with act.Fori(0, TILES - 1) as t:
                    scores(t + 1, P)
                    gates(t)
                scores(TILES, TS)
                gates(TILES - 1)
                gates(TILES)

            @block.tensor
            def _(pe):
                def scores(t, n):
                    for c in range(K2 + 1):
                        if c < K2:
                            if isinstance(t, int) and t == 0 and c % 4 == 0:
                                pe.wait_ge(wq_in[c // 4], 16)
                            pe.wait_ge(q_taken, t * K2 + c + 1)
                            for k in range(KC):
                                rhs = h[:, k, t * P:t * P + n] if isinstance(t, int) else h[:, k, bass.ds(t * P, n)]
                                mm = pe.matmul(q_ps[:, c % 2, 0:n], wq[:, c, k, :], rhs,
                                               start=(k == 0), stop=(k == KC - 1))
                            mm.then_inc(q_done, 1)
                        if c > 0:
                            d = c - 1
                            pe.wait_ge(q_taken, t * K2 + d + 1 + 2)
                            if d % 4 == 0:
                                pe.wait_ge(sc_taken, t * 4 + d // 4 + 1)
                            pe.matmul(sc_ps[0:n, d // 4, (d % 4) * NK:(d % 4 + 1) * NK], qh[:, d % 4, 0:n],
                                      keys[:, d % 2, :], start=True, stop=True).then_inc(sc_done, 1)

                def turn(t):
                    pe.wait_ge(picked, t + 1)
                    pe.wait_ge(kept, t + 1)
                    for e in range(3):
                        mm = pe.transpose(pick_ps[:, e * P:(e + 1) * P], pick[:, e, :], ident)
                    mm.then_inc(turned, 1)

                pe.sem_inc(sc_done, 4)
                pe.sem_inc(kept, 1)
                pe.wait_ge(keys_in, 16)
                scores(0, P)
                with pe.Fori(0, TILES - 1) as t:
                    scores(t + 1, P)
                    turn(t)
                scores(TILES, TS)
                turn(TILES - 1)
                turn(TILES)


def weights_phase(nc, a, s, sem):
    NQ = 4
    PER = 2 * TB
    NG4 = PER // NQ
    POOL_ROWS = 2
    with ExitStack() as ctx:
        def sb(name, shape):
            return ctx.enter_context(nc.sbuf_tensor(name, shape, F32))

        left = sb("left", [P, 4, NQ, NK])
        right = sb("right", [P, 4, NQ, NK])
        e1 = sb("e1", [P, PER])
        mine = sb("choice_v", [P, 3, PER])
        out = sb("w_stage", [P, 2, NK, TB])
        ps = ctx.enter_context(nc.psum_tensor("w_ps", [P, 8, 512], F32))
        pool_chain, dve_chain = sem("w_pool_chain"), sem("w_dve_chain")
        left_ready, right_ready, w_done, w_taken = (
            sem("left_ready"), sem("right_ready"), sem("w_done"), sem("w_taken"))
        w_out = [sem(f"w_out{u}") for u in range(2)]
        w_passed = sem("w_passed")
        away = sb("e1_distance", [P, 2, NK])
        act_e1 = sb("e1_a", [P, PER])
        away_ready, act_ready, act_e1_in = sem("away_ready"), sem("act_row_ready"), sem("act_e1_in")
        iota = s["const"][:, C_IOTA:C_IOTA + NK]

        with nc.Block() as block:
            @block.gpsimd
            def _(pool):
                link = Chain(pool, pool_chain)
                with pool.Fori(0, T // PER) as i, link.turns(i, T // PER, 1):
                    link.link(pool.tensor_copy(e1[:, :], s["choice"][:, 0, bass.ds(i * PER, PER)]))
                    for g in range(NG4):
                        pool.wait_ge(w_done, i * NG4 + g + 1)
                        pool.sem_inc(w_passed, 1)
                        for n in range(POOL_ROWS):
                            t = g * NQ + n
                            ins = pool.tensor_scalar(left[:, g % 4, n, :], iota, e1[:, t:t + 1], None,
                                                     ALU.is_equal)
                        ins.then_inc(left_ready, 1)
                    pool.wait_ge(left_ready, (i + 1) * NG4)

            @block.vector
            def _(dve):
                link = Chain(dve, dve_chain)
                with dve.Fori(0, T // PER) as i, link.turns(i, T // PER, 1):
                    link.link(dve.tensor_copy(mine[:, :, :], s["choice"][:, :, bass.ds(i * PER, PER)]))
                    for g in range(NG4):
                        dve.wait_ge(w_done, i * NG4 + g + 1)
                        for n in range(POOL_ROWS, NQ - 1):
                            t = g * NQ + n
                            dve.tensor_scalar(left[:, g % 4, n, :], iota, mine[:, 0, t:t + 1], None,
                                              ALU.is_equal)
                        for n in range(NQ):
                            t = g * NQ + n
                            ins = dve.tensor_scalar(right[:, g % 4, n, :], iota, mine[:, 1, t:t + 1],
                                                    mine[:, 2, t:t + 1], ALU.is_equal, ALU.mult)
                        ins.then_inc(right_ready, 1)
                    dve.wait_ge(right_ready, (i + 1) * NG4)

            @block.tensor
            def _(pe):
                pe.sem_inc(w_done, 4)
                with pe.Fori(0, T // PER) as i:
                    for g in range(NG4):
                        pe.wait_ge(left_ready, i * NG4 + g + 1)
                        pe.wait_ge(right_ready, i * NG4 + g + 1)
                        pe.wait_ge(act_ready, i * NG4 + g + 1)
                        pe.wait_ge(w_taken, i * NG4 + g + 1)
                        for n in range(NQ):
                            mm = pe.matmul(ps[:, g % 8, n * NK:(n + 1) * NK], left[:, g % 4, n, :],
                                           right[:, g % 4, n, :], start=True, stop=True)
                        mm.then_inc(w_done, 1)

            @block.scalar
            def _(act):
                act.sem_inc(w_taken, 8)
                for u in range(2):
                    act.sem_inc(w_out[u], 16)

                def keep(i, g):
                    b = g * NQ // TB
                    if g * NQ % TB == 0:
                        act.wait_ge(w_out[b], (i + 1) * 16)
                    act.wait_ge(w_done, i * NG4 + g + 1 + 4)
                    t = g * NQ % TB
                    act.copy(out[:, b, :, t:t + NQ].rearrange("p e t -> p t e"),
                             ps[:, g % 8, :].rearrange("p (t e) -> p t e", e=NK)).then_inc(w_taken, 1)

                with act.Fori(0, T // PER) as i:
                    act.copy(act_e1[:, :], s["choice"][:, 0, bass.ds(i * PER, PER)]).then_inc(act_e1_in, 1)
                    act.wait_ge(act_e1_in, i + 1)
                    for g in range(NG4):
                        act.wait_ge(w_done, i * NG4 + g + 1)
                        t = g * NQ + NQ - 1
                        act.activation(away[:, g % 2, :], iota, ACT.Abs, scale=-1.0,
                                       bias=act_e1[:, t:t + 1]).then_inc(away_ready, 1)
                        act.wait_ge(away_ready, i * NG4 + g + 1)
                        act.activation(left[:, g % 4, NQ - 1, :], away[:, g % 2, :], ACT.Relu, scale=-1.0,
                                       bias=1.0).then_inc(act_ready, 1)
                        if g >= 2:
                            keep(i, g - 2)
                    keep(i, NG4 - 2)
                    keep(i, NG4 - 1)

            @block.sync
            def _(sp):
                with sp.Fori(0, T // PER) as i:
                    for b in range(2):
                        sp.wait_ge(w_taken, i * NG4 + (b + 1) * (NG4 // 2) + 8)
                        sp.dma_start(a["w"][i * 2 + b], out[:, b, :, :]).then_inc(w_out[b], 16)
                for b in range(2):
                    sp.wait_ge(w_out[b], 16 * (T // PER + 1))


def experts_phase(nc, a, s, sem):
    NB = 3
    with ExitStack() as ctx:
        def sb(name, shape, dt=F32):
            return ctx.enter_context(nc.sbuf_tensor(name, shape, dt))

        u = sb("u_chunks", [P, GRP, KC, P])
        v = sb("v_group", [P, GRP, D])
        w = sb("w_groups", [P, 2, NTB, GRP, TB])
        h16 = sb("h_parts", [P, 2, KC, T], F16)
        u16 = sb("u_parts", [P, 2, GRP, KC, P], F16)
        v16 = sb("v_parts", [P, 2, GRP, D], F16)
        a16 = sb("act_parts", [P, 2, GRP, T], F16)
        act_sb = sb("gelu", [P, NB, 384])
        act_top = sb("act_top", [P, GRP])
        dot_unit = sb("dot_unit", [P, 2])
        h_unit = sb("h_unit", [P, 1])
        sum_unit = sb("sum_unit", [P, 1])
        ps = ctx.enter_context(nc.psum_tensor("expert_ps", [P, 2, NS, 512], F32))
        scale_ps = ctx.enter_context(nc.psum_tensor("scale_ps", [P, 512], F32))
        u_in = [sem(f"u_in{j}") for j in range(GRP)]
        v_in = sem("v_in")
        w_in = [sem(f"wt_in{p}") for p in range(2)]
        dot_done, gelu_done, act_done, sum_done, sum_taken = (
            sem("dot_done"), sem("gelu_done"), sem("act_done"), sem("sum_done"), sem("sum_taken"))
        h_hi, u_hi, v_hi, a_hi = sem("h_hi"), sem("u_hi"), sem("v_hi"), sem("a_hi")
        h_split, u_split, v_split, a_split = sem("h_split"), sem("u_split"), sem("v_split"), sem("a_split")
        chain = sem("experts_chain")
        scales = Scales(nc, sb, sem, s, scale_ps)
        S_ACT, S_V, S_U = 0, 1, 2
        h, acc = s["h"], s["acc"]
        PER_A = GRP * NS
        PER_B = KC * NS
        LAST = NGRP - 1
        LOOPS = (NGRP - 4) // 2

        def tokens(slot, j, t0, n):
            return w[:, slot, t0 // TB:(t0 + n) // TB, j, :]

        def flat(x):
            return x.rearrange("p (b t) -> p b t", t=TB)

        def rounds(eng, body):
            with eng.Fori(0, LOOPS) as i:
                for p in range(2):
                    body(i * 2 + p, i, p, 0)
            for g in range(2 * LOOPS, NGRP):
                body(g, g // 2, g % 2, g)

        with nc.Block() as block:
            @block.sync
            def _(sp):
                def load_u(g, j):
                    sp.dma_start(u[:, j, :, :], a["u"][g * GRP + j]).then_inc(u_in[j], 16)

                def load_w(g, p):
                    cols = slice(g * GRP, (g + 1) * GRP) if isinstance(g, int) else bass.ds(g * GRP, GRP)
                    sp.dma_start(w[:, p, :, :, :],
                                 a["w"][:, :, cols, :].rearrange("b p e t -> p b (e t)")).then_inc(w_in[p], 16)

                for j in range(GRP):
                    load_u(0, j)
                load_w(0, 0)
                sp.dma_start(v[:, :, :], a["v"][0]).then_inc(v_in, 16)
                load_w(1, 1)
                for g in (1, 2):
                    for j in range(GRP):
                        sp.wait_ge(u_split, (g - 1) * GRP + j + 1)
                        load_u(g, j)

                def turn(g, i, p, at):
                    if at < LAST:
                        sp.wait_ge(v_split, (g + 1) * GRP)
                        sp.dma_start(v[:, :, :], a["v"][g + 1]).then_inc(v_in, 16)
                    if at < LAST - 1:
                        sp.wait_ge(a_split, (g + 1) * GRP)
                        load_w(g + 2, p)
                    if at < LAST - 2:
                        for j in range(GRP):
                            sp.wait_ge(u_split, (g + 2) * GRP + j + 1)
                            load_u(g + 3, j)

                rounds(sp, turn)

            @block.tensor
            def _(pe):
                def dot(g, c=None, at=0):
                    for j in range(GRP):
                        pe.wait_ge(u_split, g * GRP + j + 1)

                        def free(q):
                            if j >= 2:
                                pe.wait_ge(gelu_done, g * PER_A + (j - 2) * NS + q + 1)
                            elif at == 1:
                                pe.wait_ge(gelu_done, (g - 1) * PER_A + (j + 2) * NS + q + 1)
                            elif at != 0:
                                pe.wait_ge(sum_taken, (g - 2) * PER_B + (KC - 2 + j) * NS + q + 1)

                        for k in range(KC):
                            if at == 0 and j == 0:
                                pe.wait_ge(h_split, k + 1)
                            product(pe, lambda q: ps[:, j % 2, q, 0:SPLITS[q][1]],
                                    lambda x: u16[:, x, j, k, :],
                                    lambda y, t0, n: h16[:, y, k, t0:t0 + n],
                                    free if k == 0 else None, dot_done if k == KC - 1 else None)
                        if j == 0 and c is not None:
                            scales.turn(pe, c)
                        if j == 1 and c is not None:
                            scales.spread_out(pe, c)

                def total(g, at=0):
                    pe.wait_ge(v_split, (g + 1) * GRP)
                    pe.wait_ge(a_split, (g + 1) * GRP)
                    for m in range(KC):
                        def free(q):
                            if m >= 2:
                                pe.wait_ge(sum_taken, g * PER_B + (m - 2) * NS + q + 1)
                            elif at < LAST:
                                pe.wait_ge(gelu_done, (g + 1) * PER_A + (2 + m) * NS + q + 1)
                            else:
                                pe.wait_ge(sum_taken, (g - 1) * PER_B + (KC - 2 + m) * NS + q + 1)

                        for j in range(GRP):
                            product(pe, lambda q: ps[:, m % 2, q, 0:SPLITS[q][1]],
                                    lambda x: v16[:, x, j, m * P:(m + 1) * P],
                                    lambda y, t0, n: a16[:, y, j, t0:t0 + n],
                                    free if j == 0 else None, sum_done if j == GRP - 1 else None)

                scales.turn(pe, 0)
                scales.spread_out(pe, 0)
                dot(0, 1)
                dot(1, 2, 1)
                total(0)
                dot(2, 3, 2)
                total(1)
                with pe.Fori(1, LOOPS + 1) as i:
                    for p in range(2):
                        dot(i * 2 + (p + 1), i * 2 + (p + 2), 2)
                        total(i * 2 + p)
                dot(LAST, LAST + 1, 2)
                total(LAST - 1)
                scales.turn(pe, LAST + 2)
                scales.spread_out(pe, LAST + 2)
                total(LAST, LAST)

            @block.scalar
            def _(act):
                def scaled(out, src, n, done):
                    act.activation(out, src, ACT.Copy, scale=scales.value[:, n:n + 1]).then_inc(done, 1)

                def gelu(g, p, chunks):
                    for j in chunks:
                        for q, (t0, n) in enumerate(SPLITS):
                            act.wait_ge(dot_done, g * PER_A + j * NS + q + 1)
                            act.wait_ge(act_done, g * PER_A + j * NS + q + 1)
                            act.activation(act_sb[:, q, 0:n], ps[:, j % 2, q, 0:n], ACT.Gelu_apprx_tanh,
                                           scale=dot_unit[:, p:p + 1]).then_inc(gelu_done, 1)

                def split_u(g):
                    act.wait_ge(dot_done, g * PER_A)
                    for j in range(GRP):
                        scaled(u16[:, 0, j, :, :], u[:, j, :, :], S_U, u_hi)

                def turn(g, i, p, at):
                    if at < LAST:
                        gelu(g + 1, 1 - p, (0, 1))
                    act.wait_ge(scales.ready, g + 3)
                    if not isinstance(g, int) or g > 0:
                        act.wait_ge(sum_done, g * PER_B)
                    for j in range(GRP):
                        scaled(flat(a16[:, 0, j, :]), w[:, p, :, j, :], S_ACT, a_hi)
                    for j in range(GRP):
                        scaled(v16[:, 0, j, :], v[:, j, :], S_V, v_hi)
                    if at < LAST:
                        gelu(g + 1, 1 - p, (2, 3))
                    if at < LAST - 1:
                        split_u(g + 2)

                act.wait_ge(scales.ready, 1)
                scaled(u16[:, 0, 0, :, :], u[:, 0, :, :], S_U, u_hi)
                for k in range(KC):
                    scaled(h16[:, 0, k, :], h[:, k, :], S_ACT, h_hi)
                for j in range(1, GRP):
                    scaled(u16[:, 0, j, :, :], u[:, j, :, :], S_U, u_hi)
                gelu(0, 0, (0, 1, 2, 3))
                act.wait_ge(scales.ready, 2)
                split_u(1)
                turn(0, 0, 0, 0)
                turn(1, 0, 1, 0)
                with act.Fori(1, LOOPS) as i:
                    for p in range(2):
                        turn(i * 2 + p, i, p, 0)
                for g in range(2 * LOOPS, NGRP):
                    turn(g, g // 2, g % 2, g)

            @block.vector
            def _(dve):
                link = Chain(dve, chain)
                tops = scales.tops

                def largest(out, src, axis=AX.X):
                    link.mark(dve.tensor_reduce(out, src, axis, ALU.max, apply_absolute_value=True))

                def rest(out, src, n, hi, done):
                    dve.scalar_tensor_tensor(out, src, scales.value[:, n:n + 1], hi, ALU.mult,
                                             ALU.subtract).then_inc(done, 1)

                def weigh(g, i, p, j):
                    if j == 0:
                        dve.wait_ge(w_in[p], (i + 1) * 16)
                    for q, (t0, n) in enumerate(SPLITS):
                        dve.wait_ge(gelu_done, g * PER_A + j * NS + q + 1)
                        x = tokens(p, j, t0, n)
                        dve.tensor_tensor(x, x, flat(act_sb[:, q, 0:n]), ALU.mult).then_inc(act_done, 1)
                    dve.wait_ge(act_done, g * PER_A + (j + 1) * NS + NB)
                    largest(act_top[:, j:j + 1], w[:, p, :, j, :], AX.XY)

                def split_u(g, chunks=range(GRP)):
                    for j in chunks:
                        dve.wait_ge(u_hi, g * GRP + j + 1)
                        rest(u16[:, 1, j, :, :], u[:, j, :, :], S_U, u16[:, 0, j, :, :], u_split)

                def top_u(g):
                    for j in range(GRP):
                        dve.wait_ge(u_in[j], (g + 1) * 16)
                    largest(tops[:, S_U:S_U + 1], u[:, :, :, :].rearrange("p j k e -> p (j k e)"))

                def top_v(g):
                    dve.wait_ge(v_in, (g + 1) * 16)
                    largest(tops[:, S_V:S_V + 1], v[:, :, :].rearrange("p j d -> p (j d)"))

                def found(g=None):
                    if g is not None:
                        link.wait(link.base + link.n)
                        link.mark(dve.tensor_reduce(tops[:, S_ACT:S_ACT + 1], act_top[:, :], AX.X, ALU.max))
                    link.wait(link.base + link.n)
                    dve.sem_inc(scales.found, 1)

                def take(c, p):
                    scales.take(dve, link.link, c)
                    v_ = scales.value
                    link.mark(dve.tensor_tensor(dot_unit[:, p:p + 1], v_[:, 3 + S_U:4 + S_U], h_unit[:, :],
                                                ALU.mult))
                    link.link(dve.tensor_tensor(sum_unit[:, :], v_[:, 3 + S_ACT:4 + S_ACT],
                                                v_[:, 3 + S_V:4 + S_V], ALU.mult))
                    dve.sem_inc(scales.ready, 1)

                def add(g, chunks):
                    for m in chunks:
                        for q, (t0, n) in enumerate(SPLITS):
                            dve.wait_ge(sum_done, g * PER_B + m * NS + q + 1)
                            x = acc[:, m, t0:t0 + n]
                            dve.scalar_tensor_tensor(x, ps[:, m % 2, q, 0:n], sum_unit[:, :], x, ALU.mult,
                                                     ALU.add).then_inc(sum_taken, 1)

                def turn(g, i, p, at):
                    found(g)
                    scales.powers(dve, link.link, g + 2)
                    if at < LAST:
                        weigh(g + 1, i + p, 1 - p, 0)
                    take(g + 2, p)
                    for j in range(GRP):
                        dve.wait_ge(a_hi, g * GRP + j + 1)
                        rest(flat(a16[:, 1, j, :]), w[:, p, :, j, :], S_ACT, flat(a16[:, 0, j, :]), a_split)
                    for j in range(GRP):
                        dve.wait_ge(v_hi, g * GRP + j + 1)
                        rest(v16[:, 1, j, :], v[:, j, :], S_V, v16[:, 0, j, :], v_split)
                    if at < LAST:
                        for j in (1, 2, 3):
                            weigh(g + 1, i + p, 1 - p, j)
                    add(g, (0,))
                    if at < LAST - 1:
                        split_u(g + 2)
                    add(g, (1, 2, 3, 4, 5, 6))
                    if at < LAST:
                        top_v(g + 1)
                    if at < LAST - 2:
                        top_u(g + 3)
                    add(g, (7,))

                dve.sem_inc(act_done, NB)
                link.link(dve.memset(tops[:, :], 1.0))
                link.mark(dve.tensor_copy(tops[:, S_ACT:S_ACT + 1], s["h_top"][:, :]))
                top_u(0)
                found()
                scales.powers(dve, link.link, 0)
                scales.take(dve, link.link, 0)
                link.mark(dve.tensor_copy(h_unit[:, :], scales.value[:, 3 + S_ACT:4 + S_ACT]))
                link.wait(link.base + link.n)
                link.link(dve.tensor_tensor(dot_unit[:, 0:1], scales.value[:, 3 + S_U:4 + S_U], h_unit[:, :],
                                            ALU.mult))
                dve.sem_inc(scales.ready, 1)
                split_u(0, (0,))
                for k in range(KC):
                    dve.wait_ge(h_hi, k + 1)
                    rest(h16[:, 1, k, :], h[:, k, :], S_ACT, h16[:, 0, k, :], h_split)
                split_u(0, (1, 2, 3))
                dve.wait_ge(h_split, KC)
                link.link(dve.memset(acc[:, :, :], 0.0))
                top_u(1)
                found()
                scales.powers(dve, link.link, 1)
                weigh(0, 0, 0, 0)
                take(1, 1)
                for j in (1, 2, 3):
                    weigh(0, 0, 0, j)
                split_u(1)
                top_v(0)
                top_u(2)
                per = 1 + Scales.POWERS_LINKS + GRP + 3 + 2
                with dve.Fori(0, LOOPS) as i, link.turns(i, LOOPS, 2 * per):
                    for p in range(2):
                        turn(i * 2 + p, i, p, 0)
                for g in range(2 * LOOPS, NGRP):
                    turn(g, g // 2, g % 2, g)


def final_phase(nc, a, s, sem):
    with ExitStack() as ctx:
        x = ctx.enter_context(nc.sbuf_tensor("x_end", [P, KC, T], F32))
        squares = ctx.enter_context(nc.sbuf_tensor("squares_end", [P, KC, T], F32))
        spare = ctx.enter_context(nc.sbuf_tensor("spare_end", [P, 2, NSEQ, LS], F32))
        ps = ctx.enter_context(nc.psum_tensor("end_ps", [P, NS, 512], F32))
        x_in, x_ready, y_ready, y_out, chain = (
            sem("x_in2"), sem("x_ready"), sem("y_final"), sem("y_out"), sem("final_chain"))
        norm = Norm(nc, sem, "norm_f", x, squares, s, ps)

        with nc.Block() as block:
            @block.sync
            def _(sp):
                for k in range(KC):
                    sp.dma_start(x[:, k, :], a["x_mid"][:, k, :]).then_inc(x_in, 16)
                for k in range(KC):
                    sp.wait_ge(y_ready, k + 1)
                    sp.dma_start(a["y_out"][:, k, :], x[:, k, :]).then_inc(y_out, 16)
                sp.wait_ge(y_out, 16 * KC)

            @block.scalar
            def _(act):
                act.wait_ge(x_ready, KC)
                norm.scalar(act)

            @block.tensor
            def _(pe):
                norm.tensor(pe)

            @block.vector
            def _(dve):
                link = Chain(dve, chain)
                dve.wait_ge(x_in, 16 * KC)
                for k in range(KC):
                    add_gated(dve, link, x[:, k, :], s["mod"][:, 5 * KC + k, :], [(0, s["acc"][:, k, 0:SEQ])],
                              s["acc"][:, k, SEQ:T], spare[:, k % 2, :, :]).then_inc(x_ready, 1)
                norm.vector(dve)
                for k in range(KC):
                    dve.scalar_tensor_tensor(x[:, k, :], x[:, k, :], s["par"][:, W_NF + k:W_NF + k + 1],
                                             s["rstd"][:, :], ALU.mult, ALU.mult).then_inc(y_ready, 1)


OUTS = {
    "y_out": (P, KC, T), "k_out": (4, P, T), "v_out": (T, AW), "conv_out": (P, 12, 1 + NSEQ, CW - 1),
    "ssm_out": (1 + NSEQ, NST, D),
}


def chunked(w):
    k, m = w.shape
    return w.reshape(k // P, P, m // P, P).transpose(2, 1, 0, 3)


def channels(v):
    return v.reshape(-1, P).T


def wide(v):
    return np.broadcast_to(v[None, :], (P, v.size))


def laid_out(i):
    x = np.concatenate([i["x_prompt"][0], i["x_sample"].reshape(TS, D)])
    c = np.concatenate([i["c_prompt"], i["c_sample"]])
    w = i["w_in"][0]
    ends = np.cumsum([0, AW, AW, AW, D, CONV, SH, D, D])
    q, k, v, z, xbc, dt, ga, gs = (w[:, ends[n]:ends[n + 1]] for n in range(8))
    par = np.concatenate([
        channels(i["norm1_w"][0]), channels(i["norm2_w"][0]), channels(i["norm_f_w"]),
        channels(i["ssm_norm_w"][0]), channels(np.repeat(i["d_skip"][0], SP_)), channels(i["b_ada"][0]),
        wide(i["sb_bias"][0]), channels(i["conv_b"][0]),
        i["conv_w"][0].reshape(CW, 12, P).transpose(2, 1, 0).reshape(P, 12 * CW),
        wide(i["dt_bias"][0]), wide(i["a_log"][0]),
    ], axis=1)
    return {
        "const": constants(),
        "par": par,
        "x": x.T.reshape(KC, P, T).transpose(1, 0, 2),
        "cond": c.T.reshape(KC, P, 1 + NSEQ).transpose(1, 0, 2),
        "w_ada": chunked(i["w_ada"][0]),
        "w_in": chunked(np.concatenate([q, k, z, xbc, ga, gs], axis=1)),
        "w_v": v.reshape(KC, P, AW).transpose(1, 0, 2),
        "w_dt": dt.reshape(KC, P, SH).transpose(1, 0, 2),
        "state_conv": i["state_conv"][0].reshape(NSEQ, CW - 1, 12, P).transpose(3, 2, 0, 1),
        "state_ssm": i["state_ssm"][0].reshape(NSEQ, D, NST).transpose(0, 2, 1),
        "pages": i["page_table"].reshape(1, NSEQ * NPAGE),
        "cache_k": i["cache_k"][0].reshape(POOL, PAGE, 4, P).transpose(0, 3, 2, 1),
        "cache_v": i["cache_v"][0].reshape(POOL, PAGE, AW),
        "w_attn": chunked(i["w_br_attn"][0]),
        "w_ssm": chunked(i["w_br_ssm"][0]),
        "w_out": chunked(i["w_out"][0]),
        "w_query": chunked(i["peer_w_query"][0]),
        "keys": np.stack([i["peer_keys1"][0].T, i["peer_keys2"][0].T], axis=1),
        "u": i["peer_u"][0].reshape(NK, NK, KC, P).transpose(1, 3, 2, 0),
        "v": i["peer_v"][0].reshape(NK, NGRP, GRP, D).transpose(1, 0, 2, 3),
    }


SCRATCH = {"proj": (NCH, P, T), "o": (AW, T), "x_mid": (P, KC, T), "w": (NTB, P, NK, TB)}


def kernel(**inputs):
    import concourse.bacc as bacc
    from concourse.bass_utils import run_bass_kernel_spmd

    nc = bacc.Bacc("TRN2", target_bir_lowering=False, num_devices=1)
    arrays, a = {}, {}
    for name, v in laid_out({k: np.asarray(v) for k, v in inputs.items()}).items():
        arrays[f"in_{name}"] = np.ascontiguousarray(v)
        a[name] = nc.dram_tensor(f"in_{name}", v.shape, mybir.dt.from_np(v.dtype), kind="ExternalInput").ap()
    for name, shape in OUTS.items():
        a[name] = nc.dram_tensor(name, shape, F32, kind="ExternalOutput").ap()
    for name, shape in SCRATCH.items():
        a[name] = nc.dram_tensor(f"tmp_{name}", shape, F32, kind="Internal").ap()
    build(nc, a)
    r = run_bass_kernel_spmd(nc, [arrays], core_ids=[0]).results[0]

    y = r["y_out"].transpose(2, 1, 0).reshape(T, D)
    k = r["k_out"].reshape(AW, T).T
    v = r["v_out"]
    conv = r["conv_out"].transpose(2, 3, 1, 0).reshape(1 + NSEQ, CW - 1, CONV)
    ssm = r["ssm_out"].transpose(0, 2, 1).reshape(1 + NSEQ, SH, SP_, NST)
    return (
        y[None, :SEQ], y[SEQ:].reshape(NSEQ, LS, D),
        k[:SEQ].reshape(1, 1, SEQ, HEADS, HD), v[:SEQ].reshape(1, 1, SEQ, HEADS, HD),
        conv[None, :1], ssm[None, :1],
        k[SEQ:].reshape(1, NSEQ, LS, HEADS, HD), v[SEQ:].reshape(1, NSEQ, LS, HEADS, HD),
        conv[None, 1:], ssm[None, 1:],
    )
```
